# Optimizing a Trainium2 kernel written in Bass

```python
import math
import jax, jax.numpy as jnp
from jax import lax
import numpy as np

D_MODEL = 1024
BATCH = 1
SEQ = 256
DEPTH = 2
DEC_BATCH = 8
DEC_SEQ = 1
PAST_LEN = 1024
PAGE_SIZE = 128

N_MIXERS = 4
GROUP_WIDTH = D_MODEL // N_MIXERS
HEAD_DIM = 64
N_GROUP_HEADS = GROUP_WIDTH // HEAD_DIM
MIX_WIDTH = N_MIXERS * GROUP_WIDTH
D_FF = ((8 * D_MODEL // 3 + 127) // 128) * 128
ROPE_THETA = 500000.0
ROPE_DIM = HEAD_DIM // 4
DILATED_PATTERNS = ((128, 1), (512, 4), (2048, 16))
WINDOW_MAX = 2048
FOX_BLOCK = 128
FORGET_BIAS_MEAN = 3.0
GDN_CHUNK = 64
CONV_W = 4
GMLP_CHUNK = 128
NORM_EPS = 1e-6
PROJ_SIZES = (GROUP_WIDTH,) * 3 + (GROUP_WIDTH,) * 3 + (N_GROUP_HEADS,) + (GROUP_WIDTH,) * 4 + (N_GROUP_HEADS,) * 2 + (GROUP_WIDTH,) * 2
PROJ_WIDTH = sum(PROJ_SIZES)

kernel_name = 'hybrid_dilated_fox_gdn_gmlp_decoder_step'

def rms_norm(x, g):
    xf = x.astype(jnp.float32)
    y = xf * lax.rsqrt(jnp.mean(xf * xf, axis=-1, keepdims=True) + NORM_EPS)
    return (y * g.astype(jnp.float32)).astype(x.dtype)

def l2_normalize(x):
    xf = x.astype(jnp.float32)
    return xf * lax.rsqrt(jnp.sum(xf * xf, axis=-1, keepdims=True) + NORM_EPS)

def heads(x):
    return x.reshape(x.shape[:-1] + (x.shape[-1] // HEAD_DIM, HEAD_DIM))

def swiglu(x, w_gate, w_up, w_down):
    return (jax.nn.silu(x @ w_gate) * (x @ w_up)) @ w_down

def ffn_half_step(x, g_pre, g_post, w_gate, w_up, w_down):
    return x + 0.5 * rms_norm(swiglu(rms_norm(x, g_pre), w_gate, w_up, w_down), g_post)

def rope_partial(x, pos):
    half = ROPE_DIM // 2
    inv_freq = ROPE_THETA ** (-jnp.arange(half, dtype=jnp.float32) / half)
    ang = pos.astype(jnp.float32)[:, None] * inv_freq[None, :]
    cos = jnp.cos(ang)[:, None, :]
    sin = jnp.sin(ang)[:, None, :]
    xr = x[..., :ROPE_DIM].astype(jnp.float32)
    x1, x2 = xr[..., :half], xr[..., half:]
    rot = jnp.concatenate([x1 * cos - x2 * sin, x2 * cos + x1 * sin], axis=-1)
    return jnp.concatenate([rot.astype(x.dtype), x[..., ROPE_DIM:]], axis=-1)

def project(h, w_in):
    cuts = np.cumsum(PROJ_SIZES)[:-1].tolist()
    return jnp.split(h @ w_in, cuts, axis=-1)

def banded_causal_attention(q, k, v, n_keys):
    n, L, H, D = q.shape
    blk = n_keys
    nb = -(-L // blk)
    pad = nb * blk - L
    qb = jnp.pad(q, ((0, 0), (0, pad), (0, 0), (0, 0))).reshape(n, nb, blk, H, D)

    def kv_blocks(x):
        xp = jnp.pad(x, ((0, 0), (blk, pad), (0, 0), (0, 0))).reshape(n, nb + 1, blk, H, D)
        return jnp.concatenate([xp[:, :-1], xp[:, 1:]], axis=2)

    kb, vb = kv_blocks(k), kv_blocks(v)
    qpos = jnp.arange(nb)[:, None] * blk + jnp.arange(blk)[None, :]
    kpos = jnp.arange(nb)[:, None] * blk - blk + jnp.arange(2 * blk)[None, :]
    dist = qpos[:, :, None] - kpos[:, None, :]
    valid = (dist >= 0) & (dist < n_keys) & (kpos[:, None, :] >= 0)
    s = jnp.einsum('nbqhd,nbkhd->nbhqk', qb, kb, preferred_element_type=jnp.float32) * HEAD_DIM ** -0.5
    s = jnp.where(valid[None, :, None], s, -jnp.inf)
    lse = jax.nn.logsumexp(s, axis=-1)
    p = jnp.exp(s - lse[..., None])
    o = jnp.einsum('nbhqk,nbkhd->nbqhd', p.astype(v.dtype), vb).reshape(n, nb * blk, H, D)[:, :L]
    lse = lse.transpose(0, 1, 3, 2).reshape(n, nb * blk, H)[:, :L]
    return o, lse

def dilated_prompt(q, k, v, window, dil):
    n, L, H, D = q.shape
    m = L // dil

    def to_sub(x):
        return x.reshape(n, m, dil, H, D).transpose(0, 2, 1, 3, 4).reshape(n * dil, m, H, D)

    o, lse = banded_causal_attention(to_sub(q), to_sub(k), to_sub(v), window // dil)
    o = o.reshape(n, dil, m, H, D).transpose(0, 2, 1, 3, 4).reshape(n, L, H, D)
    lse = lse.reshape(n, dil, m, H).transpose(0, 2, 1, 3).reshape(n, L, H)
    return o, lse

def dilated_sample(q, k_all, v_all, wb, window, dil):
    T = q.shape[1]
    n_keys = window // dil
    idx = wb + jnp.arange(T)[:, None] - dil * jnp.arange(n_keys)[None, :]
    valid = idx >= 0
    idx = jnp.maximum(idx, 0)
    kg = k_all[:, idx]
    vg = v_all[:, idx]
    s = jnp.einsum('nthd,ntkhd->nthk', q, kg, preferred_element_type=jnp.float32) * HEAD_DIM ** -0.5
    s = jnp.where(valid[None, :, None, :], s, -jnp.inf)
    lse = jax.nn.logsumexp(s, axis=-1)
    p = jnp.exp(s - lse[..., None])
    o = jnp.einsum('nthk,ntkhd->nthd', p.astype(v_all.dtype), vg)
    return o, lse

def combine_by_denominator(results):
    o = jnp.stack([r[0] for r in results], axis=0)
    lse = jnp.stack([r[1] for r in results], axis=0)
    wts = jax.nn.softmax(lse, axis=0)
    return jnp.einsum('pnlh,pnlhd->nlhd', wts, o.astype(jnp.float32)).astype(o.dtype)

def fox_attend(q, k, v, cum_k, cum_q, q_pos):
    s = jnp.einsum('nqhd,nkhd->nhqk', q, k, preferred_element_type=jnp.float32) * HEAD_DIM ** -0.5
    s = s + cum_q[..., :, None] - cum_k[..., None, :]
    k_pos = jnp.arange(k.shape[1])
    s = jnp.where(k_pos[None, :] <= q_pos[:, None], s, -jnp.inf)
    p = jax.nn.softmax(s, axis=-1)
    return jnp.einsum('nhqk,nkhd->nqhd', p.astype(v.dtype), v)

def fox_prompt(q, k, v, logf):
    n, L, H, D = q.shape
    nb = L // FOX_BLOCK
    cum_t = jnp.cumsum(logf, axis=1).transpose(0, 2, 1)
    q_blocks = q.reshape(n, nb, FOX_BLOCK, H, D).transpose(1, 0, 2, 3, 4)
    c_blocks = cum_t.reshape(n, H, nb, FOX_BLOCK).transpose(2, 0, 1, 3)
    p_blocks = jnp.arange(L).reshape(nb, FOX_BLOCK)
    o = lax.map(lambda a: fox_attend(a[0], k, v, cum_t, a[1], a[2]), (q_blocks, c_blocks, p_blocks))
    return o.transpose(1, 0, 2, 3, 4).reshape(n, L, H, D)

def gated_delta_chunked(q, k, v, g, beta, s0):
    n, L, H, DK = q.shape
    DV = v.shape[-1]
    C = GDN_CHUNK
    nc = -(-L // C)
    pad = nc * C - L

    def chunks(x):
        x = jnp.pad(x, ((0, 0), (0, pad)) + ((0, 0),) * (x.ndim - 2))
        x = x.reshape((n, nc, C) + x.shape[2:])
        return jnp.moveaxis(jnp.moveaxis(x, 1, 0), 3, 2)

    qc, kc, vc, gch, bch = chunks(q), chunks(k), chunks(v), chunks(g), chunks(beta)
    gcum = jnp.cumsum(gch, axis=-1)
    i = jnp.arange(C)
    incl = i[:, None] >= i[None, :]
    strict = i[:, None] > i[None, :]
    decay = jnp.exp(jnp.where(incl, gcum[..., :, None] - gcum[..., None, :], -jnp.inf))
    kbeta = kc * bch[..., None]
    a_mat = jnp.where(strict, jnp.einsum('...id,...jd->...ij', kbeta, kc) * decay, 0.0)
    eye = jnp.eye(C, dtype=jnp.float32)
    t_mat = lax.linalg.triangular_solve(eye + a_mat, jnp.broadcast_to(eye, a_mat.shape), left_side=True, lower=True)
    u = t_mat @ (vc * bch[..., None])
    w = t_mat @ (kbeta * jnp.exp(gcum)[..., None])
    qk = jnp.einsum('...id,...jd->...ij', qc, kc) * decay

    def step(s, xs):
        q_i, k_i, u_i, w_i, g_i, qk_i = xs
        v_new = u_i - w_i @ s
        o_i = (q_i * jnp.exp(g_i)[..., None]) @ s + qk_i @ v_new
        g_last = g_i[..., -1:]
        s = s * jnp.exp(g_last)[..., None] + jnp.einsum('nhck,nhcv->nhkv', k_i * jnp.exp(g_last - g_i)[..., None], v_new)
        return s, o_i

    s_fin, o = lax.scan(step, s0, (qc, kc, u, w, gcum, qk))
    o = jnp.moveaxis(jnp.moveaxis(o, 2, 3), 0, 1).reshape(n, nc * C, H, DV)[:, :L]
    return o, s_fin

def gdn_branch(qc, kc, vc, ac, bc, conv_buf, s0, conv_w, a_log, dt_bias):
    raw = jnp.concatenate([qc, kc, vc], axis=-1)
    L = raw.shape[1]
    xin = jnp.concatenate([conv_buf.astype(raw.dtype), raw], axis=1)
    conv = jax.nn.silu(sum(xin[:, j:j + L] * conv_w[j] for j in range(CONV_W)))
    q, k, v = jnp.split(conv, 3, axis=-1)
    q = l2_normalize(heads(q)) * HEAD_DIM ** -0.5
    k = l2_normalize(heads(k))
    v = heads(v).astype(jnp.float32)
    g = -jnp.exp(a_log.astype(jnp.float32)) * jax.nn.softplus(ac.astype(jnp.float32) + dt_bias.astype(jnp.float32))
    beta = jax.nn.sigmoid(bc.astype(jnp.float32))
    o, s_new = gated_delta_chunked(q, k, v, g, beta, s0.astype(jnp.float32))
    return o, s_new, xin[:, -(CONV_W - 1):]

def gmlp_branch(ud, vd, ws, bs, gv):
    u = jax.nn.gelu(ud)
    v = rms_norm(jax.nn.gelu(vd), gv)
    n, L, _ = v.shape
    nc = -(-L // GMLP_CHUNK)
    pad = nc * GMLP_CHUNK - L
    vch = jnp.pad(v, ((0, 0), (0, pad), (0, 0))).reshape(n, nc, GMLP_CHUNK, N_GROUP_HEADS, HEAD_DIM)
    tri = jnp.tril(jnp.ones((GMLP_CHUNK, GMLP_CHUNK), dtype=bool))
    ws_c = jnp.where(tri, ws, 0.0).astype(v.dtype)
    mixed = jnp.einsum('gts,ncsgd->nctgd', ws_c, vch) + bs.T.astype(v.dtype)[None, None, :, :, None]
    mixed = mixed.reshape(n, nc * GMLP_CHUNK, N_GROUP_HEADS, HEAD_DIM)[:, :L]
    return heads(u) * mixed, v

def merge_groups(o_a, o_b, o_c, z_c, o_d, out_g, w_out):
    n, l = o_a.shape[:2]
    parts = [rms_norm(o_a, out_g[0]),
             rms_norm(o_b, out_g[1]),
             rms_norm(o_c.astype(o_a.dtype), out_g[2]) * jax.nn.silu(heads(z_c)),
             rms_norm(o_d, out_g[3])]
    return jnp.concatenate(parts, axis=2).reshape(n, l, MIX_WIDTH) @ w_out

def mix_prompt(h, lw):
    w_in, out_g, w_out, fox_b, conv_w, a_log, dt_b, ws, bs, gv = lw
    n, L, _ = h.shape
    pos = jnp.arange(L)
    qa, ka, va, qb, kb, vb, fb, qc, kc, vc, zc, ac, bc, ud, vd = project(h, w_in)
    qa, ka, va = rope_partial(heads(qa), pos), rope_partial(heads(ka), pos), heads(va)
    o_a = combine_by_denominator([dilated_prompt(qa, ka, va, w, d) for (w, d) in DILATED_PATTERNS])
    qb, kb, vb = heads(qb), heads(kb), heads(vb)
    logf = jax.nn.log_sigmoid(fb.astype(jnp.float32) + fox_b.astype(jnp.float32))
    o_b = fox_prompt(qb, kb, vb, logf)
    conv0 = jnp.zeros((n, CONV_W - 1, 3 * GROUP_WIDTH), h.dtype)
    s0 = jnp.zeros((n, N_GROUP_HEADS, HEAD_DIM, HEAD_DIM), jnp.float32)
    o_c, s_c, conv_c = gdn_branch(qc, kc, vc, ac, bc, conv0, s0, conv_w, a_log, dt_b)
    o_d, _ = gmlp_branch(ud, vd, ws, bs, gv)
    y = merge_groups(o_a, o_b, o_c, zc, o_d, out_g, w_out)
    keep = max(L - WINDOW_MAX, 0)
    return y, (kb, vb, logf, ka[:, keep:], va[:, keep:], s_c, conv_c)

def mix_sample(h, past_k, past_v, past_logf, swa_k, swa_v, gdn_s, gdn_conv, lw):
    w_in, out_g, w_out, fox_b, conv_w, a_log, dt_b, ws, bs, gv = lw
    n, T, _ = h.shape
    past = past_k.shape[1]
    pos = past + jnp.arange(T)
    qa, ka, va, qb, kb, vb, fb, qc, kc, vc, zc, ac, bc, ud, vd = project(h, w_in)
    qa, ka, va = rope_partial(heads(qa), pos), rope_partial(heads(ka), pos), heads(va)
    wb = swa_k.shape[1]
    ka_all = jnp.concatenate([swa_k, ka], axis=1)
    va_all = jnp.concatenate([swa_v, va], axis=1)
    o_a = combine_by_denominator([dilated_sample(qa, ka_all, va_all, wb, w, d) for (w, d) in DILATED_PATTERNS])
    qb, kb, vb = heads(qb), heads(kb), heads(vb)
    logf = jax.nn.log_sigmoid(fb.astype(jnp.float32) + fox_b.astype(jnp.float32))
    kb_all = jnp.concatenate([past_k, kb], axis=1)
    vb_all = jnp.concatenate([past_v, vb], axis=1)
    cum_t = jnp.cumsum(jnp.concatenate([past_logf.astype(jnp.float32), logf], axis=1), axis=1).transpose(0, 2, 1)
    o_b = fox_attend(qb, kb_all, vb_all, cum_t, cum_t[:, :, past:], pos)
    o_c, s_c, conv_c = gdn_branch(qc, kc, vc, ac, bc, gdn_conv, gdn_s, conv_w, a_log, dt_b)
    o_d, v_d = gmlp_branch(ud, vd, ws, bs, gv)
    y = merge_groups(o_a, o_b, o_c, zc, o_d, out_g, w_out)
    return y, (kb, vb, logf, ka, va, s_c, conv_c, v_d)

def setup_inputs(seed: int = 0) -> dict:
    key = jax.random.key(seed)
    ks = jax.random.split(key, 32)
    f32 = jnp.float32
    n_pages = PAST_LEN // PAGE_SIZE
    n_used = DEC_BATCH * n_pages
    n_pool = n_used + max(1, n_used // 4)
    wb = min(WINDOW_MAX, PAST_LEN)

    def nrm(k, shape, scale=1.0):
        return scale * jax.random.normal(k, shape, f32)

    page_table = jax.random.permutation(ks[5], n_pool)[:n_used].reshape(DEC_BATCH, n_pages).astype(jnp.int32)
    dt = jnp.exp(jax.random.uniform(ks[15], (DEPTH, N_GROUP_HEADS), f32, minval=math.log(1e-3), maxval=math.log(1e-1)))
    return {
        'x_prompt': nrm(ks[0], (BATCH, SEQ, D_MODEL)),
        'x_sample': nrm(ks[1], (DEC_BATCH, DEC_SEQ, D_MODEL)),
        'cache_fox_k': nrm(ks[2], (n_pool, DEPTH, PAGE_SIZE, N_GROUP_HEADS, HEAD_DIM)),
        'cache_fox_v': nrm(ks[3], (n_pool, DEPTH, PAGE_SIZE, N_GROUP_HEADS, HEAD_DIM)),
        'cache_fox_logf': jax.nn.log_sigmoid(FORGET_BIAS_MEAN + nrm(ks[4], (n_pool, DEPTH, PAGE_SIZE, N_GROUP_HEADS))),
        'page_table': page_table,
        'state_swa_k': nrm(ks[6], (DEC_BATCH, DEPTH, wb, N_GROUP_HEADS, HEAD_DIM)),
        'state_swa_v': nrm(ks[7], (DEC_BATCH, DEPTH, wb, N_GROUP_HEADS, HEAD_DIM)),
        'state_gdn_s': nrm(ks[8], (DEC_BATCH, DEPTH, N_GROUP_HEADS, HEAD_DIM, HEAD_DIM), HEAD_DIM ** -0.5),
        'state_gdn_conv': nrm(ks[9], (DEC_BATCH, DEPTH, CONV_W - 1, 3 * GROUP_WIDTH)),
        'norm_g': 1.0 + nrm(ks[10], (DEPTH, 6, D_MODEL), 0.1),
        'w_in': nrm(ks[11], (DEPTH, D_MODEL, PROJ_WIDTH), D_MODEL ** -0.5),
        'w_out': nrm(ks[12], (DEPTH, MIX_WIDTH, D_MODEL), MIX_WIDTH ** -0.5),
        'out_norm_g': 1.0 + nrm(ks[13], (DEPTH, N_MIXERS, N_GROUP_HEADS, HEAD_DIM), 0.1),
        'fox_bias': FORGET_BIAS_MEAN + nrm(ks[14], (DEPTH, N_GROUP_HEADS), 0.1),
        'gdn_conv_w': nrm(ks[16], (DEPTH, CONV_W, 3 * GROUP_WIDTH), CONV_W ** -0.5),
        'gdn_a_log': jnp.log(jax.random.uniform(ks[17], (DEPTH, N_GROUP_HEADS), f32, minval=1.0, maxval=16.0)),
        'gdn_dt_bias': dt + jnp.log(-jnp.expm1(-dt)),
        'gmlp_ws': nrm(ks[18], (DEPTH, N_GROUP_HEADS, GMLP_CHUNK, GMLP_CHUNK), GMLP_CHUNK ** -0.5),
        'gmlp_bs': 1.0 + nrm(ks[19], (DEPTH, N_GROUP_HEADS, GMLP_CHUNK), 0.1),
        'gmlp_norm_g': 1.0 + nrm(ks[20], (DEPTH, GROUP_WIDTH), 0.1),
        'ffn1_gate': nrm(ks[21], (DEPTH, D_MODEL, D_FF), D_MODEL ** -0.5),
        'ffn1_up': nrm(ks[22], (DEPTH, D_MODEL, D_FF), D_MODEL ** -0.5),
        'ffn1_down': nrm(ks[23], (DEPTH, D_FF, D_MODEL), D_FF ** -0.5),
        'ffn2_gate': nrm(ks[24], (DEPTH, D_MODEL, D_FF), D_MODEL ** -0.5),
        'ffn2_up': nrm(ks[25], (DEPTH, D_MODEL, D_FF), D_MODEL ** -0.5),
        'ffn2_down': nrm(ks[26], (DEPTH, D_FF, D_MODEL), D_FF ** -0.5),
    }

def reference(x_prompt, x_sample, cache_fox_k, cache_fox_v, cache_fox_logf, page_table,
              state_swa_k, state_swa_v, state_gdn_s, state_gdn_conv,
              norm_g, w_in, w_out, out_norm_g, fox_bias, gdn_conv_w, gdn_a_log, gdn_dt_bias,
              gmlp_ws, gmlp_bs, gmlp_norm_g,
              ffn1_gate, ffn1_up, ffn1_down, ffn2_gate, ffn2_up, ffn2_down):
    n_seq, n_pages = page_table.shape
    past = n_pages * PAGE_SIZE
    xp, xs = x_prompt, x_sample
    st_p, st_s = [], []
    for l in range(DEPTH):
        g = norm_g[l]
        lw = (w_in[l], out_norm_g[l], w_out[l], fox_bias[l], gdn_conv_w[l], gdn_a_log[l],
              gdn_dt_bias[l], gmlp_ws[l], gmlp_bs[l], gmlp_norm_g[l])
        xp = ffn_half_step(xp, g[0], g[1], ffn1_gate[l], ffn1_up[l], ffn1_down[l])
        xs = ffn_half_step(xs, g[0], g[1], ffn1_gate[l], ffn1_up[l], ffn1_down[l])
        m_p, s_p = mix_prompt(rms_norm(xp, g[2]), lw)
        xp = xp + rms_norm(m_p, g[3])
        past_k = cache_fox_k[page_table, l].reshape(n_seq, past, N_GROUP_HEADS, HEAD_DIM)
        past_v = cache_fox_v[page_table, l].reshape(n_seq, past, N_GROUP_HEADS, HEAD_DIM)
        past_logf = cache_fox_logf[page_table, l].reshape(n_seq, past, N_GROUP_HEADS)
        m_s, s_s = mix_sample(rms_norm(xs, g[2]), past_k, past_v, past_logf,
                              state_swa_k[:, l], state_swa_v[:, l], state_gdn_s[:, l], state_gdn_conv[:, l], lw)
        xs = xs + rms_norm(m_s, g[3])
        xp = ffn_half_step(xp, g[4], g[5], ffn2_gate[l], ffn2_up[l], ffn2_down[l])
        xs = ffn_half_step(xs, g[4], g[5], ffn2_gate[l], ffn2_up[l], ffn2_down[l])
        st_p.append(s_p)
        st_s.append(s_s)
    (fox_k_prompt, fox_v_prompt, fox_logf_prompt, swa_k_prompt, swa_v_prompt,
     gdn_s_prompt, gdn_conv_prompt) = [jnp.stack(z, axis=1) for z in zip(*st_p)]
    (fox_k_sample, fox_v_sample, fox_logf_sample, swa_k_sample, swa_v_sample,
     gdn_s_sample, gdn_conv_sample, gmlp_v_sample) = [jnp.stack(z, axis=1) for z in zip(*st_s)]
    y_prompt, y_sample = xp, xs
    return (y_prompt, y_sample, fox_k_prompt, fox_v_prompt, fox_logf_prompt,
            fox_k_sample, fox_v_sample, fox_logf_sample,
            swa_k_prompt, swa_v_prompt, swa_k_sample, swa_v_sample,
            gdn_s_prompt, gdn_conv_prompt, gdn_s_sample, gdn_conv_sample, gmlp_v_sample)


_drawn_inputs = setup_inputs


def setup_inputs(seed=0):
    import zlib

    import numpy as np

    out = dict(_drawn_inputs(seed))
    spreads = {}
    factors = {}
    for name, (base, spread) in spreads.items():
        noise = np.random.default_rng([zlib.crc32(name.encode()), seed]).standard_normal(out[name].shape)
        drawn = base * np.exp(spread * noise) if base else spread * noise
        out[name] = __import__('jax').numpy.asarray(drawn.astype(out[name].dtype))
    for name, factor in factors.items():
        out[name] = (out[name] * factor).astype(out[name].dtype)
    return out
```

```python
from contextlib import ExitStack

import numpy as np

import concourse.bass as bass
from concourse import mybir

F32 = mybir.dt.float32
F32R = mybir.dt.float32r
I32 = mybir.dt.int32
ALU = mybir.AluOpType
ACT = mybir.ActivationFunctionType
AX = mybir.AxisListType
RMAX = bass.bass_isa.ReduceOp.max

P = 128
D = 1024
KT = D // P
L = 256
NT = L // P
B = 8
N = L + B
DEPTH = 2
FF = 2816
FT = FF // P
H, HD = 4, 64
GW = H * HD
NPG = 8
PAST = 1024
PW = 3084
NPT = 25
QA, KA, VA, QB_, KB_, VB_, FB, QC, ZC, AC, UD, VD = 0, 256, 512, 768, 1024, 1280, 1536, 1540, 2308, 2564, 2572, 2828
CT0 = QC // P
NCT = 7
COFF = QC - CT0 * P
EPS = 1e-6
NEG = -1e30
CACHE_T = 3
NKT = NPG + CACHE_T
FOX_PG, SWA_PG = NPG + 1, CACHE_T + 1
NPAGE = FOX_PG + SWA_PG
LEVELS = (2, 4, 8, 16, 32, 64)



def constants():
    i = np.arange(P)
    col, parts = {}, []

    def put(name, a):
        a = np.asarray(a, np.float64).reshape(a.shape[0], -1)
        full = np.zeros((P, a.shape[1]))
        full[:a.shape[0]] = a
        col[name] = (sum(p.shape[1] for p in parts), a.shape[1])
        parts.append(full)

    put("ident", np.eye(P))
    put("upto", (i[:, None] <= i[None, :]))
    put("after", (i[:, None] > i[None, :]))
    put("strict", (i[:, None] < i[None, :]))
    put("ones", np.ones((P, P)))
    put("same_state", (i[:, None] // 4 == i[None, :] // 4))
    put("causal", np.where(i[:, None] <= i[None, :], 0.0, NEG))
    blocks = ((0, 0), (1, 0), (1, 1))
    dist = np.stack([(tq * P + i)[:, None] - (tk * P + i)[None, :] for tq, tk in blocks], 1)
    times = sum(((dist >= 0) & (dist < w) & (dist % d == 0)).astype(float)
                for w, d in ((128, 1), (512, 4), (2048, 16)))
    put("swa_mask", np.where(times > 0, np.log(np.maximum(times, 1)), NEG))
    put("fox_mask", np.where(dist >= 0, 0.0, NEG))
    low = lambda b: ((i[:, None] // (2 * b) == i[None, :] // (2 * b)) & (i[:, None] % (2 * b) >= b)
                     & (i[None, :] % (2 * b) < b))
    put("level1T", low(1).T)
    for b in LEVELS:
        put(f"level{b}", low(b))
    put("head_rows", np.repeat(np.eye(4), P, 1))
    freq = 500000.0 ** (-np.arange(8, dtype=np.float32) / np.float32(8))
    ang = (np.arange(L, dtype=np.float32)[:, None] * freq.astype(np.float32)[None]).astype(np.float32)
    turn = lambda a: a.reshape(NT, P, 8).transpose(1, 0, 2)
    put("cos", turn(np.cos(ang)))
    put("sin", turn(np.sin(ang)))
    last = (np.float32(PAST) * freq.astype(np.float32)).astype(np.float32)
    put("cos_s", np.tile(np.cos(last), (B, 1)))
    put("sin_s", np.tile(np.sin(last), (B, 1)))
    window = np.zeros((P, CACHE_T))
    window[0, 0:2] = NEG
    window[PAST // 16:, 2] = NEG
    put("window", np.repeat(window, H, 1))
    put("own_bias", np.repeat(np.stack([np.where(np.eye(P, B) > 0, 0.0, NEG),
                                        np.where(np.eye(P, B) > 0, np.log(3.0), NEG)], 2), H, 2))
    put("head_block", np.repeat(np.tile(np.eye(4), (9, 1)), HD, 1))
    rows = np.zeros((36, 4, B))
    for pair in range(4):
        for k in range(2):
            rows[32 * k:32 * k + H, pair, 2 * pair + k] = 1
    put("to_token", rows)
    put("eps", np.full((P, 1), EPS))
    scale = np.ones((P, 1))
    scale[0:32] = HD ** -0.5
    put("q_scale", scale)
    put("sign", np.tile(np.repeat([-1.0, 1.0, -1.0], 4), (P, 1)))
    return np.concatenate(parts, 1).astype(np.float32), col


CONST, COL = constants()
NCONST = CONST.shape[1]


def build(nc, io):
    GU_P, DN_P, WI_P, WO_P = FT // 2, KT, 7, 2
    PH = ["gu1", "dn1", "wi", "wo", "gu2", "dn2"]
    PAIRS = dict(zip(PH, [GU_P, DN_P, WI_P, WO_P, GU_P, DN_P]))
    P0 = {n: sum(PAIRS[m] for m in PH[:k]) for k, n in enumerate(PH)}
    INC = {"gu1": 2, "dn1": 1, "wi": 2, "wo": 2, "gu2": 2, "dn2": 1}
    TOTAL = {n: PAIRS[n] * INC[n] - (1 if n == "wi" else 0) for n in PH}
    M0 = {n: sum(TOTAL[m] for m in PH[:k]) for k, n in enumerate(PH)}
    FULL = ((0, 1024), (1024, 2048))
    HALVES = {"gu1": FULL, "dn1": ((0, 768), (768, 1408)), "wi": FULL, "wi_last": ((0, 256), (256, 512)),
              "wo": FULL, "gu2": FULL, "dn2": ((0, 768), (768, 1408))}

    ctx = ExitStack()
    with ctx:
        here = [(nc.sbuf_base + 31) // 32 * 32]

        def place(name, shape, dt=F32, at=None):
            size = 4 * int(np.prod(shape[1:]))
            off = here[0] if at is None else at
            if at is None:
                here[0] += (size + 31) // 32 * 32
            return nc.alloc_sbuf_tensor_at(name, list(shape), dt, offset=off)

        x = place("x", [P, KT, N])
        const = place("const", [P, NCONST])
        ptab = place("ptab", [1, B * NPG], I32)
        r_post = place("r_post", [P, N])
        ss_acc = place("ss_acc", [P, N])
        gains = place("gains", [P, 48])
        param12 = place("param12", [P, 12])
        mul12 = place("mul12", [P, 12])
        a_log = place("a_log", [P, 4])
        gate_in = place("gate_in", [P, 3, 12])
        gate_t = place("gate_t", [P, 3, 12])
        gate = place("gate", [P, 3, 12])
        cum = place("cum", [P, 24])
        eg = place("eg", [P, 3, 8])
        rows = place("rows", [4, 4, L])
        og = place("og", [P, D])
        gv = place("gv", [P, GW])
        wst = place("wst", [P, H, P])
        bst = place("bst", [P, H])
        cwt = place("cwt", [P, NCT, 4])
        ws0 = place("ws0", [B, 2, H])
        small = place("small", [P, 160])
        sx = place("sx", [P, B, 2, H])
        bias = place("bias", [P, B, NKT, H])
        w_at = here[0]
        raw = [place(f"raw{s}", [P, 2048]) for s in range(2)]
        whi = [place(f"whi{s}", [P, 2048], F32R) for s in range(2)]
        wlo = [place(f"wlo{s}", [P, 2048], F32R) for s in range(2)]
        cursor = [w_at]

        def scratch(name, n, shape=None):
            t = place(name, shape or [P, n], at=cursor[0])
            cursor[0] += 4 * n
            assert cursor[0] <= here[0]
            return t

        q_bc = scratch("q_bc", 1024, [P, 2, 512])
        prod = scratch("prod", NKT * GW, [P, NKT, GW])
        dt_ = scratch("dt_", 1024, [P, 2, 512])
        at_ = scratch("at_", 1024, [P, 2, 512])
        qkt = scratch("qkt", 1024, [P, 2, 512])
        ys = scratch("ys", 1024, [P, 2, 512])
        conv_t = place("conv_t", [P, NCT, L], at=cursor[0])
        tt = scratch("tt", 1024, [P, 2, 512])
        tm = scratch("tm", 1024, [P, 2, 512])
        kb_n = scratch("kb_n", 512, [P, 2, GW])
        kd = scratch("kd", 512, [P, 2, GW])
        vn = scratch("vn", 512, [P, 2, GW])
        st_s = scratch("st_s", 128, [P, 2, HD])
        k_at = here[0]
        kslot = place("kslot", [P, 2, NKT, GW])
        yt = place("yt", [P, KT, N], at=k_at)
        sq8 = place("sq8", [P, KT, N], at=k_at + 4 * KT * N)
        v_at = here[0]
        vslot = place("vslot", [P, 2, NKT, GW + 1])
        nhi = place("nhi", [P, KT, N], F32R, at=v_at)
        nlo = place("nlo", [P, KT, N], F32R, at=v_at + 4 * KT * N)
        f_at = here[0]
        proj = place("proj", [P, NPT, N])
        tok = place("tok", [P, NT, PW])
        f_end = here[0]
        hhi = place("hhi", [P, FT, N], F32R, at=f_at)
        hlo = place("hlo", [P, FT, N], F32R, at=f_at + 4 * FT * N)
        s_t = place("s_t", [P, 2, N], at=f_at + 8 * FT * N)
        h_t = place("h_t", [P, 2, N], at=f_at + 8 * FT * N + 8 * N)
        assert f_at + 8 * FT * N + 16 * N <= f_end
        xin = place("xin", [P, 3, D], at=f_at)
        gin = place("gin", [P, P], at=f_at)
        win = place("win", [P, H, P], at=f_at + 4 * P)
        bin_ = place("bin_", [H, P], at=f_at + 4 * P * 5)
        cwin = place("cwin", [4, NCT * P], at=f_at + 4 * P * 6)
        flat = proj[:, :, :].rearrange("p t n -> p (t n)")
        smx = flat[:, 0:1536].rearrange("p (h k) -> p h k", h=H)
        qkT = flat[:, 6 * N:6 * N + 1024].rearrange("p (t n) -> p t n", t=4)
        ck = flat[:, 12 * N:12 * N + 2 * NCT * P].rearrange("p (a n) -> p a n", a=2)
        kqT = flat[:, 19 * N:19 * N + 1536].rearrange("p (k a n) -> p k a n", k=3, a=2)
        smp = place("smp", [B, PW])
        smp_o = place("smp_o", [B, D])
        ptr = place("ptr", [P, 3, 512])
        otok = place("otok", [P, NT, D])
        sqt = ptr[:, 0:2, :].rearrange("p a n -> p (a n)")
        cv = place("cv", [96, 9, HD])
        kq16 = place("kq16", [P, 2, 16])
        v64 = place("v64", [P, HD])
        gb = place("gb", [P, 2])
        state = place("state", [P, 16, HD], at=w_at)
        s13 = place("s13", [P, 2, NPAGE, H])
        pmax = place("pmax", [P, 2, 2, H])
        pmax_all = place("pmax_all", [P, 2, 2, H])
        oms = place("oms", [36, 4, 512])
        v_own = scratch("v_own", 2 * (GW + 1), [B, 2, GW + 1])

        ps = ctx.enter_context(nc.psum_tensor("ps", [P, 8, 512], F32))

        def C(name, rows_=P):
            a, n = COL[name]
            return const[0:rows_, a:a + n]

        ident, ones = C("ident"), C("ones")

        def dram(name, shape):
            return nc.dram_tensor(name, shape, F32, kind="Internal").ap()

        d_logf = dram("d_logf", [B * NPG, P * H])
        d_q = dram("d_q", [B, 512])
        d_cnew = dram("d_cnew", [3, B, GW])
        d_cold = dram("d_cold", [3, 3, B, GW])
        d_cw = dram("d_cw", [4, 3, B, GW])
        d_cn = dram("d_cn", [3, B, GW])
        d_gate = dram("d_gate", [B, H, 2])
        d_oc = dram("d_oc", [B, GW])

        sems = {}

        def S(name):
            if name not in sems:
                sems[name] = ctx.enter_context(nc.semaphore(name))
            return sems[name]

        class Chain:

            def __init__(self, eng, name):
                self.eng, self.name, self.n = eng, name, 0

            def __call__(self, ins):
                ins.then_inc(S(self.name), 1)
                self.n += 1
                self.eng.wait_ge(S(self.name), self.n)

        def kt_view(ap, k):
            return ap.rearrange("p (k m) -> p k m", k=k)

        with nc.Block() as blk:
            @blk.sync
            def _(sp):
                sp.dma_start(const[:, :], io["const"]).then_inc(S("row_in"), 16)
                sp.dma_start(xin[:, 0:2, :], io["x_prompt"][0].rearrange("(t p) d -> p t d", p=P)).then_inc(S("par_in"), 16)
                sp.dma_start(xin[0:B, 2, :], io["x_sample"].rearrange("b t d -> (b t) d")).then_inc(S("par_in"), 16)
                sp.dma_start(ptab[:, :], io["page_table"].rearrange("(o b) g -> o (b g)", o=1)).then_inc(S("row_in"), 16)
                sp.wait_ge(S("row_in"), 32)

            @blk.tensor
            def _(pe):
                pe.wait_ge(S("row_in"), 32)
                pe.wait_ge(S("par_in"), 32)
                for t in range(KT):
                    for a in range(NT):
                        pe.transpose(ps[:, t, a * P:(a + 1) * P], xin[:, a, t * P:(t + 1) * P], ident)
                    pe.transpose(ps[:, t, L:N], xin[0:B, 2, t * P:(t + 1) * P], C("ident", B)[:, 0:B]).then_inc(S("par_turned"), 1)

            @blk.vector
            def _(dve):
                for t in range(KT):
                    dve.wait_ge(S("par_turned"), t + 1)
                    dve.tensor_copy(x[:, t, :], ps[:, t, 0:N]).then_inc(S("par_taken"), 1)

            @blk.gpsimd
            def _(pool):
                pool.memset(gate_in[:, :, :], 0.0).then_inc(S("slot_zero"), 1)
                pool.memset(param12[:, :], 0.0).then_inc(S("slot_zero"), 1)
                pool.memset(oms[:, :, :], 0.0).then_inc(S("slot_zero"), 1)
                pool.memset(cum[:, :], 0.0).then_inc(S("slot_zero"), 1)

        nc.all_engine_barrier()
        for s in sems.values():
            nc.gpsimd.sem_clear(s)
        nc.all_engine_barrier()

        with nc.Fori(0, DEPTH) as l:
            with nc.Block() as blk:

                @blk.sync
                def _(sp):
                    def load(name, s, pair, dst, src):
                        if not (isinstance(pair, int) and pair == 0):
                            sp.wait_ge(S(f"w_lo{s}"), 2 * pair)
                        sp.dma_start(dst, src).then_inc(S(f"w_raw{s}"), 16)

                    def wide(s, pair, w, j):
                        load("", s, pair, kt_view(raw[s][:, :], 8),
                             w.rearrange("(k p) m -> p k m", p=P)[:, :, bass.ds(j * 256, 256)])

                    def gu(k, j):
                        base = P0[f"gu{k}"]
                        wide(0, base + j, io[f"ffn{k}_gate"][l], j)
                        wide(1, base + j, io[f"ffn{k}_up"][l], j)

                    def dn(k, j):
                        base = P0[f"dn{k}"]
                        v = io[f"ffn{k}_down"][l].rearrange("(k p) m -> p k m", p=P)
                        for s in range(2):
                            load("", s, base + j, kt_view(raw[s][:, 0:1408], 11), v[:, 11 * s:11 * s + 11, bass.ds(j * P, P)])

                    g48 = io["norm_g"][l].rearrange("i (t p) -> (i t) p", p=P)
                    sp.dma_start(gin[0:48, :], g48).then_inc(S("par_in"), 16)
                    sp.dma_start(win[:, :, :], io["gmlp_ws"][l].rearrange("g t s -> t g s")).then_inc(S("par_in"), 16)
                    sp.dma_start(bin_[:, :], io["gmlp_bs"][l]).then_inc(S("par_in"), 16)
                    sp.wait_ge(S("cw_zero"), 1)
                    sp.dma_start(cwin[:, COFF:COFF + 768], io["gdn_conv_w"][l]).then_inc(S("par_in"), 16)
                    bc = lambda ap, n, parts=P: ap.rearrange("(o n) -> o n", o=1).broadcast_to([parts, n])
                    for dst, src, n in ((param12[:, 0:4], io["fox_bias"], 4), (param12[:, 4:8], io["gdn_dt_bias"], 4),
                                        (a_log[:, :], io["gdn_a_log"], 4), (gv[:, :], io["gmlp_norm_g"], GW)):
                        sp.dma_start(dst, bc(src[l], n)).then_inc(S("row_in"), 16)
                    sp.dma_start(og[:, :], bc(io["out_norm_g"][l].rearrange("m h d -> (m h d)"), D)).then_inc(S("row_in"), 16)
                    with nc.allow_non_contiguous_dma(reason="eight values"):
                        sp.dma_start(ws0[:, 0, :], io["gmlp_ws"][l][:, 0, 0:1].rearrange("g o -> o g").broadcast_to([B, H])).then_inc(S("row_in"), 16)
                        sp.dma_start(ws0[:, 1, :], io["gmlp_bs"][l][:, 0:1].rearrange("g o -> o g").broadcast_to([B, H])).then_inc(S("row_in"), 16)
                    for j in range(4):
                        sp.dma_start(d_cw[j], io["gdn_conv_w"][l, j:j + 1].rearrange("o (c f) -> c o f", c=3).broadcast_to([3, B, GW])).then_inc(S("conv_pre"), 16)
                    for j in range(3):
                        sp.dma_start(d_cold[j], io["state_gdn_conv"][:, l, j].rearrange("b (c f) -> c b f", c=3)).then_inc(S("conv_pre"), 16)
                    sp.wait_ge(S("conv_pre"), 7 * 16)
                    sp.dma_start(cv[:, 0:4, :], d_cw.rearrange("j c b (h e) -> (c b h) j e", h=H)).then_inc(S("conv_in"), 16)
                    sp.dma_start(cv[:, 4:7, :], d_cold.rearrange("j c b (h e) -> (c b h) j e", h=H)).then_inc(S("conv_in"), 16)

                    gu(1, 0)
                    with sp.Fori(0, B * NPG) as i:
                        page = sp.value_load(ptab[0:1, bass.ds(i, 1)], min_val=0, max_val=io["n_pool"] - 1)
                        sp.dma_start(d_logf[bass.ds(i, 1)], io["cache_fox_logf"][bass.ds(page, 1), l].rearrange("o p h -> o (p h)")).then_inc(S("logf_pre"), 16)
                    with sp.Fori(1, GU_P) as j:
                        gu(1, j)
                    with sp.Fori(0, DN_P) as j:
                        dn(1, j)
                    with sp.Fori(0, WI_P - 1) as j:
                        for s in range(2):
                            load("", s, P0["wi"] + j, kt_view(raw[s][:, :], 8),
                                 io["w_in"][l].rearrange("(k p) m -> p k m", p=P)[:, :, bass.ds(j * 512 + s * 256, 256)])
                    for s in range(2):
                        load("", s, P0["wi"] + WI_P - 1, kt_view(raw[s][:, 0:512], 4),
                             io["w_in"][l].rearrange("(k p) m -> p k m", p=P)[:, 4 * s:4 * s + 4, PW - P:PW])
                    sp.wait_ge(S("logf_pre"), 16 * B * NPG)
                    sp.wait_ge(S("n_ready"), 16)
                    sp.dma_start(otok[0:B * NPG, 0, 0:512], d_logf).then_inc(S("logf_in"), 16)

                    def keys(i, b):
                        for g in range(NPG):
                            page = sp.value_load(ptab[0:1, bass.ds(b * NPG + g, 1)], min_val=0, max_val=io["n_pool"] - 1)
                            sp.dma_start(kslot[:, i, g, :], io["cache_fox_k"][bass.ds(page, 1), l].rearrange("o p h d -> p (o h d)")).then_inc(S(f"k_in{i}"), 16)
                            sp.dma_start(vslot[:, i, g, 0:GW], io["cache_fox_v"][bass.ds(page, 1), l].rearrange("o p h d -> p (o h d)")).then_inc(S(f"v_in{i}"), 16)
                        for src, dst, m, sem in (("state_swa_k", kslot, GW, "k_in"), ("state_swa_v", vslot, GW, "v_in")):
                            a = io[src][bass.ds(b, 1), l].rearrange("o r h d -> r (o h d)")
                            sp.dma_start(dst[:, i, NPG, 0:m], a[PAST - P:PAST, :]).then_inc(S(f"{sem}{i}"), 16)
                            sp.dma_start(dst[:, i, NPG + 1, 0:m], a[PAST - 4 * P:PAST, :].rearrange("(r f) d -> r f d", f=4)[:, 0, :]).then_inc(S(f"{sem}{i}"), 16)
                            sp.dma_start(dst[0:PAST // 16, i, NPG + 2, 0:m], a[0:PAST, :].rearrange("(r f) d -> r f d", f=16)[:, 0, :]).then_inc(S(f"{sem}{i}"), 16)

                    def queries(i, b):
                        sp.dma_start(q_bc[:, i, :], d_q[bass.ds(b, 1)].broadcast_to([P, 512])).then_inc(S(f"q_in{i}"), 16)

                    for s in range(2):
                        sp.wait_ge(S(f"mm_done{s}"), M0["wo"])
                    sp.wait_ge(S("slot_zero"), 4)
                    for i in range(2):
                        keys(i, i)
                    st = S("stored")
                    sp.wait_ge(S("tok_act"), 14)
                    sp.wait_ge(S("tok_dve"), 7)
                    for c in range(3):
                        sp.dma_start(d_cnew[c], smp[:, QC + c * GW:QC + (c + 1) * GW]).then_inc(S("regroup"), 16)
                    sp.wait_ge(S("regroup"), 48)
                    sp.dma_start(cv[:, 7, :], d_cnew.rearrange("c b (h e) -> (c b h) e", h=H)).then_inc(S("conv_in"), 16)
                    o = io["outs"]
                    sp.dma_start(o["gdn_conv_prompt"][0, l], tok[P - 3:P, 1, QC:QC + 768]).then_inc(st, 16)
                    sp.dma_start(o["gdn_conv_sample"][:, l, 2], smp[:, QC:QC + 768]).then_inc(st, 16)
                    sp.dma_start(o["gdn_conv_sample"][:, l, 0:2], io["state_gdn_conv"][:, l, 1:3]).then_inc(st, 16)
                    pr = lambda ap: ap.rearrange("(t p) h d -> p t (h d)", p=P)
                    sp.dma_start(pr(o["fox_k_prompt"][0, l]), tok[:, :, KB_:KB_ + GW]).then_inc(st, 16)
                    sp.dma_start(pr(o["fox_v_prompt"][0, l]), tok[:, :, VB_:VB_ + GW]).then_inc(st, 16)
                    sp.dma_start(pr(o["swa_v_prompt"][0, l]), tok[:, :, VA:VA + GW]).then_inc(st, 16)
                    sm = lambda ap: ap.rearrange("b t h d -> b (t h d)")
                    sp.dma_start(sm(o["fox_k_sample"][:, l]), smp[:, KB_:KB_ + GW]).then_inc(st, 16)
                    sp.dma_start(sm(o["fox_v_sample"][:, l]), smp[:, VB_:VB_ + GW]).then_inc(st, 16)
                    sp.dma_start(sm(o["swa_v_sample"][:, l]), smp[:, VA:VA + GW]).then_inc(st, 16)
                    sp.wait_ge(S("rope"), 2)
                    sp.dma_start(pr(o["swa_k_prompt"][0, l]), tok[:, :, KA:KA + GW]).then_inc(st, 16)
                    sp.dma_start(sm(o["swa_k_sample"][:, l]), smp[:, KA:KA + GW]).then_inc(st, 16)
                    sp.dma_start(d_q[:, 0:GW], smp[:, QA:QA + GW]).then_inc(S("q_pre"), 16)
                    sp.dma_start(d_q[:, GW:512], smp[:, QB_:QB_ + GW]).then_inc(S("q_pre"), 16)
                    sp.wait_ge(S("gates"), 1)
                    sp.dma_start(o["fox_logf_prompt"][0, l].rearrange("(t p) h -> p t h", p=P), gate[:, 0:2, 0:4]).then_inc(st, 16)
                    sp.dma_start(o["fox_logf_sample"][:, l].rearrange("b t h -> b (t h)"), gate[0:B, 2, 0:4]).then_inc(st, 16)
                    with nc.allow_non_contiguous_dma(reason="gates of eight samples"):
                        for k in range(2):
                            sp.dma_start(d_gate[:, :, k:k + 1], gate[0:B, 2, 4 + 4 * k:8 + 4 * k].unsqueeze(2)).then_inc(S("gb_pre"), 16)
                    for b in range(B):
                        sp.dma_start(state[16 * b:16 * b + 16, :, :].rearrange("p k v -> p (k v)"),
                                     io["state_gdn_s"][b, l].rearrange("h (c k) v -> (h c) (k v)", c=4)).then_inc(S("state_in"), 16)
                    sp.wait_ge(S("gb_pre"), 32)
                    for c in range(4):
                        sp.dma_start(gb[c:P:4, :], d_gate.rearrange("b h k -> (b h) k")).then_inc(S("state_in"), 16)
                    sp.wait_ge(S("s_conv"), 1)
                    sp.dma_start(d_cn.rearrange("c b (h e) -> (c b h) e", h=H), cv[:, 8, :]).then_inc(S("regroup"), 16)
                    sp.wait_ge(S("regroup"), 64)
                    for k in range(2):
                        sp.dma_start(kq16[:, k, :], d_cn[k].rearrange("b (g e) -> (b g) e", e=16)).then_inc(S("state_in"), 16)
                    for c in range(4):
                        sp.dma_start(v64[c:P:4, :], d_cn[2].rearrange("b (h e) -> (b h) e", e=HD)).then_inc(S("state_in"), 16)
                    sp.wait_ge(S("s_state"), 1)
                    for b in range(B):
                        sp.dma_start(o["gdn_s_sample"][b, l].rearrange("h (c k) v -> (h c) (k v)", c=4),
                                     state[16 * b:16 * b + 16, :, :].rearrange("p k v -> p (k v)")).then_inc(S("s_state_out"), 16)
                    sp.wait_ge(S("s_out"), 1)
                    sp.dma_start(d_oc.rearrange("b (h e) -> (b h) e", e=HD), v64[0:P:4, :]).then_inc(S("regroup"), 16)
                    sp.wait_ge(S("regroup"), 80)
                    sp.dma_start(smp_o[:, 512:768], d_oc).then_inc(S("oc_in"), 16)
                    sp.wait_ge(S("s_state_out"), 16 * B)
                    sp.wait_ge(S("q_pre"), 32)
                    for i in range(2):
                        queries(i, i)
                    with sp.Fori(1, B // 2) as j:
                        for i in range(2):
                            sp.wait_ge(S(f"k_used{i}"), j)
                            sp.wait_ge(S(f"v_used{i}"), j)
                            queries(i, 2 * j + i)
                            keys(i, 2 * j + i)
                    sp.wait_ge(S("gmlp_v"), 1)
                    sp.dma_start(o["gmlp_v_sample"][:, l].rearrange("b t d -> b (t d)"), smp[:, VD:VD + GW]).then_inc(st, 16)
                    sp.wait_ge(S("p_state"), 4)
                    for h in range(H):
                        sp.dma_start(o["gdn_s_prompt"][0, l, h], st_s[64 * (h % 2):64 * (h % 2) + 64, h // 2, :]).then_inc(st, 16)
                    sp.wait_ge(S("mixed"), 1)
                    sp.wait_ge(st, 16 * 18)
                    for j in range(WO_P):
                        for s in range(2):
                            load("", s, P0["wo"] + j, kt_view(raw[s][:, :], 8),
                                 io["w_out"][l].rearrange("(k p) m -> p k m", p=P)[:, :, j * 512 + s * 256:j * 512 + s * 256 + 256])
                    with sp.Fori(0, GU_P) as j:
                        gu(2, j)
                    with sp.Fori(0, DN_P) as j:
                        dn(2, j)

                @blk.scalar
                def _(act):
                    ch = Chain(act, "act_ch")
                    last = lambda n: {"wi": "wi_last"}.get(n, n)

                    def hi(n, j, s, special=None):
                        pair = P0[n] + j
                        act.wait_ge(S(f"w_raw{s}"), 16 * (pair + 1))
                        done = M0[n] + INC[n] * j
                        if not (isinstance(done, int) and done == 0):
                            act.wait_ge(S(f"mm_done{s}"), done)
                        for a, b in HALVES[special or n]:
                            act.activation(whi[s][:, a:b], raw[s][:, a:b], ACT.Copy).then_inc(S(f"w_hi{s}"), 1)

                    def gu_step(k, j, nxt):
                        n = f"gu{k}"
                        for f in range(2):
                            act.wait_ge(S("mm_done0"), M0[n] + 2 * j + f + 1)
                            act.activation(s_t[:, f, :], ps[:, f, 0:N], ACT.Silu).then_inc(S("gate_taken"), 1)
                        hi(*nxt, 0)
                        for f in range(2):
                            act.wait_ge(S("up_taken"), 22 * (k - 1) + 2 * j + f + 3)
                            act.activation(hhi[:, bass.ds(2 * j + f, 1), :].rearrange("p o n -> p (o n)"),
                                           h_t[:, f, :], ACT.Copy).then_inc(S("h_hi"), 1)
                        hi(*nxt, 1)

                    def evac_y(n, e, t, bank, s, i):
                        act.activation(yt[:, bass.ds(t, 1), :].rearrange("p o n -> p (o n)"), ps[:, bank, 0:N], ACT.Copy).then_inc(S("y_copied"), 1)
                        act.activation(sq8[:, bass.ds(t, 1), :].rearrange("p o n -> p (o n)"), ps[:, bank, 0:N], ACT.Square).then_inc(S("sq"), 1)

                    def dn_pair(k, q, nxt):
                        n, e = f"dn{k}", {1: 1, 2: 5}[k]
                        for m in range(2):
                            j = 2 * q + m
                            if nxt[m]:
                                hi(*nxt[m], 0)
                            act.wait_ge(S("mm_done1"), M0[n] + j + 1)
                            evac_y(n, e, j, 4 + m, 1, 0)
                            if nxt[m]:
                                hi(*nxt[m], 1)

                    def rsqrt_of(e):
                        act.wait_ge(S("ss"), e + 1)
                        ch(act.activation(r_post[:, :], ps[:, 7, 0:N], ACT.Ln, bias=C("eps"), scale=1.0 / D))
                        act.activation(r_post[:, :], r_post[:, :], ACT.Exp, scale=-0.5).then_inc(S("r"), 1)

                    def pre(e):
                        for t in range(KT):
                            act.wait_ge(S("x_new"), 8 * (e // 2) + t + 1)
                            act.activation(sq8[:, t, :], x[:, t, :], ACT.Square).then_inc(S("sq"), 1)
                        rsqrt_of(e)
                        for t in range(KT):
                            act.wait_ge(S("n_full"), 8 * (e // 2) + t + 1)
                            act.activation(nhi[:, t, :], yt[:, t, :], ACT.Copy).then_inc(S("n_hi"), 1)

                    act.sem_inc(S("gate_taken"), 2)
                    act.sem_inc(S("pa_taken"), 2)
                    act.wait_ge(S("row_in"), 7 * 16)
                    act.activation(mul12[:, 4:8], a_log[:, :], ACT.Exp).then_inc(S("a_exp"), 1)
                    hi("gu1", 0, 0)
                    hi("gu1", 0, 1)
                    pre(0)
                    with act.Fori(0, GU_P - 1) as j:
                        gu_step(1, j, ("gu1", j + 1))
                    gu_step(1, GU_P - 1, ("dn1", 0))
                    with act.Fori(0, DN_P // 2 - 1) as q:
                        dn_pair(1, q, [("dn1", 2 * q + 1), ("dn1", 2 * q + 2)])
                    dn_pair(1, DN_P // 2 - 1, [("dn1", DN_P - 1), ("wi", 0)])
                    rsqrt_of(1)
                    pre(2)

                    def wi_step(j, nxt):
                        for i in range(2):
                            act.wait_ge(S("mm_done0"), M0["wi"] + 2 * j + i + 1)
                            act.activation(proj[:, bass.ds(4 * j + i, 1), :].rearrange("p o n -> p (o n)"), ps[:, i, 0:N], ACT.Copy).then_inc(S("pa_taken"), 1)
                        hi("wi", j + 1, 0, special=nxt)
                        hi("wi", j + 1, 1, special=nxt)

                    with act.Fori(0, WI_P - 2) as j:
                        wi_step(j, None)
                    wi_step(WI_P - 2, "wi_last")
                    act.wait_ge(S("mm_done1"), M0["wi"] + TOTAL["wi"])
                    act.activation(proj[:, NPT - 1, :], ps[:, 0, 0:N], ACT.Copy).then_inc(S("pa_taken"), 1)

                    for g in range(7):
                        w = 512 if g < 6 else 12
                        c0 = 0 if g < 6 else P - 12
                        bk = 3 * (g % 2)
                        act.wait_ge(S("turned"), 3 * g + 1)
                        act.activation(tok[:, 0, 512 * g:512 * g + w], ps[:, bk, c0:c0 + w], ACT.Copy).then_inc(S("tok_act"), 1)
                        act.wait_ge(S("turned"), 3 * g + 3)
                        act.activation(smp[:, 512 * g:512 * g + w], ps[0:B, bk + 2, c0:c0 + w], ACT.Copy).then_inc(S("tok_act"), 1)
                    act.wait_ge(S("gate_z"), 1)
                    ch(act.activation(gate_t[:, :, :], gate_in[:, :, :], ACT.Abs))
                    ch(act.activation(gate_t[:, :, :], gate_t[:, :, :], ACT.Exp, scale=-1.0))
                    act.activation(gate_t[:, :, :], gate_t[:, :, :], ACT.Ln, bias=1.0).then_inc(S("gate_ln"), 1)
                    act.wait_ge(S("gate_sp"), 1)
                    act.activation(gate[:, :, 8:12], gate[:, :, 8:12], ACT.Exp).then_inc(S("gates"), 1)
                    act.wait_ge(S("cum_sb"), 2)
                    ch(act.activation(eg[:, 0:2, :], eg[:, 0:2, :], ACT.Exp))
                    act.activation(eg[:, 2, :], eg[:, 2, :], ACT.Exp).then_inc(S("eg"), 1)
                    act.wait_ge(S("dt_masked"), 1)
                    act.activation(dt_[:, :, :], dt_[:, :, :], ACT.Exp).then_inc(S("dt"), 1)
                    act.wait_ge(S("tok_dve"), 7)
                    act.activation(tok[:, :, ZC:ZC + GW], tok[:, :, ZC:ZC + GW], ACT.Silu).then_inc(S("silu_z"), 1)
                    act.activation(smp[:, ZC:ZC + GW], smp[:, ZC:ZC + GW], ACT.Silu).then_inc(S("silu_z"), 1)
                    for t in range(NCT):
                        act.wait_ge(S("conv"), t + 1)
                        act.activation(conv_t[:, t, :], conv_t[:, t, :], ACT.Silu).then_inc(S("conv_silu"), 1)
                    act.wait_ge(S("s_conv_raw"), 1)
                    act.activation(cv[:, 8, :], cv[:, 7, :], ACT.Silu).then_inc(S("s_silu"), 1)
                    act.activation(tok[:, :, UD:UD + 512], tok[:, :, UD:UD + 512], ACT.Gelu_apprx_tanh).then_inc(S("gelu"), 1)
                    act.activation(smp[:, UD:UD + 512], smp[:, UD:UD + 512], ACT.Gelu_apprx_tanh).then_inc(S("gelu"), 1)
                    act.wait_ge(S("ck_turned"), 1)
                    act.activation(ck[:, 0, 0:512], ps[:, 6, :], ACT.Copy).then_inc(S("ck_act"), 1)
                    act.activation(ck[:, 0, 512:896], ps[:, 7, 0:384], ACT.Copy).then_inc(S("ck_act"), 1)
                    def softmax(m):
                        act.wait_ge(S("row_max"), m + 1)
                        for h in range(H):
                            for t in range(NT):
                                sl = smx[:, h, 0:P] if t == 0 else smx[:, h, P:3 * P]
                                act.activation(sl, sl, ACT.Exp, bias=small[:, 32 + 4 * t + h:33 + 4 * t + h],
                                               accum_out=small[:, 40 + 4 * t + h:41 + 4 * t + h]).then_inc(S("p_exp"), 1)
                        for i, k in enumerate((0, 2)):
                            act.wait_ge(S("p_turned"), 3 * m + k + 1)
                            act.activation(ptr[:, k, :], ps[:, k, :], ACT.Copy).then_inc(S("ptr_act"), 1)

                    softmax(0)
                    act.wait_ge(S("mix_ss"), 1)
                    ch(act.activation(small[0:64, 0:1], small[0:64, 0:1], ACT.Ln, bias=C("eps", 64)))
                    act.activation(small[0:64, 0:1], small[0:64, 0:1], ACT.Exp, scale=-0.5).then_inc(S("mix_r"), 1)
                    act.wait_ge(S("qk_turned"), 1)
                    act.activation(qkT[:, :, 0:P], ps[:, 4, :].rearrange("p (t n) -> p t n", t=4), ACT.Copy).then_inc(S("qk_act"), 1)
                    softmax(1)
                    act.wait_ge(S("mix_ss"), 2)
                    ch(act.activation(small[:, 8:24], small[:, 8:24], ACT.Ln, bias=C("eps")))
                    act.activation(small[:, 8:24], small[:, 8:24], ACT.Exp, scale=-0.5).then_inc(S("mix_r"), 1)
                    act.wait_ge(S("mix_ss"), 3)
                    ch(act.activation(small[:, 24:27], small[:, 24:27], ACT.Ln, bias=C("eps"), scale=1.0 / GW))
                    act.activation(small[:, 24:27], small[:, 24:27], ACT.Exp, scale=-0.5).then_inc(S("mix_r"), 1)

                    act.wait_ge(S("kq_turned"), 1)
                    act.activation(kqT[:, 0:2, :, 0:P], ps[:, 4, :].rearrange("p (k a n) -> p k a n", k=2, a=2), ACT.Copy).then_inc(S("kq_act"), 1)
                    act.activation(kqT[:, 2, :, 0:P], ps[:, 5, 0:256].rearrange("p (a n) -> p a n", a=2), ACT.Copy).then_inc(S("kq_act"), 1)
                    act.wait_ge(S("tt_turned"), 2)
                    for t in range(NT):
                        act.activation(tm[:, t, :], ps[:, 4 + t, :], ACT.Copy).then_inc(S("tm_act"), 1)
                    act.wait_ge(S("state_in"), 16 * (B + 4 + 2 + 4))
                    act.activation(small[:, 120:121], gb[:, 0:1], ACT.Exp).then_inc(S("sg"), 1)

                    with act.Fori(0, B // 2) as j:
                        act.wait_ge(S("s13"), j + 1)
                        act.activation(s13[:, :, :, :], s13[:, :, :, :], ACT.Exp).then_inc(S("s_exp"), 1)

                    act.wait_ge(S("mix_ss"), 4)
                    ch(act.activation(small[:, 64:96], small[:, 64:96], ACT.Ln, bias=C("eps"), scale=1.0 / HD))
                    act.activation(small[:, 64:96], small[:, 64:96], ACT.Exp, scale=-0.5).then_inc(S("mix_r"), 1)
                    act.wait_ge(S("mix_ss"), 5)
                    ch(act.activation(small[0:B, 96:112], small[0:B, 96:112], ACT.Ln, bias=C("eps", B), scale=1.0 / HD))
                    act.activation(small[0:B, 96:112], small[0:B, 96:112], ACT.Exp, scale=-0.5).then_inc(S("mix_r"), 1)
                    for t in range(KT):
                        act.wait_ge(S("o_turned"), t + 1)
                        act.activation(nhi[:, t, :], ps[:, t, 0:N], ACT.Copy).then_inc(S("o_hi"), 1)

                    hi("wo", 0, 0)
                    hi("wo", 0, 1)
                    for j in range(WO_P):
                        nxt = ("wo", 1) if j == 0 else ("gu2", 0)
                        for s in range(2):
                            for i in range(2):
                                act.wait_ge(S(f"mm_done{s}"), M0["wo"] + 2 * j + i + 1)
                                evac_y("wo", 3, 4 * j + 2 * s + i, 2 * s + i, s, i)
                            hi(*nxt, s)
                    rsqrt_of(3)
                    pre(4)
                    with act.Fori(0, GU_P - 1) as j:
                        gu_step(2, j, ("gu2", j + 1))
                    gu_step(2, GU_P - 1, ("dn2", 0))
                    with act.Fori(0, DN_P // 2 - 1) as q:
                        dn_pair(2, q, [("dn2", 2 * q + 1), ("dn2", 2 * q + 2)])
                    dn_pair(2, DN_P // 2 - 1, [("dn2", DN_P - 1), None])
                    rsqrt_of(5)

                @blk.gpsimd
                def _(pool):
                    ch = Chain(pool, "pool_ch")
                    tt_ = pool.tensor_tensor

                    def sumsq(e):
                        pool.wait_ge(S("sq"), 8 * e + 2)
                        ch(tt_(ss_acc[:, :], sq8[:, 0, :], sq8[:, 1, :], ALU.add))
                        for t in range(2, KT):
                            pool.wait_ge(S("sq"), 8 * e + t + 1)
                            ins = tt_(ss_acc[:, :], ss_acc[:, :], sq8[:, t, :], ALU.add)
                            if t < KT - 1:
                                ch(ins)
                            else:
                                ins.then_inc(S("ss_acc"), 1)

                    ch(pool.memset(cwin[:, :], 0.0))
                    pool.sem_inc(S("cw_zero"), 1)
                    for e in range(3):
                        sumsq(e)
                    for s in range(2):
                        pool.wait_ge(S(f"mm_done{s}"), M0["wo"])
                    for i in range(2):
                        if i:
                            pool.wait_ge(S("slot_ones"), i)
                        pool.memset(kslot[64:P, i, NPG + 2, :], 0.0).then_inc(S("slot_zero"), 1)
                        pool.wait_ge(S("slot_zero"), 2 * i + 1)
                        pool.memset(vslot[64:P, i, NPG + 2, :], 0.0).then_inc(S("slot_zero"), 1)
                        pool.wait_ge(S("slot_zero"), 2 * i + 2)
                        pool.memset(vslot[:, i, :, GW:GW + 1], 1.0).then_inc(S("slot_ones"), 1)
                    pool.wait_ge(S("conv_in"), 48)
                    acc = cv[:, 7, :]
                    ch(tt_(acc, acc, cv[:, 3, :], ALU.mult))
                    for j in range(3):
                        ch(tt_(cv[:, 4 + j, :], cv[:, 4 + j, :], cv[:, j, :], ALU.mult))
                    ch(tt_(cv[:, 4, :], cv[:, 4, :], cv[:, 5, :], ALU.add))
                    ch(tt_(cv[:, 4, :], cv[:, 4, :], cv[:, 6, :], ALU.add))
                    tt_(acc, acc, cv[:, 4, :], ALU.add).then_inc(S("s_conv_raw"), 1)
                    for j in range(B // 2):
                        pool.wait_ge(S("s_max"), j + 1)
                        pool.partition_all_reduce(pmax_all[:, :, :, :].rearrange("p a m h -> p (a m h)"),
                                                  pmax[:, :, :, :].rearrange("p a m h -> p (a m h)"), P, RMAX).then_inc(S("s_max_all"), 1)
                    for e in range(3, 6):
                        sumsq(e)

                @blk.vector
                def _(dve):
                    ch = Chain(dve, "dve_ch")
                    tt2, ts, stt, red = dve.tensor_tensor, dve.tensor_scalar, dve.scalar_tensor_tensor, dve.tensor_reduce

                    def lo(n, j, s, special=None):
                        for i, (a, b) in enumerate(HALVES[special or n]):
                            dve.wait_ge(S(f"w_hi{s}"), 2 * (P0[n] + j) + i + 1)
                            tt2(wlo[s][:, a:b], raw[s][:, a:b], whi[s][:, a:b].bitcast(F32), ALU.subtract).then_inc(S(f"w_lo{s}"), 1)

                    def gu_step(k, j, nxt):
                        n = f"gu{k}"
                        lo(*nxt, 0)
                        for f in range(2):
                            dve.wait_ge(S("mm_done1"), M0[n] + 2 * j + f + 1)
                            dve.wait_ge(S("gate_taken"), 22 * (k - 1) + 2 * j + f + 3)
                            tt2(h_t[:, f, :], s_t[:, f, :], ps[:, 2 + f, 0:N], ALU.mult).then_inc(S("up_taken"), 1)
                            dve.wait_ge(S("h_hi"), 22 * (k - 1) + 2 * j + f + 1)
                            at = bass.ds(2 * j + f, 1)
                            tt2(hlo[:, at, :].rearrange("p o n -> p (o n)"), h_t[:, f, :],
                                hhi[:, at, :].rearrange("p o n -> p (o n)").bitcast(F32), ALU.subtract).then_inc(S("h_ready"), 1)
                        lo(*nxt, 1)

                    def post(e):
                        dve.wait_ge(S("r"), e + 1)
                        dve.wait_ge(S("y_copied"), 8 * (e // 2 + 1))
                        for t in range(KT):
                            ch(stt(yt[:, t, :], yt[:, t, :], gains[:, 8 * e + t:8 * e + t + 1], r_post[:, :], ALU.mult, ALU.mult))
                            tt2(x[:, t, :], x[:, t, :], yt[:, t, :], ALU.add).then_inc(S("x_new"), 1)

                    def pre(e):
                        dve.wait_ge(S("r"), e + 1)
                        for t in range(KT):
                            stt(yt[:, t, :], x[:, t, :], gains[:, 8 * e + t:8 * e + t + 1], r_post[:, :], ALU.mult, ALU.mult).then_inc(S("n_full"), 1)
                            if t:
                                lo_n(e, t - 1)
                        lo_n(e, KT - 1)

                    def lo_n(e, t):
                        dve.wait_ge(S("n_hi"), 8 * (e // 2) + t + 1)
                        tt2(nlo[:, t, :], yt[:, t, :], nhi[:, t, :].bitcast(F32), ALU.subtract).then_inc(S("n_ready"), 1)

                    dve.sem_inc(S("up_taken"), 2)
                    dve.sem_inc(S("pd_taken"), 2)
                    dve.sem_inc(S("x_new"), 8)
                    lo("gu1", 0, 0)
                    lo("gu1", 0, 1)
                    dve.wait_ge(S("par_turned"), 1)
                    ch(dve.tensor_copy(gains[:, :], ps[:, 0, 0:48]))
                    dve.wait_ge(S("par_turned"), 3)
                    tt2(wst[:, :, :], ps[:, 1, :].rearrange("p (g t) -> p g t", g=H), C("upto").unsqueeze(1).broadcast_to([P, H, P]), ALU.mult).then_inc(S("par_taken"), 1)
                    dve.tensor_copy(bst[:, :], ps[:, 2, 0:H]).then_inc(S("par_taken"), 1)
                    dve.tensor_copy(cwt[:, :, :], ps[:, 3, 0:28].rearrange("p (t j) -> p t j", j=4)).then_inc(S("par_taken"), 1)
                    for e in (1, 5):
                        ch(ts(gains[:, 8 * e:8 * e + 8], gains[:, 8 * e:8 * e + 8], 0.5, None, ALU.mult))
                    dve.wait_ge(S("a_exp"), 1)
                    ch(ts(mul12[:, 4:8], mul12[:, 4:8], -1.0, None, ALU.mult))
                    ch(dve.memset(mul12[:, 0:4], -1.0))
                    ch(dve.memset(mul12[:, 8:12], -1.0))
                    pre(0)
                    with dve.Fori(0, GU_P - 1) as j:
                        gu_step(1, j, ("gu1", j + 1))
                    gu_step(1, GU_P - 1, ("dn1", 0))
                    with dve.Fori(1, DN_P) as j:
                        lo("dn1", j, 0)
                        lo("dn1", j, 1)
                    lo("wi", 0, 0)
                    lo("wi", 0, 1)
                    post(1)
                    pre(2)

                    def wi_step(j, nxt):
                        lo("wi", j + 1, 0, special=nxt)
                        for i in range(2):
                            dve.wait_ge(S("mm_done1"), M0["wi"] + 2 * j + i + 1)
                            dve.tensor_copy(proj[:, bass.ds(4 * j + 2 + i, 1), :].rearrange("p o n -> p (o n)"), ps[:, 2 + i, 0:N]).then_inc(S("pd_taken"), 1)
                        lo("wi", j + 1, 1, special=nxt)

                    with dve.Fori(0, WI_P - 2) as j:
                        wi_step(j, None)
                    wi_step(WI_P - 2, "wi_last")

                    for g in range(7):
                        w = 512 if g < 6 else 12
                        c0 = 0 if g < 6 else P - 12
                        dve.wait_ge(S("turned"), 3 * g + 2)
                        dve.tensor_copy(tok[:, 1, 512 * g:512 * g + w], ps[:, 3 * (g % 2) + 1, c0:c0 + w]).then_inc(S("tok_dve"), 1)
                    dve.wait_ge(S("tok_dve"), 7)
                    dve.wait_ge(S("tok_act"), 14)
                    dve.wait_ge(S("row_in"), 7 * 16)
                    dve.tensor_copy(gate_in[:, 0:2, 0:4], tok[:, :, FB:FB + 4])
                    dve.tensor_copy(gate_in[:, 0:2, 4:12], tok[:, :, AC:AC + 8])
                    dve.tensor_copy(gate_in[0:B, 2, 0:4], smp[:, FB:FB + 4])
                    ch(dve.tensor_copy(gate_in[0:B, 2, 4:12], smp[:, AC:AC + 8]))
                    ch(tt2(gate_in[:, :, :], gate_in[:, :, :], param12[:, :].unsqueeze(1).broadcast_to([P, 3, 12]), ALU.add))
                    tt2(gate_in[:, :, :], gate_in[:, :, :], C("sign").unsqueeze(1).broadcast_to([P, 3, 12]), ALU.mult).then_inc(S("gate_z"), 1)
                    def rope(src, parts, t, cos, sin, w):
                        a, b = src[..., 0:8], src[..., 8:16]
                        sh = [parts, t, 8, 8] if t else [parts, 8, 8]
                        up = lambda c: c.rearrange("p (t f) -> p t f", t=t).unsqueeze(2).broadcast_to(sh) if t else c.unsqueeze(1).broadcast_to(sh)
                        tmp = [w[:, k].rearrange("p (t h f) -> p t h f", t=t, h=8) if t else w[:, k].rearrange("p (h f) -> p h f", h=8) for k in range(4)]
                        if t:
                            for u in range(t):
                                aa, bb = a[:, u], b[:, u]
                                cc, ss = up(cos)[:, u], up(sin)[:, u]
                                tt2(tmp[0][:, u], aa, cc, ALU.mult)
                                tt2(tmp[1][:, u], bb, ss, ALU.mult)
                                tt2(tmp[2][:, u], bb, cc, ALU.mult)
                                ch(tt2(tmp[3][:, u], aa, ss, ALU.mult))
                                tt2(aa, tmp[0][:, u], tmp[1][:, u], ALU.subtract)
                                ins = tt2(bb, tmp[2][:, u], tmp[3][:, u], ALU.add)
                                if u < t - 1:
                                    ch(ins)
                        else:
                            tt2(tmp[0], a, up(cos), ALU.mult)
                            tt2(tmp[1], b, up(sin), ALU.mult)
                            tt2(tmp[2], b, up(cos), ALU.mult)
                            ch(tt2(tmp[3], a, up(sin), ALU.mult))
                            tt2(a, tmp[0], tmp[1], ALU.subtract)
                            ins = tt2(b, tmp[2], tmp[3], ALU.add)
                        ins.then_inc(S("rope"), 1)

                    w4 = sqt[:, 0:512].rearrange("p (k n) -> p k n", k=4)
                    rope(tok[:, :, 0:512].rearrange("p t (h d) -> p t h d", h=8), P, 2, C("cos"), C("sin"), w4)
                    rope(smp[:, 0:512].rearrange("p (h d) -> p h d", h=8), B, 0, C("cos_s", B), C("sin_s", B), w4[0:B, :, 0:64])
                    dve.wait_ge(S("gate_ln"), 1)
                    ch(stt(gate[:, :, :], gate_in[:, :, :], 0.0, gate_t[:, :, :], ALU.max, ALU.add))
                    tt2(gate[:, :, :], gate[:, :, :], mul12[:, :].unsqueeze(1).broadcast_to([P, 3, 12]), ALU.mult).then_inc(S("gate_sp"), 1)
                    dve.wait_ge(S("par_taken"), 3)
                    for t in range(NCT):
                        src = proj[:, CT0 + t, :]
                        ch(ts(conv_t[:, t, :], src[:, 0:L], cwt[:, t, 3:4], None, ALU.mult))
                        for k in (1, 2, 3):
                            ins = stt(conv_t[:, t, k:L], src[:, 0:L - k], cwt[:, t, 3 - k:4 - k], conv_t[:, t, k:L], ALU.mult, ALU.add)
                            if k < 3:
                                ch(ins)
                            else:
                                ins.then_inc(S("conv"), 1)
                    dve.wait_ge(S("cum_mm"), 1)
                    dve.tensor_copy(cum[:, :], ps[:, 6, 0:24]).then_inc(S("cum_sb"), 1)
                    dve.wait_ge(S("cum_sb"), 1)
                    cg = cum[:, 0:16].rearrange("p (t k) -> p t k", t=2)[:, :, 4:8]
                    tot = cum[:, 16:24].rearrange("p (t k) -> p t k", t=2)
                    dve.tensor_copy(eg[:, 0, :].rearrange("p (t k) -> p t k", t=2), cg)
                    dve.tensor_copy(eg[:, 1, :].rearrange("p (t k) -> p t k", t=2), tot)
                    tt2(eg[:, 2, :].rearrange("p (t k) -> p t k", t=2), tot, cg, ALU.subtract).then_inc(S("cum_sb"), 1)
                    dve.wait_ge(S("rows_mm"), 1)
                    fr = ps[0:4, 7, 0:256]
                    gr = ps[0:4, 7, 256:512]
                    ts(rows[:, 0, :], fr, 8.0, None, ALU.mult)
                    ts(rows[:, 1, :], fr, -8.0, None, ALU.mult)
                    ts(rows[:, 2, :], gr, 1.0, None, ALU.mult)
                    ts(rows[:, 3, :], gr, -1.0, None, ALU.mult).then_inc(S("rows"), 1)
                    dve.wait_ge(S("dt_mm"), 1)
                    tt2(dt_[:, :, :].rearrange("p t (h i) -> p (t h) i", h=H), ps[:, 4:6, :].rearrange("p t (h i) -> p (t h) i", h=H),
                        C("causal").unsqueeze(1).broadcast_to([P, 2 * H, P]), ALU.add).then_inc(S("dt_masked"), 1)

                    def masked(m, name):
                        dve.wait_ge(S("scores"), m + 1)
                        ch(stt(smx, ps[:, 0:4, 0:384], HD ** -0.5, C(name).unsqueeze(1).broadcast_to([P, H, 384]), ALU.mult, ALU.add))
                        red(small[:, 32:36], smx[:, :, 0:P], AX.X, ALU.max, negate=True)
                        red(small[:, 36:40], smx[:, :, P:3 * P], AX.X, ALU.max, negate=True).then_inc(S("row_max"), 1)

                    def attend_out(m, c0):
                        dve.wait_ge(S("p_turned"), 3 * m + 2)
                        dve.tensor_copy(ptr[:, 1, :], ps[:, 1, :]).then_inc(S("ptr_dve"), 1)
                        dve.wait_ge(S("p_exp"), 8 * (m + 1))
                        ch(dve.reciprocal(small[:, 48:56], small[:, 40:48]))
                        dve.wait_ge(S("o_mm"), m + 1)
                        tt2(otok[:, :, c0:c0 + GW].rearrange("p t (h d) -> p t h d", h=H), ps[:, 3, :].rearrange("p (t h d) -> p t h d", t=2, h=H),
                            small[:, 48:56].rearrange("p (t h) -> p t h", t=2).unsqueeze(3).broadcast_to([P, 2, H, HD]), ALU.mult).then_inc(S("o_att"), 1)

                    masked(0, "fox_mask")
                    dve.wait_ge(S("lf_turned"), 1)
                    dve.tensor_copy(sqt[:, 0:256], ps[:, 6, 0:256]).then_inc(S("lf_sb"), 1)
                    tt2(sqt[0:B, 256:512].rearrange("p (h b g) -> p h b g", h=H, b=B),
                        C("ident", B)[:, 0:B].unsqueeze(1).unsqueeze(3).broadcast_to([B, H, B, NPG]),
                        gate[0:B, 2, 0:4].unsqueeze(2).unsqueeze(3).broadcast_to([B, H, B, NPG]), ALU.mult).then_inc(S("lf_sb"), 1)
                    dve.wait_ge(S("ck_turned"), 2)
                    dve.tensor_copy(ck[:, 1, 0:512], ps[:, 4, :])
                    dve.tensor_copy(ck[:, 1, 512:896], ps[:, 5, 0:384]).then_inc(S("ck_dve"), 1)
                    dve.wait_ge(S("dec_mm"), 1)
                    dve.tensor_copy(bias[:, :, 0:NPG, :], ps[:, 6, 256:512].rearrange("p (h b g) -> p b g h", h=H, b=B))
                    ch(dve.tensor_copy(bias[:, :, NPG:NKT, :], C("window").rearrange("p (g h) -> p g h", h=H).unsqueeze(1).broadcast_to([P, B, CACHE_T, H])))
                    own = v_own[:, 0, 0:GW]
                    for k, (qc, kc) in enumerate(((QB_, KB_), (QA, KA))):
                        ch(tt2(own, smp[:, qc:qc + GW], smp[:, kc:kc + GW], ALU.mult))
                        ch(red(small[0:B, 112 + 4 * k:116 + 4 * k], own.rearrange("p (h d) -> p h d", h=H), AX.X, ALU.add))
                    ch(ts(small[0:B, 112:120], small[0:B, 112:120], HD ** -0.5, None, ALU.mult))
                    ch(dve.tensor_copy(sx[:, :, :, :], C("own_bias").rearrange("p (b k h) -> p b k h", b=B, k=2)))
                    ch(tt2(sx[0:B, :, :, :].rearrange("p b k h -> p b (k h)"), sx[0:B, :, :, :].rearrange("p b k h -> p b (k h)"),
                           small[0:B, 112:120].unsqueeze(1).broadcast_to([B, B, 8]), ALU.add))
                    dve.memset(v_own[:, :, GW:GW + 1], 1.0)
                    ch(dve.tensor_copy(v_own[:, 0, 0:GW], smp[:, VB_:VB_ + GW]))
                    dve.tensor_copy(v_own[:, 1, 0:GW], smp[:, VA:VA + GW]).then_inc(S("v_own"), 1)
                    dve.wait_ge(S("s_silu"), 1)
                    dve.memset(small[64:96, 0:1], 1.0)
                    ch(tt2(cv[0:64, 7, :], cv[0:64, 8, :], cv[0:64, 8, :], ALU.mult))
                    red(small[0:64, 0:1], cv[0:64, 7, :], AX.X, ALU.add).then_inc(S("mix_ss"), 1)
                    attend_out(0, 256)
                    dve.wait_ge(S("mix_r"), 1)
                    ts(cv[:, 8, :], cv[:, 8, :], small[0:96, 0:1], C("q_scale", 96), ALU.mult, ALU.mult).then_inc(S("s_conv"), 1)
                    dve.wait_ge(S("qk_turned"), 1)
                    dve.tensor_copy(qkT[:, :, P:L], ps[:, 5, :].rearrange("p (t n) -> p t n", t=4)).then_inc(S("qk_dve"), 1)
                    masked(1, "swa_mask")
                    dve.wait_ge(S("ck_act"), 2)
                    dve.wait_ge(S("ck_dve"), 1)
                    qk = ck[:, :, COFF:COFF + 512]
                    kb2 = kb_n[:, :, :].rearrange("p t n -> p (t n)")
                    for t in range(NT):
                        ch(tt2(kb2, qk[:, t], qk[:, t], ALU.mult))
                        ins = red(small[:, 8 + 8 * t:16 + 8 * t], kb2.rearrange("p (h d) -> p h d", d=HD), AX.X, ALU.add)
                        if t == 0:
                            ch(ins)
                    ins.then_inc(S("mix_ss"), 1)
                    dve.wait_ge(S("gelu"), 2)
                    dve.wait_ge(S("mix_ss"), 2)
                    for t in range(NT):
                        ch(tt2(kb2[:, 0:GW], tok[:, t, VD:VD + GW], tok[:, t, VD:VD + GW], ALU.mult))
                        ch(red(small[:, 24 + t:25 + t], kb2[:, 0:GW], AX.X, ALU.add))
                    ch(dve.memset(small[:, 26:27], 1.0))
                    ch(tt2(kb2[0:B, 0:GW], smp[:, VD:VD + GW], smp[:, VD:VD + GW], ALU.mult))
                    red(small[0:B, 26:27], kb2[0:B, 0:GW], AX.X, ALU.add).then_inc(S("mix_ss"), 1)
                    attend_out(1, 0)
                    dve.wait_ge(S("mix_r"), 2)
                    for t in range(NT):
                        ch(ts(small[:, 8 + 8 * t:12 + 8 * t], small[:, 8 + 8 * t:12 + 8 * t], HD ** -0.5, None, ALU.mult))
                    for t in range(NT):
                        q8 = qk[:, t].rearrange("p (h d) -> p h d", d=HD)
                        tt2(q8, q8, small[:, 8 + 8 * t:16 + 8 * t].unsqueeze(2).broadcast_to([P, 8, HD]), ALU.mult).then_inc(S("qk_n"), 1)
                    dve.wait_ge(S("qk_n"), 2)
                    dve.wait_ge(S("eg"), 1)
                    dve.wait_ge(S("gates"), 1)
                    k4 = ck[:, :, COFF + GW:COFF + 2 * GW].rearrange("p t (h d) -> p t h d", h=H)
                    v4 = ck[:, :, COFF + 2 * GW:COFF + 3 * GW].rearrange("p t (h d) -> p t h d", h=H)
                    four = lambda ap: ap.rearrange("p t (h d) -> p t h d", h=H)
                    bt = gate[:, 0:2, 8:12].unsqueeze(3).broadcast_to([P, 2, H, HD])
                    tt2(four(kb_n[:, :, :]), k4, bt, ALU.mult).then_inc(S("kb"), 1)
                    tt2(v4, v4, bt, ALU.mult)
                    ch(tt2(four(kd[:, :, :]), k4, eg[:, 2, :].rearrange("p (t k) -> p t k", t=2).unsqueeze(3).broadcast_to([P, 2, H, HD]), ALU.mult))
                    dve.wait_ge(S("kq_turned"), 2)
                    dve.tensor_copy(kqT[:, 0:2, :, P:L], ps[:, 6, :].rearrange("p (k a n) -> p k a n", k=2, a=2))
                    dve.tensor_copy(kqT[:, 2, :, P:L], ps[:, 7, 0:256].rearrange("p (a n) -> p a n", a=2)).then_inc(S("kq_dve"), 1)
                    dve.wait_ge(S("mix_r"), 3)
                    for t in range(NT):
                        ins = stt(tok[:, t, VD:VD + GW], tok[:, t, VD:VD + GW], small[:, 24 + t:25 + t], gv[:, :], ALU.mult, ALU.mult)
                    ins.then_inc(S("v_n"), 1)
                    stt(smp[:, VD:VD + GW], smp[:, VD:VD + GW], small[0:B, 26:27], gv[0:B, :], ALU.mult, ALU.mult).then_inc(S("gmlp_v"), 1)
                    dve.wait_ge(S("gmlp_v"), 1)
                    od = smp_o[:, 768:1024].rearrange("p (h d) -> p h d", h=H)
                    eight = lambda ap: ap.unsqueeze(2).broadcast_to([B, H, HD])
                    ch(tt2(od, smp[:, VD:VD + GW].rearrange("p (h d) -> p h d", h=H), eight(ws0[:, 0, :]), ALU.mult))
                    ch(tt2(od, od, eight(ws0[:, 1, :]), ALU.add))
                    ch(tt2(smp_o[:, 768:1024], smp_o[:, 768:1024], smp[:, UD:UD + GW], ALU.mult))
                    dve.wait_ge(S("gmlp_mm"), 1)
                    mix = otok[:, :, 768:1024]
                    ch(tt2(four(mix), ps[:, 3, :].rearrange("p (t h d) -> p t h d", t=2, h=H), bst[:, :].unsqueeze(1).unsqueeze(3).broadcast_to([P, 2, H, HD]), ALU.add))
                    ch(tt2(mix, mix, tok[:, :, UD:UD + GW], ALU.mult))
                    dve.wait_ge(S("dt"), 1)
                    for t in range(NT):
                        dve.wait_ge(S("kk_mm"), t + 1)
                        kk = ps[:, 4 + 2 * t:6 + 2 * t, :].rearrange("p a (b k i) -> p a b k i", b=2, k=2)
                        h22 = lambda ap: ap.rearrange("p (b a i) -> p a b i", b=2, a=2)
                        h4 = lambda ap: ap.rearrange("p (h i) -> p h i", h=H)
                        ch(tt2(h22(at_[:, t, :]), kk[:, :, :, 0, :], h22(dt_[:, t, :]), ALU.mult))
                        tt2(h22(qkt[:, t, :]), kk[:, :, :, 1, :], h22(dt_[:, t, :]), ALU.mult).then_inc(S("qkt"), 1)
                    h8 = lambda ap: ap.rearrange("p t (h i) -> p (t h) i", h=H)
                    wide = lambda name: C(name).unsqueeze(1).broadcast_to([P, 8, P])
                    tt2(h8(at_[:, :, :]), h8(at_[:, :, :]), wide("strict"), ALU.mult).then_inc(S("at"), 1)
                    dve.wait_ge(S("at"), 1)
                    ch(tt2(h8(tt[:, :, :]), h8(at_[:, :, :]), wide("level1T"), ALU.mult))
                    tt2(h8(tt[:, :, :]), wide("ident"), h8(tt[:, :, :]), ALU.subtract).then_inc(S("tt0"), 1)
                    n = 0
                    for k, b in enumerate(LEVELS):
                        for t in range(NT):
                            dve.wait_ge(S(f"y_mm{t}"), k + 1)
                            m = C(f"level{b}").unsqueeze(1).broadcast_to([P, H, P])
                            tt2(h4(ys[:, t, :]), h4(ps[:, 3 * t, :]), m, ALU.mult).then_inc(S(f"ys{t}"), 1)
                        for t in range(NT):
                            dve.wait_ge(S(f"z_mm{t}"), k + 1)
                            dve.wait_ge(S("tm_act"), 2)
                            if k < len(LEVELS) - 1:
                                tt2(tm[:, t, :], tm[:, t, :], ps[:, 3 * t + 1, :], ALU.subtract)
                            tt2(tt[:, t, :], tt[:, t, :], ps[:, 3 * t + 2, :], ALU.subtract).then_inc(S(f"lev{t}"), 1)
                    dve.wait_ge(S("vn_mm"), 1)
                    dve.tensor_copy(vn[:, 0, :], ps[:, 0, 0:GW]).then_inc(S("vn"), 1)
                    dve.wait_ge(S("oc_mm"), 1)
                    dve.tensor_copy(otok[:, 0, 512:768], ps[:, 1, 0:GW])
                    dve.tensor_copy(st_s[:, :, :], ps[:, 2, 0:128].rearrange("p (a v) -> p a v", a=2)).then_inc(S("st"), 1)
                    dve.wait_ge(S("ks_mm"), 1)
                    e1 = eg[:, 0, 4:8].rearrange("p (b a) -> p a b", a=2).unsqueeze(3).broadcast_to([P, 2, 2, HD])
                    hh = lambda ap: ap.rearrange("p (b a d) -> p a b d", b=2, a=2)
                    ks = lambda kind: ps[:, 3:5, P * kind:P * kind + P].rearrange("p a (b d) -> p a b d", b=2)
                    ch(tt2(hh(kb_n[:, 0, :]), ks(0), e1, ALU.mult))
                    tt2(kb_n[:, 0, :], ck[:, 1, COFF + 2 * GW:COFF + 3 * GW], kb_n[:, 0, :], ALU.subtract).then_inc(S("rhs1"), 1)
                    tt2(hh(kb_n[:, 1, :]), ks(1), e1, ALU.mult)
                    dve.wait_ge(S("vn_mm"), 2)
                    dve.tensor_copy(vn[:, 1, :], ps[:, 0, 0:GW]).then_inc(S("vn"), 1)
                    dve.wait_ge(S("oc_mm"), 2)
                    ch(tt2(otok[:, 1, 512:768], kb_n[:, 1, :], ps[:, 1, 0:GW], ALU.add))
                    for h in range(H):
                        p0 = 64 * (h % 2)
                        sl = st_s[p0:p0 + 64, h // 2, :]
                        stt(sl, sl, eg[p0:p0 + 64, 1, 4 + h:5 + h], ps[p0:p0 + 64, 2, 64 * (h // 2):64 * (h // 2) + 64], ALU.mult, ALU.add).then_inc(S("p_state"), 1)

                    dve.wait_ge(S("state_in"), 16 * (B + 4 + 2 + 4))
                    eb = small[:, 120:122]
                    dve.wait_ge(S("sg"), 1)
                    kc16 = kq16[:, 1, :].unsqueeze(2).broadcast_to([P, 16, HD])
                    qc16 = kq16[:, 0, :].unsqueeze(2).broadcast_to([P, 16, HD])
                    sk = prod[:, 0:4, :].rearrange("p a b -> p (a b)").rearrange("p (k v) -> p k v", k=16)
                    ch(ts(state[:, :, :], state[:, :, :], eb[:, 0:1], None, ALU.mult))
                    ch(tt2(sk, state[:, :, :], kc16, ALU.mult))
                    red(prod[:, 4, 0:HD], sk.rearrange("p k v -> p v k"), AX.X, ALU.add).then_inc(S("sk"), 1)
                    dve.wait_ge(S("sk_mm"), 1)
                    ch(tt2(v64[:, :], v64[:, :], ps[:, 6, 0:HD], ALU.subtract))
                    ch(ts(v64[:, :], v64[:, :], gb[:, 1:2], None, ALU.mult))
                    ch(tt2(sk, kc16, v64[:, :].unsqueeze(1).broadcast_to([P, 16, HD]), ALU.mult))
                    tt2(state[:, :, :], state[:, :, :], sk, ALU.add).then_inc(S("s_state"), 1)
                    dve.wait_ge(S("s_state"), 1)
                    ch(tt2(sk, state[:, :, :], qc16, ALU.mult))
                    red(prod[:, 4, 0:HD], sk.rearrange("p k v -> p v k"), AX.X, ALU.add).then_inc(S("sk"), 1)
                    dve.wait_ge(S("sk_mm"), 2)
                    dve.tensor_copy(v64[:, :], ps[:, 6, 0:HD]).then_inc(S("s_out"), 1)

                    base = ch.n
                    with dve.Fori(0, B // 2) as j:
                        for i in range(2):
                            dve.wait_ge(S(f"k_in{i}"), 16 * (NPG + CACHE_T) * (j + 1))
                            dve.wait_ge(S(f"q_in{i}"), 16 * (j + 1))
                            qb = q_bc[:, i, GW:512].unsqueeze(1).broadcast_to([P, NPG, GW])
                            qa = q_bc[:, i, 0:GW].unsqueeze(1).broadcast_to([P, CACHE_T, GW])
                            if i == 1:
                                dve.wait_ge(S("s_red"), 4 * j + 2)
                            tt2(prod[:, 0:NPG, :], kslot[:, i, 0:NPG, :], qb, ALU.mult)
                            tt2(prod[:, NPG:NKT, :], kslot[:, i, NPG:NKT, :], qa, ALU.mult).then_inc(S(f"k_used{i}"), 1)
                            dve.wait_ge(S(f"k_used{i}"), j + 1)
                            if i == 0:
                                dve.wait_ge(S("pv_ok"), j + 1)
                            four_ = lambda ap: ap.rearrange("p g (h d) -> p g h d", h=H)
                            red(s13[:, i, 0:NPG, :], four_(prod[:, 0:NPG, :]), AX.X, ALU.add).then_inc(S("s_red"), 1)
                            red(s13[:, i, FOX_PG:FOX_PG + CACHE_T, :], four_(prod[:, NPG:NKT, :]), AX.X, ALU.add).then_inc(S("s_red"), 1)
                        dve.wait_ge(S("s_red"), 4 * j + 4)
                        bj = bias[:, bass.ds(2 * j, 2), :, :]
                        sc = HD ** -0.5
                        for i in range(2):
                            f = lambda ap: ap.rearrange("p g h -> p (g h)")
                            stt(f(s13[:, i, 0:NPG, :]), f(s13[:, i, 0:NPG, :]), sc, bj[:, i, 0:NPG, :].rearrange("p g h -> p (g h)"), ALU.mult, ALU.add)
                            stt(f(s13[:, i, FOX_PG:FOX_PG + CACHE_T, :]), f(s13[:, i, FOX_PG:FOX_PG + CACHE_T, :]), sc,
                                bj[:, i, NPG:NKT, :].rearrange("p g h -> p (g h)"), ALU.mult, ALU.add)
                        xj = sx[:, bass.ds(2 * j, 2), :, :]
                        dve.tensor_copy(s13[:, :, NPG, :], xj[:, :, 0, :])
                        dve.tensor_copy(s13[:, :, NPAGE - 1, :], xj[:, :, 1, :]).then_inc(S("s_sc"), 1)
                        dve.wait_ge(S("s_sc"), j + 1)
                        for i in range(2):
                            red(pmax[:, i, 0, :], s13[:, i, 0:FOX_PG, :].rearrange("p g h -> p h g"), AX.X, ALU.max)
                            ins = red(pmax[:, i, 1, :], s13[:, i, FOX_PG:NPAGE, :].rearrange("p g h -> p h g"), AX.X, ALU.max)
                        ins.then_inc(S("s_max"), 1)
                        dve.wait_ge(S("s_max_all"), j + 1)
                        for i in range(2):
                            tt2(s13[:, i, 0:FOX_PG, :], s13[:, i, 0:FOX_PG, :], pmax_all[:, i, 0, :].unsqueeze(1).broadcast_to([P, FOX_PG, H]), ALU.subtract)
                            ins = tt2(s13[:, i, FOX_PG:NPAGE, :], s13[:, i, FOX_PG:NPAGE, :], pmax_all[:, i, 1, :].unsqueeze(1).broadcast_to([P, SWA_PG, H]), ALU.subtract)
                        ins.then_inc(S("s13"), 1)
                        for i in range(2):
                            dve.wait_ge(S("pv_mm"), 2 * j + i + 1)
                            p0 = 32 * i
                            for m in range(2):
                                dve.reciprocal(small[p0:p0 + H, 124 + m:125 + m], ps[p0:p0 + H, 6 + m, GW:GW + 1]).then_inc(S("rc"), 1)
                            dve.wait_ge(S("rc"), 4 * j + 2 * i + 2)
                            for m in range(2):
                                c0 = GW * (1 - m)
                                ins = stt(oms[p0:p0 + H, bass.ds(j, 1), c0:c0 + GW].rearrange("p o n -> p (o n)"), ps[p0:p0 + H, 6 + m, 0:GW],
                                          small[p0:p0 + H, 124 + m:125 + m], const[p0:p0 + H, COL["head_block"][0]:COL["head_block"][0] + GW], ALU.mult, ALU.mult)
                            ins.then_inc(S("oms"), 1)

                    for t in range(NT):
                        ch(tt2(sqt[:, :], otok[:, t, :], otok[:, t, :], ALU.mult))
                        ins = red(small[:, 64 + 16 * t:80 + 16 * t], sqt[:, :].rearrange("p (h d) -> p h d", d=HD), AX.X, ALU.add)
                        if t == 0:
                            ch(ins)
                    ins.then_inc(S("mix_ss"), 1)
                    dve.wait_ge(S("mix_ss"), 4)
                    dve.wait_ge(S("so_mm"), 1)
                    dve.tensor_copy(smp_o[:, 0:512], ps[0:B, 5, :]).then_inc(S("so"), 1)
                    dve.wait_ge(S("so"), 1)
                    dve.wait_ge(S("oc_in"), 16)
                    ch(tt2(sqt[0:B, :], smp_o[:, :], smp_o[:, :], ALU.mult))
                    red(small[0:B, 96:112], sqt[0:B, :].rearrange("p (h d) -> p h d", d=HD), AX.X, ALU.add).then_inc(S("mix_ss"), 1)
                    dve.wait_ge(S("mix_r"), 4)
                    dve.wait_ge(S("silu_z"), 2)
                    for t in range(NT):
                        o16 = otok[:, t, :].rearrange("p (h d) -> p h d", d=HD)
                        ch(tt2(o16, o16, small[:, 64 + 16 * t:80 + 16 * t].unsqueeze(2).broadcast_to([P, 16, HD]), ALU.mult))
                    ch(tt2(otok[:, :, :], otok[:, :, :], og[:, :].unsqueeze(1).broadcast_to([P, 2, D]), ALU.mult))
                    tt2(otok[:, :, 512:768], otok[:, :, 512:768], tok[:, :, ZC:ZC + GW], ALU.mult).then_inc(S("mixed"), 1)
                    dve.wait_ge(S("mix_r"), 5)
                    o16 = smp_o[:, :].rearrange("p (h d) -> p h d", d=HD)
                    ch(tt2(o16, o16, small[0:B, 96:112].unsqueeze(2).broadcast_to([B, 16, HD]), ALU.mult))
                    ch(tt2(smp_o[:, :], smp_o[:, :], og[0:B, :], ALU.mult))
                    tt2(smp_o[:, 512:768], smp_o[:, 512:768], smp[:, ZC:ZC + GW], ALU.mult).then_inc(S("mixed"), 1)
                    for t in range(KT):
                        dve.wait_ge(S("o_hi"), t + 1)
                        tt2(nlo[:, t, :], ps[:, t, 0:N], nhi[:, t, :].bitcast(F32), ALU.subtract).then_inc(S("mix_ready"), 1)

                    lo("wo", 0, 0)
                    lo("wo", 0, 1)
                    for s in range(2):
                        lo("wo", 1, s)
                    for s in range(2):
                        lo("gu2", 0, s)
                    post(3)
                    pre(4)
                    with dve.Fori(0, GU_P - 1) as j:
                        gu_step(2, j, ("gu2", j + 1))
                    gu_step(2, GU_P - 1, ("dn2", 0))
                    with dve.Fori(1, DN_P) as j:
                        lo("dn2", j, 0)
                        lo("dn2", j, 1)
                    post(5)

                @blk.tensor
                def _(pe):
                    mm, tr = pe.matmul, pe.transpose

                    def three(out, s, woff, hi_, lo_, first, last):
                        wh, wl = whi[s][:, woff:woff + P], wlo[s][:, woff:woff + P]
                        mm(out, wh, hi_, start=first, stop=False)
                        mm(out, wh, lo_, start=False, stop=False)
                        return mm(out, wl, hi_, start=False, stop=last)

                    def split_ready(n, j, s, part):
                        pe.wait_ge(S(f"w_lo{s}"), 2 * (P0[n] + j) + part + 1)

                    def wide_chunk(n, j, s, banks, free):
                        for i in range(2):
                            free(i)
                            for k in range(KT):
                                if i == 0 and k in (0, 4):
                                    split_ready(n, j, s, k // 4)
                                ins = three(ps[:, banks[i], 0:N], s, k * 256 + i * P, nhi[:, k, :], nlo[:, k, :], k == 0, k == KT - 1)
                            ins.then_inc(S(f"mm_done{s}"), 1)

                    def gu_step(k, j):
                        n = f"gu{k}"
                        wide_chunk(n, j, 0, (0, 1), lambda i: pe.wait_ge(S("gate_taken"), 22 * (k - 1) + 2 * j + i + 1))
                        wide_chunk(n, j, 1, (2, 3), lambda i: pe.wait_ge(S("up_taken"), 22 * (k - 1) + 2 * j + i + 1))

                    def dn_pair(k, q):
                        n, e = f"dn{k}", {1: 1, 2: 5}[k]
                        for m in range(2):
                            j = 2 * q + m
                            pe.wait_ge(S("sq"), 8 * e + j - 1)
                            for s in range(2):
                                for kk in range(11):
                                    if kk in (0, 6):
                                        split_ready(n, j, s, kk // 6)
                                    t = 11 * s + kk
                                    ins = three(ps[:, 4 + m, 0:N], s, kk * P, hhi[:, t, :], hlo[:, t, :], t == 0, t == FT - 1)
                                ins.then_inc(S(f"mm_done{s}"), 1)

                    def ss(e):
                        pe.wait_ge(S("ss_acc"), e + 1)
                        mm(ps[:, 7, 0:N], ones, ss_acc[:, :], start=True, stop=True).then_inc(S("ss"), 1)

                    pe.wait_ge(S("par_in"), 64)
                    tr(ps[:, 0, 0:48], gin[0:48, :], C("ident", 48)[:, 0:48]).then_inc(S("par_turned"), 1)
                    for g in range(H):
                        tr(ps[:, 1, g * P:(g + 1) * P], win[:, g, :], ident)
                    tr(ps[:, 2, 0:H], bin_[:, :], C("ident", H)[:, 0:H]).then_inc(S("par_turned"), 1)
                    for t in range(NCT):
                        ins = tr(ps[:, 3, 4 * t:4 * t + 4], cwin[:, t * P:(t + 1) * P], C("ident", 4)[:, 0:4])
                    ins.then_inc(S("par_turned"), 1)
                    ss(0)
                    pe.wait_ge(S("par_taken"), 3)
                    pe.wait_ge(S("n_ready"), 8)
                    with pe.Fori(0, GU_P) as j:
                        gu_step(1, j)
                    pe.wait_ge(S("h_ready"), 22)
                    with pe.Fori(0, DN_P // 2) as q:
                        dn_pair(1, q)
                    ss(1)
                    ss(2)
                    pe.wait_ge(S("n_ready"), 16)
                    with pe.Fori(0, WI_P - 1) as j:
                        wide_chunk("wi", j, 0, (0, 1), lambda i: pe.wait_ge(S("pa_taken"), 2 * j + i + 1))
                        wide_chunk("wi", j, 1, (2, 3), lambda i: pe.wait_ge(S("pd_taken"), 2 * j + i + 1))
                    pe.wait_ge(S("pa_taken"), 2 * (WI_P - 1) + 1)
                    for s in range(2):
                        for k in range(4):
                            if k in (0, 2):
                                split_ready("wi", WI_P - 1, s, k // 2)
                            t = 4 * s + k
                            ins = three(ps[:, 0, 0:N], s, k * P, nhi[:, t, :], nlo[:, t, :], t == 0, t == KT - 1)
                        ins.then_inc(S(f"mm_done{s}"), 1)

                    pe.wait_ge(S("pa_taken"), 2 + 2 * (WI_P - 1) + 1)
                    pe.wait_ge(S("pd_taken"), 2 + 2 * (WI_P - 1))
                    for g in range(7):
                        bk = 3 * (g % 2)
                        if g >= 2:
                            pe.wait_ge(S("tok_act"), 2 * (g - 1))
                            pe.wait_ge(S("tok_dve"), g - 1)
                        for part in range(3):
                            for i in range(4 if g < 6 else 1):
                                a, b = (part * P, part * P + P) if part < 2 else (L, N)
                                ins = tr(ps[0:b - a, bk + part, i * P:(i + 1) * P], proj[:, 4 * g + i, a:b], ident)
                            ins.then_inc(S("turned"), 1)
                    pe.wait_ge(S("gates"), 1)
                    mm(ps[:, 6, 0:8], C("upto"), gate[:, 0, 0:8], start=True, stop=True)
                    mm(ps[:, 6, 8:12], ones, gate[:, 0, 0:4], start=True, stop=False)
                    mm(ps[:, 6, 8:12], C("upto"), gate[:, 1, 0:4], start=False, stop=True)
                    mm(ps[:, 6, 12:16], C("upto"), gate[:, 1, 4:8], start=True, stop=True)
                    mm(ps[:, 6, 16:20], ones, gate[:, 0, 4:8], start=True, stop=True)
                    mm(ps[:, 6, 20:24], ones, gate[:, 1, 4:8], start=True, stop=True).then_inc(S("cum_mm"), 1)
                    pe.wait_ge(S("cum_sb"), 1)
                    for k, c0 in enumerate((0, 8, 4, 12)):
                        ins = tr(ps[0:4, 7, k * P:(k + 1) * P], cum[:, c0:c0 + 4], ident)
                    ins.then_inc(S("rows_mm"), 1)
                    pe.wait_ge(S("rows"), 1)
                    hr = lambda h: C("head_rows", 4)[:, h * P:(h + 1) * P]
                    for t in range(NT):
                        for h in range(H):
                            o = ps[:, 4 + t, h * P:(h + 1) * P]
                            mm(o, rows[:, 3, t * P:(t + 1) * P], hr(h), start=True, stop=False)
                            ins = mm(o, hr(h), rows[:, 2, t * P:(t + 1) * P], start=False, stop=True)
                    ins.then_inc(S("dt_mm"), 1)

                    def scores(m, q, k):
                        for h in range(H):
                            p0 = 64 * (h % 2)
                            qh, kh = q(h // 2)[p0:p0 + 64], k(h // 2)[p0:p0 + 64]
                            for c, qt, kt in ((0, 0, 0), (P, 1, 0), (2 * P, 1, 1)):
                                o = ps[:, h, c:c + P]
                                ins = mm(o, qh[:, qt * P:qt * P + P], kh[:, kt * P:kt * P + P], start=True, stop=(m == 1))
                                if m == 0:
                                    mm(o, rows[:, 0, qt * P:qt * P + P], hr(h), start=False, stop=False)
                                    ins = mm(o, hr(h), rows[:, 1, kt * P:kt * P + P], start=False, stop=True)
                        ins.then_inc(S("scores"), 1)

                    scores(0, lambda a: proj[:, 6 + a, :], lambda a: proj[:, 8 + a, :])
                    pe.wait_ge(S("conv_silu"), NCT)
                    pe.wait_ge(S("dt_masked"), 1)
                    for t in range(NT):
                        for c in range(NCT):
                            bk = (6 if t == 0 else 4) + c // 4
                            ins = tr(ps[:, bk, (c % 4) * P:(c % 4 + 1) * P], conv_t[:, c, t * P:(t + 1) * P], ident)
                        ins.then_inc(S("ck_turned"), 1)

                    def turn_p(m):
                        pe.wait_ge(S("p_exp"), 8 * (m + 1))
                        for k in range(3):
                            for h in range(H):
                                ins = tr(ps[:, k, h * P:(h + 1) * P], smx[:, h, k * P:(k + 1) * P], ident)
                            ins.then_inc(S("p_turned"), 1)

                    def values(m, c0):
                        pe.wait_ge(S("ptr_act"), 2 * (m + 1))
                        pe.wait_ge(S("ptr_dve"), m + 1)
                        for h in range(H):
                            hs = slice(h * P, (h + 1) * P)
                            v = lambda t: tok[:, t, c0 + h * HD:c0 + (h + 1) * HD]
                            o0, o1 = ps[:, 3, h * HD:(h + 1) * HD], ps[:, 3, GW + h * HD:GW + (h + 1) * HD]
                            mm(o0, ptr[:, 0, hs], v(0), start=True, stop=True)
                            mm(o1, ptr[:, 1, hs], v(0), start=True, stop=False)
                            ins = mm(o1, ptr[:, 2, hs], v(1), start=False, stop=True)
                        ins.then_inc(S("o_mm"), 1)

                    pe.wait_ge(S("ck_act"), 2)
                    pe.wait_ge(S("logf_in"), 16)
                    lf = otok[0:B * NPG, 0, 0:512].rearrange("p (n h) -> p n h", h=H)
                    for h in range(H):
                        ins = tr(ps[:, 6, h * 64:(h + 1) * 64], lf[:, :, h], C("ident", 64)[:, 0:64])
                    ins.then_inc(S("lf_turned"), 1)
                    pe.wait_ge(S("lf_sb"), 2)
                    lfs = sqt[:, 0:256]
                    dec = ps[:, 6, 256:512]
                    mm(dec, C("after"), lfs, start=True, stop=False)
                    v3 = lambda ap: ap.rearrange("p (q g) -> p q g", g=NPG)
                    for s in range(1, NPG):
                        mm(v3(dec)[:, :, 0:NPG - s], ones, v3(lfs)[:, :, s:NPG], start=False, stop=False, skip_group_check=True)
                    mm(dec, C("ones", B), sqt[0:B, 256:512], start=False, stop=True).then_inc(S("dec_mm"), 1)
                    turn_p(0)
                    values(0, VB_)
                    pe.wait_ge(S("rope"), 2)
                    pe.wait_ge(S("ck_dve"), 1)
                    for t in range(NT):
                        for c in range(4):
                            ins = tr(ps[:, 4 + t, c * P:(c + 1) * P], tok[:, t, c * P:(c + 1) * P], ident)
                    ins.then_inc(S("qk_turned"), 1)
                    pe.wait_ge(S("qk_act"), 1)
                    pe.wait_ge(S("qk_dve"), 1)
                    pe.wait_ge(S("o_att"), 1)
                    scores(1, lambda a: qkT[:, a, :], lambda a: qkT[:, 2 + a, :])
                    turn_p(1)
                    values(1, VA)
                    pe.wait_ge(S("kb"), 1)
                    pe.wait_ge(S("qk_n"), 2)
                    pe.wait_ge(S("dec_mm"), 1)
                    for t in range(NT):
                        kinds = (ck[:, t, COFF + GW:COFF + 2 * GW], kb_n[:, t, :], ck[:, t, COFF:COFF + GW])
                        for k, src in enumerate(kinds):
                            for a in range(2):
                                n = 2 * k + a
                                ins = tr(ps[:, (4, 6)[t] + n // 4, (n % 4) * P:(n % 4 + 1) * P], src[:, a * P:(a + 1) * P], ident)
                        ins.then_inc(S("kq_turned"), 1)
                    pe.wait_ge(S("v_n"), 1)
                    pe.wait_ge(S("o_att"), 2)
                    for t in range(NT):
                        for g in range(H):
                            ins = mm(ps[:, 3, t * GW + g * HD:t * GW + (g + 1) * HD], wst[:, g, :], tok[:, t, VD + g * HD:VD + (g + 1) * HD], start=True, stop=True)
                    ins.then_inc(S("gmlp_mm"), 1)
                    pe.wait_ge(S("kq_act"), 2)
                    pe.wait_ge(S("kq_dve"), 1)
                    for t in range(NT):
                        for h in range(H):
                            p0, a = 64 * (h % 2), h // 2
                            ins = mm(ps[:, (4, 6)[t] + h % 2, (h // 2) * 256:(h // 2) * 256 + 256], kqT[p0:p0 + 64, 0, a, t * P:(t + 1) * P],
                                     kqT[p0:p0 + 64, 1:3, a, t * P:(t + 1) * P], start=True, stop=True)
                        ins.then_inc(S("kk_mm"), 1)
                    pe.wait_ge(S("tt0"), 1)
                    for t in range(NT):
                        for h in range(H):
                            hs = slice(h * P, (h + 1) * P)
                            ins = tr(ps[:, 4 + t, hs], tt[:, t, hs], ident)
                        ins.then_inc(S("tt_turned"), 1)
                    for k in range(len(LEVELS)):
                        for t in range(NT):
                            if k == 0:
                                pe.wait_ge(S("tm_act"), t + 1)
                                if t == 0:
                                    pe.wait_ge(S("gmlp_mm"), 1)
                                    pe.wait_ge(S("tt0"), 1)
                            else:
                                pe.wait_ge(S(f"lev{t}"), k)
                            for h in range(H):
                                hs = slice(h * P, (h + 1) * P)
                                ins = mm(ps[:, 3 * t, hs], at_[:, t, hs], tm[:, t, hs], start=True, stop=True)
                            ins.then_inc(S(f"y_mm{t}"), 1)
                        for t in range(NT):
                            pe.wait_ge(S(f"ys{t}"), k + 1)
                            if k == 0 and t == 0:
                                pe.wait_ge(S("tm_act"), 2)
                            for h in range(H):
                                hs = slice(h * P, (h + 1) * P)
                                if k < len(LEVELS) - 1:
                                    mm(ps[:, 3 * t + 1, hs], tt[:, t, hs], ys[:, t, hs], start=True, stop=True)
                                ins = mm(ps[:, 3 * t + 2, hs], ys[:, t, hs], tt[:, t, hs], start=True, stop=True)
                            ins.then_inc(S(f"z_mm{t}"), 1)
                    nl = len(LEVELS)
                    pe.wait_ge(S("lev0"), nl)
                    pe.wait_ge(S("lev1"), nl)
                    hd = lambda h: slice(h * HD, (h + 1) * HD)
                    hp = lambda h: slice(h * P, (h + 1) * P)

                    def new_values(t, rhs):
                        for h in range(H):
                            ins = mm(ps[:, 0, hd(h)], tt[:, t, hp(h)], rhs[:, hd(h)], start=True, stop=True)
                        ins.then_inc(S("vn_mm"), 1)

                    def out_state(t):
                        pe.wait_ge(S("vn"), t + 1)
                        for h in range(H):
                            mm(ps[:, 1, hd(h)], qkt[:, t, hp(h)], vn[:, t, hd(h)], start=True, stop=True)
                        for h in range(H):
                            p0, a = 64 * (h % 2), h // 2
                            ins = mm(ps[p0:p0 + 64, 2, a * HD:(a + 1) * HD], kd[:, t, hd(h)], vn[:, t, hd(h)], start=True, stop=True)
                        ins.then_inc(S("oc_mm"), 1)

                    new_values(0, ck[:, 0, COFF + 2 * GW:COFF + 3 * GW])
                    out_state(0)
                    pe.wait_ge(S("st"), 1)
                    for kind in (1, 2):
                        for h in range(H):
                            p0, a = 64 * (h % 2), h // 2
                            c = P * (kind - 1) + a * HD
                            ins = mm(ps[:, 3 + h % 2, c:c + HD], kqT[p0:p0 + 64, kind, a, P:L], st_s[p0:p0 + 64, a, :], start=True, stop=True)
                    ins.then_inc(S("ks_mm"), 1)
                    pe.wait_ge(S("rhs1"), 1)
                    new_values(1, kb_n[:, 0, :])
                    out_state(1)
                    for k in range(2):
                        pe.wait_ge(S("sk"), k + 1)
                        mm(ps[:, 6, 0:HD], C("same_state"), prod[:, 4, 0:HD], start=True, stop=True).then_inc(S("sk_mm"), 1)
                    pe.sem_inc(S("pv_ok"), 1)
                    pe.wait_ge(S("slot_ones"), 2)
                    pe.wait_ge(S("slot_zero"), 4)
                    pe.wait_ge(S("v_own"), 1)
                    pe.wait_ge(S("s_out"), 1)
                    pe.wait_ge(S("kk_mm"), 2)
                    with pe.Fori(0, B // 2) as j:
                        pe.wait_ge(S("s_exp"), j + 1)
                        for i in range(2):
                            pe.wait_ge(S(f"v_in{i}"), 16 * (NPG + CACHE_T) * (j + 1))
                            p0 = 32 * i
                            for m, pages, own_page in ((0, range(0, NPG), NPG), (1, range(FOX_PG, FOX_PG + CACHE_T), NPAGE - 1)):
                                o = ps[p0:p0 + H, 6 + m, 0:GW + 1]
                                for g in pages:
                                    src = g if m == 0 else g - 1
                                    mm(o, s13[:, i, g, :], vslot[:, i, src, :], start=(g == pages[0]), stop=False)
                                ins = mm(o, s13[0:B, i, own_page, :], v_own[:, m, :], start=False, stop=True)
                                if m == 1:
                                    ins.then_inc(S("pv_mm"), 1)
                        pe.wait_ge(S("oms"), 2 * j + 2)
                        pe.sem_inc(S("v_used0"), 1)
                        pe.sem_inc(S("v_used1"), 1)
                        pe.sem_inc(S("pv_ok"), 1)
                    for j in range(B // 2):
                        ins = mm(ps[0:B, 5, :], C("to_token", 36)[:, j * B:(j + 1) * B], oms[:, j, :], start=(j == 0), stop=(j == B // 2 - 1))
                    ins.then_inc(S("so_mm"), 1)
                    pe.wait_ge(S("so"), 1)
                    pe.wait_ge(S("mixed"), 2)
                    for t in range(KT):
                        for a in range(NT):
                            tr(ps[:, t, a * P:(a + 1) * P], otok[:, a, t * P:(t + 1) * P], ident)
                        tr(ps[:, t, L:N], smp_o[:, t * P:(t + 1) * P], C("ident", B)[:, 0:B]).then_inc(S("o_turned"), 1)

                    pe.wait_ge(S("mix_ready"), 8)
                    for j in range(WO_P):
                        for s in range(2):
                            wide_chunk("wo", j, s, (2 * s, 2 * s + 1), lambda i: pe.wait_ge(S("sq"), 24 + 4 * j + 2 * s + i - 3) if j else None)
                    ss(3)
                    ss(4)
                    pe.wait_ge(S("n_ready"), 24)
                    with pe.Fori(0, GU_P) as j:
                        gu_step(2, j)
                    pe.wait_ge(S("h_ready"), 44)
                    with pe.Fori(0, DN_P // 2) as q:
                        dn_pair(2, q)
                    ss(5)

            nc.all_engine_barrier()
            for s in sems.values():
                nc.gpsimd.sem_clear(s)
            nc.all_engine_barrier()

        with nc.Block() as blk:
            @blk.tensor
            def _(pe):
                for t in range(KT):
                    if t >= 4:
                        pe.wait_ge(S("par_taken"), 2 * (t - 3))
                    for a in range(NT):
                        pe.transpose(ps[:, 2 * (t % 4), a * P:(a + 1) * P], x[:, t, a * P:(a + 1) * P], ident)
                    pe.transpose(ps[0:B, 2 * (t % 4) + 1, 0:P], x[:, t, L:N], ident).then_inc(S("par_turned"), 1)

            @blk.vector
            def _(dve):
                for t in range(KT):
                    dve.wait_ge(S("par_turned"), t + 1)
                    dve.tensor_copy(xin[:, 0:2, t * P:(t + 1) * P], ps[:, 2 * (t % 4), 0:L].rearrange("p (a n) -> p a n", a=2)).then_inc(S("par_taken"), 1)
                    dve.tensor_copy(xin[0:B, 2, t * P:(t + 1) * P], ps[0:B, 2 * (t % 4) + 1, 0:P]).then_inc(S("par_taken"), 1)

            @blk.sync
            def _(sp):
                sp.wait_ge(S("par_taken"), 16)
                sp.dma_start(io["outs"]["y_prompt"][0].rearrange("(t p) d -> p t d", p=P), xin[:, 0:2, :]).then_inc(S("stored"), 16)
                sp.dma_start(io["outs"]["y_sample"].rearrange("b t d -> (b t) d"), xin[0:B, 2, :]).then_inc(S("stored"), 16)
                sp.wait_ge(S("stored"), 32)


_INS = ["x_prompt", "x_sample", "cache_fox_k", "cache_fox_v", "cache_fox_logf", "page_table", "state_swa_k", "state_swa_v",
        "state_gdn_s", "state_gdn_conv", "norm_g", "w_in", "w_out", "out_norm_g", "fox_bias", "gdn_conv_w", "gdn_a_log",
        "gdn_dt_bias", "gmlp_ws", "gmlp_bs", "gmlp_norm_g", "ffn1_gate", "ffn1_up", "ffn1_down", "ffn2_gate", "ffn2_up", "ffn2_down"]
_OUTS = {
    "y_prompt": (1, L, D), "y_sample": (B, 1, D),
    "fox_k_prompt": (1, DEPTH, L, H, HD), "fox_v_prompt": (1, DEPTH, L, H, HD), "fox_logf_prompt": (1, DEPTH, L, H),
    "fox_k_sample": (B, DEPTH, 1, H, HD), "fox_v_sample": (B, DEPTH, 1, H, HD), "fox_logf_sample": (B, DEPTH, 1, H),
    "swa_k_prompt": (1, DEPTH, L, H, HD), "swa_v_prompt": (1, DEPTH, L, H, HD),
    "swa_k_sample": (B, DEPTH, 1, H, HD), "swa_v_sample": (B, DEPTH, 1, H, HD),
    "gdn_s_prompt": (1, DEPTH, H, HD, HD), "gdn_conv_prompt": (1, DEPTH, 3, 768),
    "gdn_s_sample": (B, DEPTH, H, HD, HD), "gdn_conv_sample": (B, DEPTH, 3, 768),
    "gmlp_v_sample": (B, DEPTH, 1, GW),
}


def kernel(**inputs):
    import numpy as _np
    import concourse.bacc as _bacc
    from concourse import mybir as _mybir
    from concourse.bass_utils import run_bass_kernel_spmd as _run

    nc = _bacc.Bacc("TRN2", target_bir_lowering=False, num_devices=1, dynamic_dma_scratch_size=1024)
    arrays, io = {}, {}
    for name in _INS + ["const"]:
        a = CONST if name == "const" else _np.ascontiguousarray(inputs[name])
        arrays[f"in_{name}_dram"] = a
        io[name] = nc.dram_tensor(f"in_{name}_dram", a.shape, _mybir.dt.from_np(a.dtype), kind="ExternalInput").ap()
    io["n_pool"] = inputs["cache_fox_k"].shape[0]
    io["outs"] = {name: nc.dram_tensor(f"out_{name}_dram", shape, _mybir.dt.from_np(_np.dtype("float32")), kind="ExternalOutput").ap()
                  for name, shape in _OUTS.items()}
    build(nc, io)
    r = _run(nc, [arrays], core_ids=[0])
    return tuple(r.results[0][f"out_{name}_dram"] for name in _OUTS)
```

```python
from contextlib import ExitStack

import numpy as np

import concourse.bass as bass
from concourse import mybir

F32 = mybir.dt.float32
F32R = mybir.dt.float32r
I32 = mybir.dt.int32
ALU = mybir.AluOpType
ACT = mybir.ActivationFunctionType
AX = mybir.AxisListType
RMAX = bass.bass_isa.ReduceOp.max

P = 128
D = 1024
KT = D // P
L = 256
NT = L // P
B = 8
N = L + B
DEPTH = 2
FF = 2816
FT = FF // P
H, HD = 4, 64
GW = H * HD
NPG = 8
PAST = 1024
PW = 3084
NPT = 25
QA, KA, VA, QB_, KB_, VB_, FB, QC, ZC, AC, UD, VD = 0, 256, 512, 768, 1024, 1280, 1536, 1540, 2308, 2564, 2572, 2828
CT0 = QC // P
NCT = 7
COFF = QC - CT0 * P
EPS = 1e-6
NEG = -1e30
CACHE_T = 3
NKT = NPG + CACHE_T
FOX_PG, SWA_PG = NPG + 1, CACHE_T + 1
NPAGE = FOX_PG + SWA_PG
LEVELS = (2, 4, 8, 16, 32, 64)
OROWS = 100


def orow(m, i):
    return 64 * m + 32 * i




def constants():
    i = np.arange(P)
    col, parts = {}, []

    def put(name, a):
        a = np.asarray(a, np.float64).reshape(a.shape[0], -1)
        full = np.zeros((P, a.shape[1]))
        full[:a.shape[0]] = a
        col[name] = (sum(p.shape[1] for p in parts), a.shape[1])
        parts.append(full)

    put("ident", np.eye(P))
    put("upto", (i[:, None] <= i[None, :]))
    put("after", (i[:, None] > i[None, :]))
    put("strict", (i[:, None] < i[None, :]))
    put("ones", np.ones((P, P)))
    put("mean", np.full((P, P), 1 / D))
    put("same_state", (i[:, None] // 4 == i[None, :] // 4))
    put("causal", np.where(i[:, None] <= i[None, :], 0.0, NEG))
    blocks = ((0, 0), (1, 0), (1, 1))
    dist = np.stack([(tq * P + i)[:, None] - (tk * P + i)[None, :] for tq, tk in blocks], 1)
    times = sum(((dist >= 0) & (dist < w) & (dist % d == 0)).astype(float)
                for w, d in ((128, 1), (512, 4), (2048, 16)))
    put("swa_mask", np.where(times > 0, np.log(np.maximum(times, 1)), NEG))
    put("fox_mask", np.where(dist >= 0, 0.0, NEG))
    low = lambda b: ((i[:, None] // (2 * b) == i[None, :] // (2 * b)) & (i[:, None] % (2 * b) >= b)
                     & (i[None, :] % (2 * b) < b))
    put("level1T", low(1).T)
    for b in LEVELS:
        put(f"level{b}", low(b))
    put("head_rows", np.repeat(np.eye(4), P, 1))
    freq = 500000.0 ** (-np.arange(8, dtype=np.float32) / np.float32(8))
    ang = (np.arange(L, dtype=np.float32)[:, None] * freq.astype(np.float32)[None]).astype(np.float32)
    turn = lambda a: a.reshape(NT, P, 8).transpose(1, 0, 2)
    put("cos", turn(np.cos(ang)))
    put("sin", turn(np.sin(ang)))
    last = (np.float32(PAST) * freq.astype(np.float32)).astype(np.float32)
    put("cos_s", np.tile(np.cos(last), (B, 1)))
    put("sin_s", np.tile(np.sin(last), (B, 1)))
    window = np.zeros((P, CACHE_T))
    window[0, 0:2] = NEG
    window[PAST // 16:, 2] = NEG
    put("window", np.repeat(window, H, 1))
    put("own_bias", np.repeat(np.stack([np.where(np.eye(P, B) > 0, 0.0, NEG),
                                        np.where(np.eye(P, B) > 0, np.log(3.0), NEG)], 2), H, 2))
    put("head_block", np.repeat(np.tile(np.eye(4), (OROWS // 4, 1)), HD, 1))
    rows = np.zeros((OROWS, 2, B // 2, B))
    for m in range(2):
        for pair in range(B // 2):
            for k in range(2):
                rows[orow(m, k):orow(m, k) + H, m, pair, 2 * pair + k] = 1
    put("to_token", rows)
    put("eps", np.full((P, 1), EPS))
    scale = np.ones((P, 1))
    scale[0:32] = HD ** -0.5
    put("q_scale", scale)
    put("sign", np.tile(np.repeat([-1.0, 1.0, -1.0], 4), (P, 1)))
    return np.concatenate(parts, 1).astype(np.float32), col


CONST, COL = constants()
NCONST = CONST.shape[1]


def build(nc, io):
    GU_P, DN_P, WI_P, WO_P = FT // 2, KT, 7, 2
    PH = ["gu1", "dn1", "wi", "wo", "gu2", "dn2"]
    PAIRS = dict(zip(PH, [GU_P, DN_P, WI_P, WO_P, GU_P, DN_P]))
    P0 = {n: sum(PAIRS[m] for m in PH[:k]) for k, n in enumerate(PH)}
    INC = {"gu1": 2, "dn1": 1, "wi": 2, "wo": 2, "gu2": 2, "dn2": 1}
    TOTAL = {n: PAIRS[n] * INC[n] - (1 if n == "wi" else 0) for n in PH}
    M0 = {n: sum(TOTAL[m] for m in PH[:k]) for k, n in enumerate(PH)}
    FULL = ((0, 1024), (1024, 2048))
    HALVES = {"gu1": FULL, "dn1": ((0, 768), (768, 1408)), "wi": FULL, "wi_last": ((0, 256), (256, 512)),
              "wo": FULL, "gu2": FULL, "dn2": ((0, 768), (768, 1408))}

    ctx = ExitStack()
    with ctx:
        here = [(nc.sbuf_base + 31) // 32 * 32]

        def place(name, shape, dt=F32, at=None):
            size = 4 * int(np.prod(shape[1:]))
            off = here[0] if at is None else at
            if at is None:
                here[0] += (size + 31) // 32 * 32
            return nc.alloc_sbuf_tensor_at(name, list(shape), dt, offset=off)

        x = place("x", [P, KT, N])
        const = place("const", [P, NCONST])
        ptab = place("ptab", [1, B * NPG], I32)
        r_post = place("r_post", [P, N])
        ss_acc = place("ss_acc", [P, N])
        gains = place("gains", [P, 48])
        param12 = place("param12", [P, 12])
        mul12 = place("mul12", [P, 12])
        a_log = place("a_log", [P, 4])
        gate_in = place("gate_in", [P, 3, 12])
        gate_t = place("gate_t", [P, 3, 12])
        gate = place("gate", [P, 3, 12])
        cum = place("cum", [P, 24])
        eg = place("eg", [P, 3, 8])
        rows = place("rows", [4, 4, L])
        og = place("og", [P, D])
        gv = place("gv", [P, GW])
        wst = place("wst", [P, H, P])
        bst = place("bst", [P, H])
        cwt = place("cwt", [P, NCT, 4])
        ws0 = place("ws0", [B, 2, H])
        small = place("small", [P, 160])
        sx = place("sx", [P, B, 2, H])
        bias = place("bias", [P, B, NKT, H])
        w_at = here[0]
        raw = [place(f"raw{s}", [P, 2048]) for s in range(2)]
        whi = [place(f"whi{s}", [P, 2048], F32R) for s in range(2)]
        wlo = [place(f"wlo{s}", [P, 2048], F32R) for s in range(2)]
        cursor = [w_at]

        def scratch(name, n, shape=None):
            t = place(name, shape or [P, n], at=cursor[0])
            cursor[0] += 4 * n
            assert cursor[0] <= here[0]
            return t

        q_bc = scratch("q_bc", 1024, [P, 2, 512])
        prod = scratch("prod", NKT * GW, [P, NKT, GW])
        state = place("state", [P, 16, HD], at=cursor[0])
        dt_ = scratch("dt_", 1024, [P, 2, 512])
        skp = place("skp", [P, 16, HD], at=cursor[0])
        at_ = scratch("at_", 1024, [P, 2, 512])
        qkt = scratch("qkt", 1024, [P, 2, 512])
        sk_r = place("sk_r", [P, HD], at=cursor[0])
        ys = scratch("ys", 1024, [P, 2, 512])
        conv_t = place("conv_t", [P, NCT, L], at=cursor[0])
        tt = scratch("tt", 1024, [P, 2, 512])
        tm = scratch("tm", 1024, [P, 2, 512])
        kb_n = scratch("kb_n", 512, [P, 2, GW])
        kd = scratch("kd", 512, [P, 2, GW])
        vn = scratch("vn", 512, [P, 2, GW])
        st_s = scratch("st_s", 128, [P, 2, HD])
        k_at = here[0]
        kslot = place("kslot", [P, 2, NKT, GW])
        yt = place("yt", [P, KT, N], at=k_at)
        sq8 = place("sq8", [P, KT, N], at=k_at + 4 * KT * N)
        v_at = here[0]
        vslot = place("vslot", [P, 2, NKT, GW + 1])
        nhi = place("nhi", [P, KT, N], F32R, at=v_at)
        nlo = place("nlo", [P, KT, N], F32R, at=v_at + 4 * KT * N)
        f_at = here[0]
        proj = place("proj", [P, NPT, N])
        tok = place("tok", [P, NT, PW])
        f_end = here[0]
        hhi = place("hhi", [P, FT, N], F32R, at=f_at)
        hlo = place("hlo", [P, FT, N], F32R, at=f_at + 4 * FT * N)
        s_t = place("s_t", [P, 2, N], at=f_at + 8 * FT * N)
        h_t = place("h_t", [P, 2, N], at=f_at + 8 * FT * N + 8 * N)
        assert f_at + 8 * FT * N + 16 * N <= f_end
        xin = place("xin", [P, 3, D], at=f_at)
        gin = place("gin", [P, P], at=f_at)
        win = place("win", [P, H, P], at=f_at + 4 * P)
        bin_ = place("bin_", [H, P], at=f_at + 4 * P * 5)
        cwin = place("cwin", [4, NCT * P], at=f_at + 4 * P * 6)
        flat = proj[:, :, :].rearrange("p t n -> p (t n)")
        smx = flat[:, 0:1536].rearrange("p (h k) -> p h k", h=H)
        qkT = flat[:, 6 * N:6 * N + 1024].rearrange("p (t n) -> p t n", t=4)
        ck = flat[:, 12 * N:12 * N + 2 * NCT * P].rearrange("p (a n) -> p a n", a=2)
        kqT = flat[:, 19 * N:19 * N + 1536].rearrange("p (k a n) -> p k a n", k=3, a=2)
        smp = place("smp", [B, PW])
        smp_o = place("smp_o", [B, D])
        ptr = place("ptr", [P, 3, 512])
        otok = place("otok", [P, NT, D])
        r_pre = ptr[:, 2, 0:N]
        sqt = ptr[:, 0:2, :].rearrange("p a n -> p (a n)")
        cv = place("cv", [96, 9, HD])
        kq16 = place("kq16", [P, 2, 16])
        v64 = place("v64", [P, HD])
        gb = place("gb", [P, 2])
        s13 = place("s13", [P, 4, NPAGE, H])
        pmax = place("pmax", [P, 2, 2, H])
        pmax_all = place("pmax_all", [P, 2, 2, H])
        oms = place("oms", [OROWS, B // 2, GW])
        v_own = scratch("v_own", 2 * (GW + 1), [B, 2, GW + 1])

        ps = ctx.enter_context(nc.psum_tensor("ps", [P, 8, 512], F32))

        def C(name, rows_=P):
            a, n = COL[name]
            return const[0:rows_, a:a + n]

        ident, ones = C("ident"), C("ones")

        def dram(name, shape):
            return nc.dram_tensor(name, shape, F32, kind="Internal").ap()

        d_logf = dram("d_logf", [B * NPG, P * H])
        d_q = dram("d_q", [B, 512])
        d_cnew = dram("d_cnew", [3, B, GW])
        d_cold = dram("d_cold", [3, 3, B, GW])
        d_cw = dram("d_cw", [4, 3, B, GW])
        d_cn = dram("d_cn", [3, B, GW])
        d_gate = dram("d_gate", [B, H, 2])
        d_oc = dram("d_oc", [B, GW])

        sems = {}

        def S(name):
            if name not in sems:
                sems[name] = ctx.enter_context(nc.semaphore(name))
            return sems[name]

        class Chain:

            def __init__(self, eng, name):
                self.eng, self.name, self.n = eng, name, 0

            def __call__(self, ins):
                ins.then_inc(S(self.name), 1)
                self.n += 1
                self.eng.wait_ge(S(self.name), self.n)

        def kt_view(ap, k):
            return ap.rearrange("p (k m) -> p k m", k=k)

        with nc.Block() as blk:
            @blk.sync
            def _(sp):
                sp.dma_start(const[:, :], io["const"]).then_inc(S("row_in"), 16)
                sp.dma_start(xin[:, 0:2, :], io["x_prompt"][0].rearrange("(t p) d -> p t d", p=P)).then_inc(S("par_in"), 16)
                sp.dma_start(xin[0:B, 2, :], io["x_sample"].rearrange("b t d -> (b t) d")).then_inc(S("par_in"), 16)
                sp.dma_start(ptab[:, :], io["page_table"].rearrange("(o b) g -> o (b g)", o=1)).then_inc(S("row_in"), 16)
                sp.wait_ge(S("row_in"), 32)

            @blk.tensor
            def _(pe):
                pe.wait_ge(S("row_in"), 32)
                pe.wait_ge(S("par_in"), 32)
                for t in range(KT):
                    for a in range(NT):
                        pe.transpose(ps[:, t, a * P:(a + 1) * P], xin[:, a, t * P:(t + 1) * P], ident)
                    pe.transpose(ps[:, t, L:N], xin[0:B, 2, t * P:(t + 1) * P], C("ident", B)[:, 0:B]).then_inc(S("par_turned"), 1)

            @blk.vector
            def _(dve):
                for t in range(KT):
                    dve.wait_ge(S("par_turned"), t + 1)
                    dve.tensor_copy(x[:, t, :], ps[:, t, 0:N]).then_inc(S("par_taken"), 1)

            @blk.gpsimd
            def _(pool):
                pool.memset(gate_in[:, :, :], 0.0).then_inc(S("slot_zero"), 1)
                pool.memset(param12[:, :], 0.0).then_inc(S("slot_zero"), 1)
                pool.memset(oms[:, :, :], 0.0).then_inc(S("slot_zero"), 1)
                pool.memset(cum[:, :], 0.0).then_inc(S("slot_zero"), 1)

        nc.all_engine_barrier()
        for s in sems.values():
            nc.gpsimd.sem_clear(s)
        nc.all_engine_barrier()

        with nc.Fori(0, DEPTH) as l:
            with nc.Block() as blk:

                @blk.sync
                def _(sp):
                    def load(name, s, pair, dst, src):
                        if not (isinstance(pair, int) and pair == 0):
                            sp.wait_ge(S(f"w_lo{s}"), 2 * pair)
                        sp.dma_start(dst, src).then_inc(S(f"w_raw{s}"), 16)

                    def wide(s, pair, w, j):
                        load("", s, pair, kt_view(raw[s][:, :], 8),
                             w.rearrange("(k p) m -> p k m", p=P)[:, :, bass.ds(j * 256, 256)])

                    def gu(k, j):
                        base = P0[f"gu{k}"]
                        wide(0, base + j, io[f"ffn{k}_gate"][l], j)
                        wide(1, base + j, io[f"ffn{k}_up"][l], j)

                    def dn(k, j):
                        base = P0[f"dn{k}"]
                        v = io[f"ffn{k}_down"][l].rearrange("(k p) m -> p k m", p=P)
                        for s in range(2):
                            load("", s, base + j, kt_view(raw[s][:, 0:1408], 11), v[:, 11 * s:11 * s + 11, bass.ds(j * P, P)])

                    g48 = io["norm_g"][l].rearrange("i (t p) -> (i t) p", p=P)
                    sp.dma_start(gin[0:48, :], g48).then_inc(S("gain_in"), 16)
                    gu(1, 0)
                    sp.dma_start(win[:, :, :], io["gmlp_ws"][l].rearrange("g t s -> t g s")).then_inc(S("par_in"), 16)
                    sp.dma_start(bin_[:, :], io["gmlp_bs"][l]).then_inc(S("par_in"), 16)
                    sp.wait_ge(S("cw_zero"), 1)
                    sp.dma_start(cwin[:, COFF:COFF + 768], io["gdn_conv_w"][l]).then_inc(S("par_in"), 16)
                    bc = lambda ap, n, parts=P: ap.rearrange("(o n) -> o n", o=1).broadcast_to([parts, n])
                    for dst, src, n in ((param12[:, 0:4], io["fox_bias"], 4), (param12[:, 4:8], io["gdn_dt_bias"], 4),
                                        (a_log[:, :], io["gdn_a_log"], 4), (gv[:, :], io["gmlp_norm_g"], GW)):
                        sp.dma_start(dst, bc(src[l], n)).then_inc(S("row_in"), 16)
                    sp.dma_start(og[:, :], bc(io["out_norm_g"][l].rearrange("m h d -> (m h d)"), D)).then_inc(S("row_in"), 16)
                    with nc.allow_non_contiguous_dma(reason="eight values"):
                        sp.dma_start(ws0[:, 0, :], io["gmlp_ws"][l][:, 0, 0:1].rearrange("g o -> o g").broadcast_to([B, H])).then_inc(S("row_in"), 16)
                        sp.dma_start(ws0[:, 1, :], io["gmlp_bs"][l][:, 0:1].rearrange("g o -> o g").broadcast_to([B, H])).then_inc(S("row_in"), 16)
                    for j in range(4):
                        sp.dma_start(d_cw[j], io["gdn_conv_w"][l, j:j + 1].rearrange("o (c f) -> c o f", c=3).broadcast_to([3, B, GW])).then_inc(S("conv_pre"), 16)
                    for j in range(3):
                        sp.dma_start(d_cold[j], io["state_gdn_conv"][:, l, j].rearrange("b (c f) -> c b f", c=3)).then_inc(S("conv_pre"), 16)
                    sp.wait_ge(S("conv_pre"), 7 * 16)
                    sp.dma_start(cv[:, 0:4, :], d_cw.rearrange("j c b (h e) -> (c b h) j e", h=H)).then_inc(S("conv_in"), 16)
                    sp.dma_start(cv[:, 4:7, :], d_cold.rearrange("j c b (h e) -> (c b h) j e", h=H)).then_inc(S("conv_in"), 16)

                    def pages(first, n):
                        for k in range(n):
                            page = sp.value_load(ptab[0:1, bass.ds(first + k, 1)], min_val=0, max_val=io["n_pool"] - 1)
                            sp.dma_start(d_logf[bass.ds(first + k, 1)], io["cache_fox_logf"][bass.ds(page, 1), l].rearrange("o p h -> o (p h)")).then_inc(S("logf_pre"), 16)

                    with sp.Fori(1, GU_P) as j:
                        gu(1, j)
                        pages((j - 1) * 4, 4)
                    with sp.Fori(0, DN_P) as j:
                        dn(1, j)
                        pages(j * 3 + 4 * (GU_P - 1), 3)
                    with sp.Fori(0, WI_P - 1) as j:
                        for s in range(2):
                            load("", s, P0["wi"] + j, kt_view(raw[s][:, :], 8),
                                 io["w_in"][l].rearrange("(k p) m -> p k m", p=P)[:, :, bass.ds(j * 512 + s * 256, 256)])
                    for s in range(2):
                        load("", s, P0["wi"] + WI_P - 1, kt_view(raw[s][:, 0:512], 4),
                             io["w_in"][l].rearrange("(k p) m -> p k m", p=P)[:, 4 * s:4 * s + 4, PW - P:PW])
                    sp.wait_ge(S("logf_pre"), 16 * B * NPG)
                    sp.wait_ge(S("n_ready"), 16)
                    sp.dma_start(otok[0:B * NPG, 0, 0:512], d_logf).then_inc(S("logf_in"), 16)

                    page_of = {}

                    def read_pages(b):
                        for g in range(NPG):
                            page_of[b, g] = sp.value_load(ptab[0:1, bass.ds(b * NPG + g, 1)], min_val=0, max_val=io["n_pool"] - 1)

                    def window(dst, i, b, src, sem):
                        a = io[src][b, l].rearrange("r h d -> r (h d)")
                        sp.dma_start(dst[:, i, NPG, 0:GW], a[PAST - P:PAST, :]).then_inc(sem, 16)
                        sp.dma_start(dst[:, i, NPG + 1, 0:GW], a[PAST - 4 * P:PAST, :].rearrange("(r f) d -> r f d", f=4)[:, 0, :]).then_inc(sem, 16)
                        sp.dma_start(dst[0:PAST // 16, i, NPG + 2, 0:GW], a[0:PAST, :].rearrange("(r f) d -> r f d", f=16)[:, 0, :]).then_inc(sem, 16)

                    def keys(b):
                        i, use = b % 2, b // 2
                        read_pages(b)
                        if use:
                            sp.wait_ge(S(f"k_used{i}"), use)
                            queries(b)
                        for g in range(NPG):
                            sp.dma_start(kslot[:, i, g, :], io["cache_fox_k"][bass.ds(page_of[b, g], 1), l].rearrange("o p h d -> p (o h d)")).then_inc(S(f"k_in{i}"), 16)
                        window(kslot, i, b, "state_swa_k", S(f"k_in{i}"))

                    def vals(b):
                        i, use = b % 2, b // 2
                        if use:
                            sp.wait_ge(S("pv_mm"), use)
                        for g in range(NPG):
                            sp.dma_start(vslot[:, i, g, 0:GW], io["cache_fox_v"][bass.ds(page_of[b, g], 1), l].rearrange("o p h d -> p (o h d)")).then_inc(S(f"v_in{i}"), 16)
                        window(vslot, i, b, "state_swa_v", S(f"v_in{i}"))

                    def queries(b):
                        sp.dma_start(q_bc[:, b % 2, :], d_q[b:b + 1].broadcast_to([P, 512])).then_inc(S(f"q_in{b % 2}"), 16)

                    for s in range(2):
                        sp.wait_ge(S(f"mm_done{s}"), M0["wo"])
                    sp.wait_ge(S("slot_zero"), 4)
                    for b in range(2):
                        keys(b)
                        vals(b)
                    o = io["outs"]
                    st = S("stored")
                    pr = lambda ap: ap.rearrange("(t p) h d -> p t (h d)", p=P)
                    sm = lambda ap: ap.rearrange("b t h d -> b (t h d)")
                    sp.wait_ge(S("tok_act"), 14)
                    sp.wait_ge(S("tok_dve"), 7)
                    for c in range(3):
                        sp.dma_start(d_cnew[c], smp[:, QC + c * GW:QC + (c + 1) * GW]).then_inc(S("regroup"), 16)
                    sp.wait_ge(S("rope"), 2)
                    sp.dma_start(d_q[:, 0:GW], smp[:, QA:QA + GW]).then_inc(S("q_pre"), 16)
                    sp.dma_start(d_q[:, GW:512], smp[:, QB_:QB_ + GW]).then_inc(S("q_pre"), 16)
                    sp.wait_ge(S("regroup"), 48)
                    sp.dma_start(cv[:, 7, :], d_cnew.rearrange("c b (h e) -> (c b h) e", h=H)).then_inc(S("conv_in"), 16)
                    sp.wait_ge(S("q_pre"), 32)
                    for b in range(2):
                        queries(b)
                    sp.dma_start(o["gdn_conv_prompt"][0, l], tok[P - 3:P, 1, QC:QC + 768]).then_inc(st, 16)
                    sp.dma_start(o["gdn_conv_sample"][:, l, 2], smp[:, QC:QC + 768]).then_inc(st, 16)
                    sp.dma_start(o["gdn_conv_sample"][:, l, 0:2], io["state_gdn_conv"][:, l, 1:3]).then_inc(st, 16)
                    sp.wait_ge(S("gates"), 1)
                    sp.dma_start(o["fox_logf_prompt"][0, l].rearrange("(t p) h -> p t h", p=P), gate[:, 0:2, 0:4]).then_inc(st, 16)
                    sp.dma_start(o["fox_logf_sample"][:, l].rearrange("b t h -> b (t h)"), gate[0:B, 2, 0:4]).then_inc(st, 16)
                    with nc.allow_non_contiguous_dma(reason="gates of eight samples"):
                        for k in range(2):
                            sp.dma_start(d_gate[:, :, k:k + 1], gate[0:B, 2, 4 + 4 * k:8 + 4 * k].unsqueeze(2)).then_inc(S("gb_pre"), 16)
                    for b in (2, 3):
                        keys(b)
                    sp.wait_ge(S("gb_pre"), 32)
                    for c in range(4):
                        sp.dma_start(gb[c:P:4, :], d_gate.rearrange("b h k -> (b h) k")).then_inc(S("state_in"), 16)
                    sp.dma_start(pr(o["fox_k_prompt"][0, l]), tok[:, :, KB_:KB_ + GW]).then_inc(st, 16)
                    sp.dma_start(pr(o["fox_v_prompt"][0, l]), tok[:, :, VB_:VB_ + GW]).then_inc(st, 16)
                    sp.dma_start(pr(o["swa_v_prompt"][0, l]), tok[:, :, VA:VA + GW]).then_inc(st, 16)
                    sp.dma_start(sm(o["fox_k_sample"][:, l]), smp[:, KB_:KB_ + GW]).then_inc(st, 16)
                    sp.dma_start(sm(o["fox_v_sample"][:, l]), smp[:, VB_:VB_ + GW]).then_inc(st, 16)
                    sp.dma_start(sm(o["swa_v_sample"][:, l]), smp[:, VA:VA + GW]).then_inc(st, 16)
                    sp.dma_start(pr(o["swa_k_prompt"][0, l]), tok[:, :, KA:KA + GW]).then_inc(st, 16)
                    sp.dma_start(sm(o["swa_k_sample"][:, l]), smp[:, KA:KA + GW]).then_inc(st, 16)
                    sp.wait_ge(S("s_conv"), 1)
                    sp.dma_start(d_cn.rearrange("c b (h e) -> (c b h) e", h=H), cv[:, 8, :]).then_inc(S("regroup"), 16)
                    for b in (2, 3):
                        vals(b)
                    sp.wait_ge(S("regroup"), 64)
                    for k in range(2):
                        sp.dma_start(kq16[:, k, :], d_cn[k].rearrange("b (g e) -> (b g) e", e=16)).then_inc(S("state_in"), 16)
                    for c in range(4):
                        sp.dma_start(v64[c:P:4, :], d_cn[2].rearrange("b (h e) -> (b h) e", e=HD)).then_inc(S("state_in"), 16)
                    for b in (4, 5):
                        keys(b)
                    sp.wait_ge(S("qkt"), 2)
                    for b in range(B):
                        sp.dma_start(state[16 * b:16 * b + 16, :, :].rearrange("p k v -> p (k v)"),
                                     io["state_gdn_s"][b, l].rearrange("h (c k) v -> (h c) (k v)", c=4)).then_inc(S("state_in"), 16)
                    for b in (4, 5):
                        vals(b)
                    for b in (6, 7):
                        keys(b)
                    sp.wait_ge(S("gmlp_v"), 1)
                    sp.dma_start(o["gmlp_v_sample"][:, l].rearrange("b t d -> b (t d)"), smp[:, VD:VD + GW]).then_inc(st, 16)
                    for b in (6, 7):
                        vals(b)
                    sp.wait_ge(S("p_state"), 4)
                    for h in range(H):
                        sp.dma_start(o["gdn_s_prompt"][0, l, h], st_s[64 * (h % 2):64 * (h % 2) + 64, h // 2, :]).then_inc(st, 16)
                    sp.wait_ge(S("s_out"), 1)
                    sp.dma_start(d_oc.rearrange("b (h e) -> (b h) e", e=HD), v64[0:P:4, :]).then_inc(S("regroup"), 16)
                    sp.wait_ge(S("s_state"), 1)
                    for b in range(B):
                        sp.dma_start(o["gdn_s_sample"][b, l].rearrange("h (c k) v -> (h c) (k v)", c=4),
                                     state[16 * b:16 * b + 16, :, :].rearrange("p k v -> p (k v)")).then_inc(S("s_state_out"), 16)
                    sp.wait_ge(S("regroup"), 80)
                    sp.dma_start(smp_o[:, 512:768], d_oc).then_inc(S("oc_in"), 16)
                    sp.wait_ge(S("s_state_out"), 16 * B)
                    sp.wait_ge(S("mixed"), 1)
                    sp.wait_ge(st, 16 * 18)
                    for j in range(WO_P):
                        for s in range(2):
                            load("", s, P0["wo"] + j, kt_view(raw[s][:, :], 8),
                                 io["w_out"][l].rearrange("(k p) m -> p k m", p=P)[:, :, j * 512 + s * 256:j * 512 + s * 256 + 256])
                    with sp.Fori(0, GU_P) as j:
                        gu(2, j)
                    with sp.Fori(0, DN_P) as j:
                        dn(2, j)

                @blk.scalar
                def _(act):
                    ch = Chain(act, "act_ch")
                    last = lambda n: {"wi": "wi_last"}.get(n, n)

                    def hi(n, j, s, special=None):
                        pair = P0[n] + j
                        act.wait_ge(S(f"w_raw{s}"), 16 * (pair + 1))
                        done = M0[n] + INC[n] * j
                        if not (isinstance(done, int) and done == 0):
                            act.wait_ge(S(f"mm_done{s}"), done)
                        for a, b in HALVES[special or n]:
                            act.activation(whi[s][:, a:b], raw[s][:, a:b], ACT.Copy).then_inc(S(f"w_hi{s}"), 1)

                    def gu_step(k, j, nxt):
                        n = f"gu{k}"
                        for f in range(2):
                            act.wait_ge(S("gate_taken"), 22 * (k - 1) + 2 * j + f + 3)
                            act.activation(s_t[:, f, :], s_t[:, f, :], ACT.Silu).then_inc(S("silu"), 1)
                        hi(*nxt, 0)
                        for f in range(2):
                            act.wait_ge(S("h_full"), 22 * (k - 1) + 2 * j + f + 1)
                            act.activation(hhi[:, bass.ds(2 * j + f, 1), :].rearrange("p o n -> p (o n)"),
                                           h_t[:, f, :], ACT.Copy).then_inc(S("h_hi"), 1)
                        hi(*nxt, 1)

                    def evac_y(n, e, t, bank, s, i):
                        act.activation(yt[:, bass.ds(t, 1), :].rearrange("p o n -> p (o n)"), ps[:, bank, 0:N], ACT.Copy).then_inc(S("y_copied"), 1)
                        act.activation(sq8[:, bass.ds(t, 1), :].rearrange("p o n -> p (o n)"), ps[:, bank, 0:N], ACT.Square).then_inc(S("sq"), 1)

                    def dn_pair(k, q, nxt):
                        n, e = f"dn{k}", {1: 1, 2: 5}[k]
                        for m in range(2):
                            j = 2 * q + m
                            if nxt[m]:
                                hi(*nxt[m], 0)
                            act.wait_ge(S("mm_done1"), M0[n] + j + 1)
                            evac_y(n, e, j, 4 + m, 1, 0)
                            if nxt[m]:
                                hi(*nxt[m], 1)

                    def rms_of(e):
                        act.wait_ge(S("ss"), e + 1)
                        act.activation(r_post[:, :] if e % 2 else r_pre, ps[:, 7, 0:N], ACT.Sqrt, bias=C("eps")).then_inc(S("rms"), 1)

                    def pre(e):
                        for t in range(KT):
                            act.wait_ge(S("x_new"), 8 * (e // 2) + t + 1)
                            act.activation(nhi[:, t, :], x[:, t, :], ACT.Copy, scale=gains[:, 8 * e + t:8 * e + t + 1]).then_inc(S("n_hi"), 1)
                            act.activation(sq8[:, t, :], x[:, t, :], ACT.Square).then_inc(S("sq"), 1)

                    act.sem_inc(S("gate_taken"), 2)
                    act.wait_ge(S("par_taken"), 1)
                    pre(0)
                    hi("gu1", 0, 0)
                    hi("gu1", 0, 1)
                    rms_of(0)
                    act.wait_ge(S("row_in"), 7 * 16)
                    act.activation(mul12[:, 4:8], a_log[:, :], ACT.Exp).then_inc(S("a_exp"), 1)
                    with act.Fori(0, GU_P - 1) as j:
                        gu_step(1, j, ("gu1", j + 1))
                    gu_step(1, GU_P - 1, ("dn1", 0))
                    with act.Fori(0, DN_P // 2 - 1) as q:
                        dn_pair(1, q, [("dn1", 2 * q + 1), ("dn1", 2 * q + 2)])
                    dn_pair(1, DN_P // 2 - 1, [("dn1", DN_P - 1), ("wi", 0)])
                    rms_of(1)
                    pre(2)
                    rms_of(2)

                    def wi_step(j, nxt):
                        hi("wi", j + 1, 0, special=nxt)
                        hi("wi", j + 1, 1, special=nxt)

                    with act.Fori(0, WI_P - 2) as j:
                        wi_step(j, None)
                    wi_step(WI_P - 2, "wi_last")

                    for g in range(7):
                        w = 512 if g < 6 else 12
                        c0 = 0 if g < 6 else P - 12
                        bk = 3 * (g % 2)
                        act.wait_ge(S("turned"), 3 * g + 1)
                        act.activation(tok[:, 0, 512 * g:512 * g + w], ps[:, bk, c0:c0 + w], ACT.Copy).then_inc(S("tok_act"), 1)
                        act.wait_ge(S("turned"), 3 * g + 3)
                        act.activation(smp[:, 512 * g:512 * g + w], ps[0:B, bk + 2, c0:c0 + w], ACT.Copy).then_inc(S("tok_act"), 1)
                    act.wait_ge(S("gate_z"), 1)
                    ch(act.activation(gate_t[:, :, :], gate_in[:, :, :], ACT.Abs))
                    ch(act.activation(gate_t[:, :, :], gate_t[:, :, :], ACT.Exp, scale=-1.0))
                    act.activation(gate_t[:, :, :], gate_t[:, :, :], ACT.Ln, bias=1.0).then_inc(S("gate_ln"), 1)
                    act.wait_ge(S("gate_sp"), 1)
                    act.activation(gate[:, :, 8:12], gate[:, :, 8:12], ACT.Exp).then_inc(S("gates"), 1)
                    act.wait_ge(S("cum_sb"), 2)
                    ch(act.activation(eg[:, 0:2, :], eg[:, 0:2, :], ACT.Exp))
                    act.activation(eg[:, 2, :], eg[:, 2, :], ACT.Exp).then_inc(S("eg"), 1)
                    act.wait_ge(S("dt_masked"), 1)
                    act.activation(dt_[:, :, :], dt_[:, :, :], ACT.Exp).then_inc(S("dt"), 1)
                    act.wait_ge(S("tok_dve"), 7)
                    act.activation(tok[:, :, ZC:ZC + GW], tok[:, :, ZC:ZC + GW], ACT.Silu).then_inc(S("silu_z"), 1)
                    act.activation(smp[:, ZC:ZC + GW], smp[:, ZC:ZC + GW], ACT.Silu).then_inc(S("silu_z"), 1)
                    for t in range(NCT):
                        act.wait_ge(S("conv"), t + 1)
                        act.activation(conv_t[:, t, :], conv_t[:, t, :], ACT.Silu).then_inc(S("conv_silu"), 1)
                    act.wait_ge(S("s_conv_raw"), 1)
                    act.activation(cv[:, 8, :], cv[:, 7, :], ACT.Silu).then_inc(S("s_silu"), 1)
                    act.activation(tok[:, :, UD:UD + 512], tok[:, :, UD:UD + 512], ACT.Gelu_apprx_tanh).then_inc(S("gelu"), 1)
                    act.activation(smp[:, UD:UD + 512], smp[:, UD:UD + 512], ACT.Gelu_apprx_tanh).then_inc(S("gelu"), 1)
                    act.wait_ge(S("ck_turned"), 1)
                    act.activation(ck[:, 0, 0:512], ps[:, 6, :], ACT.Copy).then_inc(S("ck_act"), 1)
                    act.activation(ck[:, 0, 512:896], ps[:, 7, 0:384], ACT.Copy).then_inc(S("ck_act"), 1)
                    def softmax(m):
                        act.wait_ge(S("row_max"), m + 1)
                        for h in range(H):
                            for t in range(NT):
                                sl = smx[:, h, 0:P] if t == 0 else smx[:, h, P:3 * P]
                                act.activation(sl, sl, ACT.Exp, bias=small[:, 32 + 4 * t + h:33 + 4 * t + h],
                                               accum_out=small[:, 40 + 4 * t + h:41 + 4 * t + h]).then_inc(S("p_exp"), 1)
                        for i, k in enumerate((0, 2)):
                            act.wait_ge(S("p_turned"), 3 * m + k + 1)
                            act.activation(ptr[:, k, :], ps[:, k, :], ACT.Copy).then_inc(S("ptr_act"), 1)

                    def sample_exp(j):
                        act.wait_ge(S("s13"), j + 1)
                        u = 2 * (j % 2)
                        act.activation(s13[:, u:u + 2, :, :], s13[:, u:u + 2, :, :], ACT.Exp).then_inc(S("s_exp"), 1)

                    softmax(0)
                    act.wait_ge(S("mix_ss"), 1)
                    ch(act.activation(small[0:64, 0:1], small[0:64, 0:1], ACT.Ln, bias=C("eps", 64)))
                    act.activation(small[0:64, 0:1], small[0:64, 0:1], ACT.Exp, scale=-0.5).then_inc(S("mix_r"), 1)
                    act.wait_ge(S("qk_turned"), 1)
                    act.activation(qkT[:, :, 0:P], ps[:, 4, :].rearrange("p (t n) -> p t n", t=4), ACT.Copy).then_inc(S("qk_act"), 1)
                    softmax(1)
                    sample_exp(0)
                    act.wait_ge(S("mix_ss"), 2)
                    ch(act.activation(small[:, 8:24], small[:, 8:24], ACT.Ln, bias=C("eps")))
                    act.activation(small[:, 8:24], small[:, 8:24], ACT.Exp, scale=-0.5).then_inc(S("mix_r"), 1)
                    act.wait_ge(S("mix_ss"), 3)
                    ch(act.activation(small[:, 24:27], small[:, 24:27], ACT.Ln, bias=C("eps"), scale=1.0 / GW))
                    act.activation(small[:, 24:27], small[:, 24:27], ACT.Exp, scale=-0.5).then_inc(S("mix_r"), 1)

                    act.wait_ge(S("kq_turned"), 1)
                    act.activation(kqT[:, 0:2, :, 0:P], ps[:, 4, :].rearrange("p (k a n) -> p k a n", k=2, a=2), ACT.Copy).then_inc(S("kq_act"), 1)
                    act.activation(kqT[:, 2, :, 0:P], ps[:, 5, 0:256].rearrange("p (a n) -> p a n", a=2), ACT.Copy).then_inc(S("kq_act"), 1)
                    act.wait_ge(S("tt_turned"), 2)
                    for t in range(NT):
                        act.activation(tm[:, t, :], ps[:, 4 + t, :], ACT.Copy).then_inc(S("tm_act"), 1)
                    sample_exp(1)
                    sample_exp(2)
                    act.wait_ge(S("state_in"), 16 * (B + 4 + 2 + 4))
                    act.activation(small[:, 120:121], gb[:, 0:1], ACT.Exp).then_inc(S("sg"), 1)
                    sample_exp(3)

                    act.wait_ge(S("mix_ss"), 4)
                    ch(act.activation(small[:, 64:96], small[:, 64:96], ACT.Ln, bias=C("eps"), scale=1.0 / HD))
                    act.activation(small[:, 64:96], small[:, 64:96], ACT.Exp, scale=-0.5).then_inc(S("mix_r"), 1)
                    act.wait_ge(S("mix_ss"), 5)
                    ch(act.activation(small[0:B, 96:112], small[0:B, 96:112], ACT.Ln, bias=C("eps", B), scale=1.0 / HD))
                    act.activation(small[0:B, 96:112], small[0:B, 96:112], ACT.Exp, scale=-0.5).then_inc(S("mix_r"), 1)
                    for t in range(KT):
                        act.wait_ge(S("o_turned"), t + 1)
                        act.activation(nhi[:, t, :], ps[:, t, 0:N], ACT.Copy).then_inc(S("o_hi"), 1)

                    hi("wo", 0, 0)
                    hi("wo", 0, 1)
                    for j in range(WO_P):
                        nxt = ("wo", 1) if j == 0 else ("gu2", 0)
                        for s in range(2):
                            for i in range(2):
                                act.wait_ge(S(f"mm_done{s}"), M0["wo"] + 2 * j + i + 1)
                                evac_y("wo", 3, 4 * j + 2 * s + i, 2 * s + i, s, i)
                            hi(*nxt, s)
                    rms_of(3)
                    pre(4)
                    rms_of(4)
                    with act.Fori(0, GU_P - 1) as j:
                        gu_step(2, j, ("gu2", j + 1))
                    gu_step(2, GU_P - 1, ("dn2", 0))
                    with act.Fori(0, DN_P // 2 - 1) as q:
                        dn_pair(2, q, [("dn2", 2 * q + 1), ("dn2", 2 * q + 2)])
                    dn_pair(2, DN_P // 2 - 1, [("dn2", DN_P - 1), None])
                    rms_of(5)

                @blk.gpsimd
                def _(pool):
                    ch = Chain(pool, "pool_ch")
                    tt_ = pool.tensor_tensor

                    def sumsq(e):
                        pool.wait_ge(S("sq"), 8 * e + 2)
                        ch(tt_(ss_acc[:, :], sq8[:, 0, :], sq8[:, 1, :], ALU.add))
                        for t in range(2, KT):
                            pool.wait_ge(S("sq"), 8 * e + t + 1)
                            ins = tt_(ss_acc[:, :], ss_acc[:, :], sq8[:, t, :], ALU.add)
                            if t < KT - 1:
                                ch(ins)
                            else:
                                ins.then_inc(S("ss_acc"), 1)

                    ch(pool.memset(cwin[:, :], 0.0))
                    pool.sem_inc(S("cw_zero"), 1)
                    for e in range(3):
                        sumsq(e)
                    for s in range(2):
                        pool.wait_ge(S(f"mm_done{s}"), M0["wo"])
                    for i in range(2):
                        if i:
                            pool.wait_ge(S("slot_ones"), i)
                        pool.memset(kslot[64:P, i, NPG + 2, :], 0.0).then_inc(S("slot_zero"), 1)
                        pool.wait_ge(S("slot_zero"), 2 * i + 1)
                        pool.memset(vslot[64:P, i, NPG + 2, :], 0.0).then_inc(S("slot_zero"), 1)
                        pool.wait_ge(S("slot_zero"), 2 * i + 2)
                        pool.memset(vslot[:, i, :, GW:GW + 1], 1.0).then_inc(S("slot_ones"), 1)
                    pool.wait_ge(S("conv_in"), 48)
                    acc = cv[:, 7, :]
                    ch(tt_(acc, acc, cv[:, 3, :], ALU.mult))
                    for j in range(3):
                        ch(tt_(cv[:, 4 + j, :], cv[:, 4 + j, :], cv[:, j, :], ALU.mult))
                    ch(tt_(cv[:, 4, :], cv[:, 4, :], cv[:, 5, :], ALU.add))
                    ch(tt_(cv[:, 4, :], cv[:, 4, :], cv[:, 6, :], ALU.add))
                    tt_(acc, acc, cv[:, 4, :], ALU.add).then_inc(S("s_conv_raw"), 1)
                    for b in range(B):
                        i, use = b % 2, b // 2
                        pool.wait_ge(S(f"k_in{i}"), 16 * NKT * (use + 1))
                        pool.wait_ge(S(f"q_in{i}"), 16 * (use + 1))
                        if b:
                            pool.wait_ge(S("s_red"), 2 * b)
                        tt_(prod[:, 0:NPG, :], kslot[:, i, 0:NPG, :], q_bc[:, i, GW:512].unsqueeze(1).broadcast_to([P, NPG, GW]), ALU.mult).then_inc(S("prod"), 1)
                        tt_(prod[:, NPG:NKT, :], kslot[:, i, NPG:NKT, :], q_bc[:, i, 0:GW].unsqueeze(1).broadcast_to([P, CACHE_T, GW]), ALU.mult).then_inc(S(f"k_used{i}"), 1)
                        if i == 1:
                            pool.wait_ge(S("s_max"), use + 1)
                            pool.partition_all_reduce(pmax_all[:, :, :, :].rearrange("p a m h -> p (a m h)"),
                                                      pmax[:, :, :, :].rearrange("p a m h -> p (a m h)"), P, RMAX).then_inc(S("s_max_all"), 1)
                    for e in range(3, 6):
                        sumsq(e)

                @blk.vector
                def _(dve):
                    ch = Chain(dve, "dve_ch")
                    tt2, ts, stt, red = dve.tensor_tensor, dve.tensor_scalar, dve.scalar_tensor_tensor, dve.tensor_reduce

                    def lo(n, j, s, special=None):
                        for i, (a, b) in enumerate(HALVES[special or n]):
                            dve.wait_ge(S(f"w_hi{s}"), 2 * (P0[n] + j) + i + 1)
                            tt2(wlo[s][:, a:b], raw[s][:, a:b], whi[s][:, a:b].bitcast(F32), ALU.subtract).then_inc(S(f"w_lo{s}"), 1)

                    def gu_step(k, j, nxt):
                        n = f"gu{k}"
                        for f in range(2):
                            dve.wait_ge(S("mm_done0"), M0[n] + 2 * j + f + 1)
                            tt2(s_t[:, f, :], ps[:, f, 0:N], r_pre, ALU.mult).then_inc(S("gate_taken"), 1)
                        lo(*nxt, 0)
                        for f in range(2):
                            dve.wait_ge(S("mm_done1"), M0[n] + 2 * j + f + 1)
                            tt2(h_t[:, f, :], ps[:, 2 + f, 0:N], r_pre, ALU.mult).then_inc(S("up_taken"), 1)
                            dve.wait_ge(S("silu"), 22 * (k - 1) + 2 * j + f + 1)
                            dve.wait_ge(S("up_taken"), 22 * (k - 1) + 2 * j + f + 3)
                            tt2(h_t[:, f, :], s_t[:, f, :], h_t[:, f, :], ALU.mult).then_inc(S("h_full"), 1)
                            dve.wait_ge(S("h_hi"), 22 * (k - 1) + 2 * j + f + 1)
                            at = bass.ds(2 * j + f, 1)
                            tt2(hlo[:, at, :].rearrange("p o n -> p (o n)"), h_t[:, f, :],
                                hhi[:, at, :].rearrange("p o n -> p (o n)").bitcast(F32), ALU.subtract).then_inc(S("h_ready"), 1)
                        lo(*nxt, 1)

                    def rsqrt_of(e):
                        r = r_post[:, :] if e % 2 else r_pre
                        dve.wait_ge(S("rms"), e + 1)
                        dve.reciprocal(r, r).then_inc(S("r"), 1)
                        dve.wait_ge(S("r"), e + 1)

                    def post(e):
                        rsqrt_of(e)
                        dve.wait_ge(S("y_copied"), 8 * (e // 2 + 1))
                        for t in range(KT):
                            ch(stt(yt[:, t, :], yt[:, t, :], gains[:, 8 * e + t:8 * e + t + 1], r_post[:, :], ALU.mult, ALU.mult))
                            tt2(x[:, t, :], x[:, t, :], yt[:, t, :], ALU.add).then_inc(S("x_new"), 1)
                            if e < 5 and t:
                                lo_n(e + 1, t - 1)
                        if e < 5:
                            lo_n(e + 1, KT - 1)

                    def lo_n(e, t):
                        dve.wait_ge(S("n_hi"), 8 * (e // 2) + t + 1)
                        if e:
                            dve.wait_ge(S("x_new"), 8 * (e // 2) + t + 1)
                        stt(nlo[:, t, :], x[:, t, :], gains[:, 8 * e + t:8 * e + t + 1], nhi[:, t, :].bitcast(F32), ALU.mult, ALU.subtract).then_inc(S("n_ready"), 1)

                    dve.sem_inc(S("up_taken"), 2)
                    dve.sem_inc(S("pd_taken"), 2)
                    dve.sem_inc(S("pa_taken"), 2)
                    dve.sem_inc(S("x_new"), 8)
                    dve.wait_ge(S("par_turned"), 1)
                    dve.tensor_copy(gains[:, :], ps[:, 4, 0:48]).then_inc(S("par_taken"), 1)
                    dve.wait_ge(S("par_taken"), 1)
                    for t in range(KT):
                        lo_n(0, t)
                    lo("gu1", 0, 0)
                    lo("gu1", 0, 1)
                    for e in (1, 5):
                        ch(ts(gains[:, 8 * e:8 * e + 8], gains[:, 8 * e:8 * e + 8], 0.5, None, ALU.mult))
                    dve.wait_ge(S("par_turned"), 3)
                    tt2(wst[:, :, :], ps[:, 5, :].rearrange("p (g t) -> p g t", g=H), C("upto").unsqueeze(1).broadcast_to([P, H, P]), ALU.mult).then_inc(S("par_taken"), 1)
                    dve.tensor_copy(bst[:, :], ps[:, 6, 0:H]).then_inc(S("par_taken"), 1)
                    dve.tensor_copy(cwt[:, :, :], ps[:, 4, 64:92].rearrange("p (t j) -> p t j", j=4)).then_inc(S("par_taken"), 1)
                    dve.wait_ge(S("a_exp"), 1)
                    ch(ts(mul12[:, 4:8], mul12[:, 4:8], -1.0, None, ALU.mult))
                    ch(dve.memset(mul12[:, 0:4], -1.0))
                    ch(dve.memset(mul12[:, 8:12], -1.0))
                    rsqrt_of(0)
                    with dve.Fori(0, GU_P - 1) as j:
                        gu_step(1, j, ("gu1", j + 1))
                    gu_step(1, GU_P - 1, ("dn1", 0))
                    with dve.Fori(1, DN_P) as j:
                        lo("dn1", j, 0)
                        lo("dn1", j, 1)
                    lo("wi", 0, 0)
                    lo("wi", 0, 1)
                    post(1)
                    rsqrt_of(2)

                    def wi_step(j, nxt):
                        for i in range(2):
                            dve.wait_ge(S("mm_done0"), M0["wi"] + 2 * j + i + 1)
                            tt2(proj[:, bass.ds(4 * j + i, 1), :].rearrange("p o n -> p (o n)"), ps[:, i, 0:N], r_pre, ALU.mult).then_inc(S("pa_taken"), 1)
                        lo("wi", j + 1, 0, special=nxt)
                        for i in range(2):
                            dve.wait_ge(S("mm_done1"), M0["wi"] + 2 * j + i + 1)
                            tt2(proj[:, bass.ds(4 * j + 2 + i, 1), :].rearrange("p o n -> p (o n)"), ps[:, 2 + i, 0:N], r_pre, ALU.mult).then_inc(S("pd_taken"), 1)
                        lo("wi", j + 1, 1, special=nxt)

                    with dve.Fori(0, WI_P - 2) as j:
                        wi_step(j, None)
                    wi_step(WI_P - 2, "wi_last")
                    dve.wait_ge(S("mm_done1"), M0["wi"] + TOTAL["wi"])
                    tt2(proj[:, NPT - 1, :], ps[:, 0, 0:N], r_pre, ALU.mult).then_inc(S("pa_taken"), 1)

                    for g in range(7):
                        w = 512 if g < 6 else 12
                        c0 = 0 if g < 6 else P - 12
                        dve.wait_ge(S("turned"), 3 * g + 2)
                        dve.tensor_copy(tok[:, 1, 512 * g:512 * g + w], ps[:, 3 * (g % 2) + 1, c0:c0 + w]).then_inc(S("tok_dve"), 1)
                    dve.wait_ge(S("tok_dve"), 7)
                    dve.wait_ge(S("tok_act"), 14)
                    dve.wait_ge(S("row_in"), 7 * 16)
                    dve.tensor_copy(gate_in[:, 0:2, 0:4], tok[:, :, FB:FB + 4])
                    dve.tensor_copy(gate_in[:, 0:2, 4:12], tok[:, :, AC:AC + 8])
                    dve.tensor_copy(gate_in[0:B, 2, 0:4], smp[:, FB:FB + 4])
                    ch(dve.tensor_copy(gate_in[0:B, 2, 4:12], smp[:, AC:AC + 8]))
                    ch(tt2(gate_in[:, :, :], gate_in[:, :, :], param12[:, :].unsqueeze(1).broadcast_to([P, 3, 12]), ALU.add))
                    tt2(gate_in[:, :, :], gate_in[:, :, :], C("sign").unsqueeze(1).broadcast_to([P, 3, 12]), ALU.mult).then_inc(S("gate_z"), 1)
                    def rope(src, parts, t, cos, sin, w):
                        a, b = src[..., 0:8], src[..., 8:16]
                        sh = [parts, t, 8, 8] if t else [parts, 8, 8]
                        up = lambda c: c.rearrange("p (t f) -> p t f", t=t).unsqueeze(2).broadcast_to(sh) if t else c.unsqueeze(1).broadcast_to(sh)
                        tmp = [w[:, k].rearrange("p (t h f) -> p t h f", t=t, h=8) if t else w[:, k].rearrange("p (h f) -> p h f", h=8) for k in range(4)]
                        if t:
                            for u in range(t):
                                aa, bb = a[:, u], b[:, u]
                                cc, ss = up(cos)[:, u], up(sin)[:, u]
                                tt2(tmp[0][:, u], aa, cc, ALU.mult)
                                tt2(tmp[1][:, u], bb, ss, ALU.mult)
                                tt2(tmp[2][:, u], bb, cc, ALU.mult)
                                ch(tt2(tmp[3][:, u], aa, ss, ALU.mult))
                                tt2(aa, tmp[0][:, u], tmp[1][:, u], ALU.subtract)
                                ins = tt2(bb, tmp[2][:, u], tmp[3][:, u], ALU.add)
                                if u < t - 1:
                                    ch(ins)
                        else:
                            tt2(tmp[0], a, up(cos), ALU.mult)
                            tt2(tmp[1], b, up(sin), ALU.mult)
                            tt2(tmp[2], b, up(cos), ALU.mult)
                            ch(tt2(tmp[3], a, up(sin), ALU.mult))
                            tt2(a, tmp[0], tmp[1], ALU.subtract)
                            ins = tt2(b, tmp[2], tmp[3], ALU.add)
                        ins.then_inc(S("rope"), 1)

                    w4 = sqt[:, 0:512].rearrange("p (k n) -> p k n", k=4)
                    rope(tok[:, :, 0:512].rearrange("p t (h d) -> p t h d", h=8), P, 2, C("cos"), C("sin"), w4)
                    rope(smp[:, 0:512].rearrange("p (h d) -> p h d", h=8), B, 0, C("cos_s", B), C("sin_s", B), w4[0:B, :, 0:64])
                    dve.wait_ge(S("gate_ln"), 1)
                    ch(stt(gate[:, :, :], gate_in[:, :, :], 0.0, gate_t[:, :, :], ALU.max, ALU.add))
                    tt2(gate[:, :, :], gate[:, :, :], mul12[:, :].unsqueeze(1).broadcast_to([P, 3, 12]), ALU.mult).then_inc(S("gate_sp"), 1)
                    dve.wait_ge(S("par_taken"), 4)
                    for t in range(NCT):
                        src = proj[:, CT0 + t, :]
                        ch(ts(conv_t[:, t, :], src[:, 0:L], cwt[:, t, 3:4], None, ALU.mult))
                        for k in (1, 2, 3):
                            ins = stt(conv_t[:, t, k:L], src[:, 0:L - k], cwt[:, t, 3 - k:4 - k], conv_t[:, t, k:L], ALU.mult, ALU.add)
                            if k < 3:
                                ch(ins)
                            else:
                                ins.then_inc(S("conv"), 1)
                    dve.wait_ge(S("cum_mm"), 1)
                    dve.tensor_copy(cum[:, :], ps[:, 6, 0:24]).then_inc(S("cum_sb"), 1)
                    dve.wait_ge(S("cum_sb"), 1)
                    cg = cum[:, 0:16].rearrange("p (t k) -> p t k", t=2)[:, :, 4:8]
                    tot = cum[:, 16:24].rearrange("p (t k) -> p t k", t=2)
                    dve.tensor_copy(eg[:, 0, :].rearrange("p (t k) -> p t k", t=2), cg)
                    dve.tensor_copy(eg[:, 1, :].rearrange("p (t k) -> p t k", t=2), tot)
                    tt2(eg[:, 2, :].rearrange("p (t k) -> p t k", t=2), tot, cg, ALU.subtract).then_inc(S("cum_sb"), 1)
                    dve.wait_ge(S("rows_mm"), 1)
                    fr = ps[0:4, 7, 0:256]
                    gr = ps[0:4, 7, 256:512]
                    ts(rows[:, 0, :], fr, 8.0, None, ALU.mult)
                    ts(rows[:, 1, :], fr, -8.0, None, ALU.mult)
                    ts(rows[:, 2, :], gr, 1.0, None, ALU.mult)
                    ts(rows[:, 3, :], gr, -1.0, None, ALU.mult).then_inc(S("rows"), 1)
                    dve.wait_ge(S("dt_mm"), 1)
                    tt2(dt_[:, :, :].rearrange("p t (h i) -> p (t h) i", h=H), ps[:, 4:6, :].rearrange("p t (h i) -> p (t h) i", h=H),
                        C("causal").unsqueeze(1).broadcast_to([P, 2 * H, P]), ALU.add).then_inc(S("dt_masked"), 1)

                    def masked(m, name):
                        dve.wait_ge(S("scores"), m + 1)
                        ch(stt(smx, ps[:, 0:4, 0:384], HD ** -0.5, C(name).unsqueeze(1).broadcast_to([P, H, 384]), ALU.mult, ALU.add))
                        red(small[:, 32:36], smx[:, :, 0:P], AX.X, ALU.max, negate=True)
                        red(small[:, 36:40], smx[:, :, P:3 * P], AX.X, ALU.max, negate=True).then_inc(S("row_max"), 1)

                    def attend_out(m, c0):
                        dve.wait_ge(S("p_turned"), 3 * m + 2)
                        dve.tensor_copy(ptr[:, 1, :], ps[:, 1, :]).then_inc(S("ptr_dve"), 1)
                        dve.wait_ge(S("p_exp"), 8 * (m + 1))
                        ch(dve.reciprocal(small[:, 48:56], small[:, 40:48]))
                        dve.wait_ge(S("o_mm"), m + 1)
                        tt2(otok[:, :, c0:c0 + GW].rearrange("p t (h d) -> p t h d", h=H), ps[:, 3, :].rearrange("p (t h d) -> p t h d", t=2, h=H),
                            small[:, 48:56].rearrange("p (t h) -> p t h", t=2).unsqueeze(3).broadcast_to([P, 2, H, HD]), ALU.mult).then_inc(S("o_att"), 1)

                    four_ = lambda ap: ap.rearrange("p g (h d) -> p g h d", h=H)

                    def sample_add(b):
                        i, u = b % 2, 2 * (b // 2 % 2) + b % 2
                        dve.wait_ge(S("prod"), b + 1)
                        red(s13[:, u, 0:NPG, :], four_(prod[:, 0:NPG, :]), AX.X, ALU.add).then_inc(S("s_red"), 1)
                        dve.wait_ge(S(f"k_used{i}"), b // 2 + 1)
                        red(s13[:, u, FOX_PG:FOX_PG + CACHE_T, :], four_(prod[:, NPG:NKT, :]), AX.X, ALU.add).then_inc(S("s_red"), 1)

                    def sample_bias(j):
                        dve.wait_ge(S("s_red"), 4 * j + 4)
                        sc = HD ** -0.5
                        f = lambda ap: ap.rearrange("p g h -> p (g h)")
                        for i in range(2):
                            b, u = 2 * j + i, 2 * (j % 2) + i
                            stt(f(s13[:, u, 0:NPG, :]), f(s13[:, u, 0:NPG, :]), sc, f(bias[:, b, 0:NPG, :]), ALU.mult, ALU.add)
                            stt(f(s13[:, u, FOX_PG:FOX_PG + CACHE_T, :]), f(s13[:, u, FOX_PG:FOX_PG + CACHE_T, :]), sc,
                                f(bias[:, b, NPG:NKT, :]), ALU.mult, ALU.add)
                        u = 2 * (j % 2)
                        dve.tensor_copy(s13[:, u:u + 2, NPG, :], sx[:, 2 * j:2 * j + 2, 0, :])
                        dve.tensor_copy(s13[:, u:u + 2, NPAGE - 1, :], sx[:, 2 * j:2 * j + 2, 1, :]).then_inc(S("s_sc"), 1)
                        dve.wait_ge(S("s_sc"), j + 1)
                        for i in range(2):
                            red(pmax[:, i, 0, :], s13[:, u + i, 0:FOX_PG, :].rearrange("p g h -> p h g"), AX.X, ALU.max)
                            ins = red(pmax[:, i, 1, :], s13[:, u + i, FOX_PG:NPAGE, :].rearrange("p g h -> p h g"), AX.X, ALU.max)
                        ins.then_inc(S("s_max"), 1)

                    def sample_shift(j):
                        u = 2 * (j % 2)
                        dve.wait_ge(S("s_max_all"), j + 1)
                        for i in range(2):
                            tt2(s13[:, u + i, 0:FOX_PG, :], s13[:, u + i, 0:FOX_PG, :], pmax_all[:, i, 0, :].unsqueeze(1).broadcast_to([P, FOX_PG, H]), ALU.subtract)
                            ins = tt2(s13[:, u + i, FOX_PG:NPAGE, :], s13[:, u + i, FOX_PG:NPAGE, :], pmax_all[:, i, 1, :].unsqueeze(1).broadcast_to([P, SWA_PG, H]), ALU.subtract)
                        ins.then_inc(S("s13"), 1)

                    def sample_out(j):
                        dve.wait_ge(S("pv_mm"), j + 1)
                        where = [orow(m, i) for m in range(2) for i in range(2)]
                        for r0 in where:
                            ins = dve.reciprocal(small[r0:r0 + H, 124:125], ps[r0:r0 + H, 7, GW:GW + 1])
                        ins.then_inc(S("rc"), 1)
                        dve.wait_ge(S("rc"), j + 1)
                        for r0 in where:
                            ins = stt(oms[r0:r0 + H, j, :], ps[r0:r0 + H, 7, 0:GW], small[r0:r0 + H, 124:125],
                                      const[r0:r0 + H, COL["head_block"][0]:COL["head_block"][0] + GW], ALU.mult, ALU.mult)
                        ins.then_inc(S("oms"), 1)

                    masked(0, "fox_mask")
                    dve.wait_ge(S("lf_turned"), 1)
                    dve.tensor_copy(sqt[:, 0:256], ps[:, 6, 0:256]).then_inc(S("lf_sb"), 1)
                    tt2(sqt[0:B, 256:512].rearrange("p (h b g) -> p h b g", h=H, b=B),
                        C("ident", B)[:, 0:B].unsqueeze(1).unsqueeze(3).broadcast_to([B, H, B, NPG]),
                        gate[0:B, 2, 0:4].unsqueeze(2).unsqueeze(3).broadcast_to([B, H, B, NPG]), ALU.mult).then_inc(S("lf_sb"), 1)
                    dve.wait_ge(S("ck_turned"), 2)
                    dve.tensor_copy(ck[:, 1, 0:512], ps[:, 4, :])
                    dve.tensor_copy(ck[:, 1, 512:896], ps[:, 5, 0:384]).then_inc(S("ck_dve"), 1)
                    dve.wait_ge(S("dec_mm"), 1)
                    dve.tensor_copy(bias[:, :, 0:NPG, :], ps[:, 6, 256:512].rearrange("p (h b g) -> p b g h", h=H, b=B))
                    ch(dve.tensor_copy(bias[:, :, NPG:NKT, :], C("window").rearrange("p (g h) -> p g h", h=H).unsqueeze(1).broadcast_to([P, B, CACHE_T, H])))
                    own = v_own[:, 0, 0:GW]
                    for k, (qc, kc) in enumerate(((QB_, KB_), (QA, KA))):
                        ch(tt2(own, smp[:, qc:qc + GW], smp[:, kc:kc + GW], ALU.mult))
                        ch(red(small[0:B, 112 + 4 * k:116 + 4 * k], own.rearrange("p (h d) -> p h d", h=H), AX.X, ALU.add))
                    ch(ts(small[0:B, 112:120], small[0:B, 112:120], HD ** -0.5, None, ALU.mult))
                    ch(dve.tensor_copy(sx[:, :, :, :], C("own_bias").rearrange("p (b k h) -> p b k h", b=B, k=2)))
                    ch(tt2(sx[0:B, :, :, :].rearrange("p b k h -> p b (k h)"), sx[0:B, :, :, :].rearrange("p b k h -> p b (k h)"),
                           small[0:B, 112:120].unsqueeze(1).broadcast_to([B, B, 8]), ALU.add))
                    dve.memset(v_own[:, :, GW:GW + 1], 1.0)
                    ch(dve.tensor_copy(v_own[:, 0, 0:GW], smp[:, VB_:VB_ + GW]))
                    dve.tensor_copy(v_own[:, 1, 0:GW], smp[:, VA:VA + GW]).then_inc(S("v_own"), 1)
                    sample_add(0)
                    dve.wait_ge(S("s_silu"), 1)
                    dve.memset(small[64:96, 0:1], 1.0)
                    ch(tt2(cv[0:64, 7, :], cv[0:64, 8, :], cv[0:64, 8, :], ALU.mult))
                    red(small[0:64, 0:1], cv[0:64, 7, :], AX.X, ALU.add).then_inc(S("mix_ss"), 1)
                    attend_out(0, 256)
                    dve.wait_ge(S("mix_r"), 1)
                    ts(cv[:, 8, :], cv[:, 8, :], small[0:96, 0:1], C("q_scale", 96), ALU.mult, ALU.mult).then_inc(S("s_conv"), 1)
                    dve.wait_ge(S("qk_turned"), 1)
                    dve.tensor_copy(qkT[:, :, P:L], ps[:, 5, :].rearrange("p (t n) -> p t n", t=4)).then_inc(S("qk_dve"), 1)
                    masked(1, "swa_mask")
                    sample_add(1)
                    sample_bias(0)
                    dve.wait_ge(S("ck_act"), 2)
                    dve.wait_ge(S("ck_dve"), 1)
                    qk = ck[:, :, COFF:COFF + 512]
                    kb2 = kb_n[:, :, :].rearrange("p t n -> p (t n)")
                    for t in range(NT):
                        ch(tt2(kb2, qk[:, t], qk[:, t], ALU.mult))
                        ins = red(small[:, 8 + 8 * t:16 + 8 * t], kb2.rearrange("p (h d) -> p h d", d=HD), AX.X, ALU.add)
                        if t == 0:
                            ch(ins)
                    ins.then_inc(S("mix_ss"), 1)
                    dve.wait_ge(S("gelu"), 2)
                    dve.wait_ge(S("mix_ss"), 2)
                    for t in range(NT):
                        ch(tt2(kb2[:, 0:GW], tok[:, t, VD:VD + GW], tok[:, t, VD:VD + GW], ALU.mult))
                        ch(red(small[:, 24 + t:25 + t], kb2[:, 0:GW], AX.X, ALU.add))
                    ch(dve.memset(small[:, 26:27], 1.0))
                    ch(tt2(kb2[0:B, 0:GW], smp[:, VD:VD + GW], smp[:, VD:VD + GW], ALU.mult))
                    red(small[0:B, 26:27], kb2[0:B, 0:GW], AX.X, ALU.add).then_inc(S("mix_ss"), 1)
                    sample_shift(0)
                    attend_out(1, 0)
                    sample_out(0)
                    dve.wait_ge(S("mix_r"), 2)
                    for t in range(NT):
                        ch(ts(small[:, 8 + 8 * t:12 + 8 * t], small[:, 8 + 8 * t:12 + 8 * t], HD ** -0.5, None, ALU.mult))
                    for t in range(NT):
                        q8 = qk[:, t].rearrange("p (h d) -> p h d", d=HD)
                        tt2(q8, q8, small[:, 8 + 8 * t:16 + 8 * t].unsqueeze(2).broadcast_to([P, 8, HD]), ALU.mult).then_inc(S("qk_n"), 1)
                    dve.wait_ge(S("qk_n"), 2)
                    dve.wait_ge(S("eg"), 1)
                    dve.wait_ge(S("gates"), 1)
                    k4 = ck[:, :, COFF + GW:COFF + 2 * GW].rearrange("p t (h d) -> p t h d", h=H)
                    v4 = ck[:, :, COFF + 2 * GW:COFF + 3 * GW].rearrange("p t (h d) -> p t h d", h=H)
                    four = lambda ap: ap.rearrange("p t (h d) -> p t h d", h=H)
                    bt = gate[:, 0:2, 8:12].unsqueeze(3).broadcast_to([P, 2, H, HD])
                    tt2(four(kb_n[:, :, :]), k4, bt, ALU.mult).then_inc(S("kb"), 1)
                    tt2(v4, v4, bt, ALU.mult)
                    ch(tt2(four(kd[:, :, :]), k4, eg[:, 2, :].rearrange("p (t k) -> p t k", t=2).unsqueeze(3).broadcast_to([P, 2, H, HD]), ALU.mult))
                    dve.wait_ge(S("kq_turned"), 2)
                    dve.tensor_copy(kqT[:, 0:2, :, P:L], ps[:, 6, :].rearrange("p (k a n) -> p k a n", k=2, a=2))
                    dve.tensor_copy(kqT[:, 2, :, P:L], ps[:, 7, 0:256].rearrange("p (a n) -> p a n", a=2)).then_inc(S("kq_dve"), 1)
                    dve.wait_ge(S("mix_r"), 3)
                    for t in range(NT):
                        ins = stt(tok[:, t, VD:VD + GW], tok[:, t, VD:VD + GW], small[:, 24 + t:25 + t], gv[:, :], ALU.mult, ALU.mult)
                    ins.then_inc(S("v_n"), 1)
                    stt(smp[:, VD:VD + GW], smp[:, VD:VD + GW], small[0:B, 26:27], gv[0:B, :], ALU.mult, ALU.mult).then_inc(S("gmlp_v"), 1)
                    dve.wait_ge(S("gmlp_v"), 1)
                    od = smp_o[:, 768:1024].rearrange("p (h d) -> p h d", h=H)
                    eight = lambda ap: ap.unsqueeze(2).broadcast_to([B, H, HD])
                    ch(tt2(od, smp[:, VD:VD + GW].rearrange("p (h d) -> p h d", h=H), eight(ws0[:, 0, :]), ALU.mult))
                    ch(tt2(od, od, eight(ws0[:, 1, :]), ALU.add))
                    ch(tt2(smp_o[:, 768:1024], smp_o[:, 768:1024], smp[:, UD:UD + GW], ALU.mult))
                    sample_add(2)
                    dve.wait_ge(S("gmlp_mm"), 1)
                    mix = otok[:, :, 768:1024]
                    ch(tt2(four(mix), ps[:, 3, :].rearrange("p (t h d) -> p t h d", t=2, h=H), bst[:, :].unsqueeze(1).unsqueeze(3).broadcast_to([P, 2, H, HD]), ALU.add))
                    ch(tt2(mix, mix, tok[:, :, UD:UD + GW], ALU.mult))
                    dve.wait_ge(S("dt"), 1)
                    for t in range(NT):
                        dve.wait_ge(S("kk_mm"), t + 1)
                        kk = ps[:, 4 + 2 * t:6 + 2 * t, :].rearrange("p a (b k i) -> p a b k i", b=2, k=2)
                        h22 = lambda ap: ap.rearrange("p (b a i) -> p a b i", b=2, a=2)
                        h4 = lambda ap: ap.rearrange("p (h i) -> p h i", h=H)
                        ch(tt2(h22(at_[:, t, :]), kk[:, :, :, 0, :], h22(dt_[:, t, :]), ALU.mult))
                        tt2(h22(qkt[:, t, :]), kk[:, :, :, 1, :], h22(dt_[:, t, :]), ALU.mult).then_inc(S("qkt"), 1)
                    h8 = lambda ap: ap.rearrange("p t (h i) -> p (t h) i", h=H)
                    wide = lambda name: C(name).unsqueeze(1).broadcast_to([P, 8, P])
                    tt2(h8(at_[:, :, :]), h8(at_[:, :, :]), wide("strict"), ALU.mult).then_inc(S("at"), 1)
                    dve.wait_ge(S("at"), 1)
                    ch(tt2(h8(tt[:, :, :]), h8(at_[:, :, :]), wide("level1T"), ALU.mult))
                    tt2(h8(tt[:, :, :]), wide("ident"), h8(tt[:, :, :]), ALU.subtract).then_inc(S("tt0"), 1)
                    sample_add(3)
                    sample_bias(1)
                    between = {0: [lambda: sample_shift(1)], 1: [lambda: sample_out(1)], 2: [lambda: sample_add(4)],
                               3: [lambda: sample_add(5), lambda: sample_bias(2)], 4: [lambda: sample_shift(2)]}
                    for k, b in enumerate(LEVELS):
                        for t in range(NT):
                            dve.wait_ge(S(f"y_mm{t}"), k + 1)
                            m = C(f"level{b}").unsqueeze(1).broadcast_to([P, H, P])
                            tt2(h4(ys[:, t, :]), h4(ps[:, 3 * t, :]), m, ALU.mult).then_inc(S(f"ys{t}"), 1)
                        for t in range(NT):
                            dve.wait_ge(S(f"z_mm{t}"), k + 1)
                            dve.wait_ge(S("tm_act"), 2)
                            if k < len(LEVELS) - 1:
                                tt2(tm[:, t, :], tm[:, t, :], ps[:, 3 * t + 1, :], ALU.subtract)
                            tt2(tt[:, t, :], tt[:, t, :], ps[:, 3 * t + 2, :], ALU.subtract).then_inc(S(f"lev{t}"), 1)
                        for step in between.get(k, []):
                            step()
                    dve.wait_ge(S("vn_mm"), 1)
                    dve.tensor_copy(vn[:, 0, :], ps[:, 0, 0:GW]).then_inc(S("vn"), 1)
                    dve.wait_ge(S("oc_mm"), 1)
                    dve.tensor_copy(otok[:, 0, 512:768], ps[:, 1, 0:GW])
                    dve.tensor_copy(st_s[:, :, :], ps[:, 2, 0:128].rearrange("p (a v) -> p a v", a=2)).then_inc(S("st"), 1)
                    dve.wait_ge(S("ks_mm"), 1)
                    e1 = eg[:, 0, 4:8].rearrange("p (b a) -> p a b", a=2).unsqueeze(3).broadcast_to([P, 2, 2, HD])
                    hh = lambda ap: ap.rearrange("p (b a d) -> p a b d", b=2, a=2)
                    ks = lambda kind: ps[:, 3:5, P * kind:P * kind + P].rearrange("p a (b d) -> p a b d", b=2)
                    ch(tt2(hh(kb_n[:, 0, :]), ks(0), e1, ALU.mult))
                    tt2(kb_n[:, 0, :], ck[:, 1, COFF + 2 * GW:COFF + 3 * GW], kb_n[:, 0, :], ALU.subtract).then_inc(S("rhs1"), 1)
                    tt2(hh(kb_n[:, 1, :]), ks(1), e1, ALU.mult)
                    dve.wait_ge(S("vn_mm"), 2)
                    dve.tensor_copy(vn[:, 1, :], ps[:, 0, 0:GW]).then_inc(S("vn"), 1)
                    dve.wait_ge(S("oc_mm"), 2)
                    ch(tt2(otok[:, 1, 512:768], kb_n[:, 1, :], ps[:, 1, 0:GW], ALU.add))
                    for h in range(H):
                        p0 = 64 * (h % 2)
                        sl = st_s[p0:p0 + 64, h // 2, :]
                        stt(sl, sl, eg[p0:p0 + 64, 1, 4 + h:5 + h], ps[p0:p0 + 64, 2, 64 * (h // 2):64 * (h // 2) + 64], ALU.mult, ALU.add).then_inc(S("p_state"), 1)

                    sample_out(2)
                    sample_add(6)
                    dve.wait_ge(S("state_in"), 16 * (B + 4 + 2 + 4))
                    eb = small[:, 120:122]
                    dve.wait_ge(S("sg"), 1)
                    kc16 = kq16[:, 1, :].unsqueeze(2).broadcast_to([P, 16, HD])
                    qc16 = kq16[:, 0, :].unsqueeze(2).broadcast_to([P, 16, HD])
                    sk = skp[:, :, :]
                    ch(ts(state[:, :, :], state[:, :, :], eb[:, 0:1], None, ALU.mult))
                    ch(tt2(sk, state[:, :, :], kc16, ALU.mult))
                    red(sk_r[:, :], sk.rearrange("p k v -> p v k"), AX.X, ALU.add).then_inc(S("sk"), 1)
                    sample_add(7)
                    sample_bias(3)
                    dve.wait_ge(S("sk_mm"), 1)
                    ch(tt2(v64[:, :], v64[:, :], ps[:, 6, 0:HD], ALU.subtract))
                    ch(ts(v64[:, :], v64[:, :], gb[:, 1:2], None, ALU.mult))
                    ch(tt2(sk, kc16, v64[:, :].unsqueeze(1).broadcast_to([P, 16, HD]), ALU.mult))
                    tt2(state[:, :, :], state[:, :, :], sk, ALU.add).then_inc(S("s_state"), 1)
                    dve.wait_ge(S("s_state"), 1)
                    ch(tt2(sk, state[:, :, :], qc16, ALU.mult))
                    red(sk_r[:, :], sk.rearrange("p k v -> p v k"), AX.X, ALU.add).then_inc(S("sk"), 1)
                    sample_shift(3)
                    dve.wait_ge(S("sk_mm"), 2)
                    dve.tensor_copy(v64[:, :], ps[:, 6, 0:HD]).then_inc(S("s_out"), 1)

                    sample_out(3)

                    for t in range(NT):
                        ch(tt2(sqt[:, :], otok[:, t, :], otok[:, t, :], ALU.mult))
                        ins = red(small[:, 64 + 16 * t:80 + 16 * t], sqt[:, :].rearrange("p (h d) -> p h d", d=HD), AX.X, ALU.add)
                        if t == 0:
                            ch(ins)
                    ins.then_inc(S("mix_ss"), 1)
                    dve.wait_ge(S("mix_ss"), 4)
                    dve.wait_ge(S("so_mm"), 1)
                    dve.tensor_copy(smp_o[:, 0:512], ps[0:B, 5, :]).then_inc(S("so"), 1)
                    dve.wait_ge(S("so"), 1)
                    dve.wait_ge(S("oc_in"), 16)
                    ch(tt2(sqt[0:B, :], smp_o[:, :], smp_o[:, :], ALU.mult))
                    red(small[0:B, 96:112], sqt[0:B, :].rearrange("p (h d) -> p h d", d=HD), AX.X, ALU.add).then_inc(S("mix_ss"), 1)
                    dve.wait_ge(S("mix_r"), 4)
                    dve.wait_ge(S("silu_z"), 2)
                    for t in range(NT):
                        o16 = otok[:, t, :].rearrange("p (h d) -> p h d", d=HD)
                        ch(tt2(o16, o16, small[:, 64 + 16 * t:80 + 16 * t].unsqueeze(2).broadcast_to([P, 16, HD]), ALU.mult))
                    ch(tt2(otok[:, :, :], otok[:, :, :], og[:, :].unsqueeze(1).broadcast_to([P, 2, D]), ALU.mult))
                    tt2(otok[:, :, 512:768], otok[:, :, 512:768], tok[:, :, ZC:ZC + GW], ALU.mult).then_inc(S("mixed"), 1)
                    dve.wait_ge(S("mix_r"), 5)
                    o16 = smp_o[:, :].rearrange("p (h d) -> p h d", d=HD)
                    ch(tt2(o16, o16, small[0:B, 96:112].unsqueeze(2).broadcast_to([B, 16, HD]), ALU.mult))
                    ch(tt2(smp_o[:, :], smp_o[:, :], og[0:B, :], ALU.mult))
                    tt2(smp_o[:, 512:768], smp_o[:, 512:768], smp[:, ZC:ZC + GW], ALU.mult).then_inc(S("mixed"), 1)
                    for t in range(KT):
                        dve.wait_ge(S("o_hi"), t + 1)
                        tt2(nlo[:, t, :], ps[:, t, 0:N], nhi[:, t, :].bitcast(F32), ALU.subtract).then_inc(S("mix_ready"), 1)

                    lo("wo", 0, 0)
                    lo("wo", 0, 1)
                    for s in range(2):
                        lo("wo", 1, s)
                    for s in range(2):
                        lo("gu2", 0, s)
                    post(3)
                    rsqrt_of(4)
                    with dve.Fori(0, GU_P - 1) as j:
                        gu_step(2, j, ("gu2", j + 1))
                    gu_step(2, GU_P - 1, ("dn2", 0))
                    with dve.Fori(1, DN_P) as j:
                        lo("dn2", j, 0)
                        lo("dn2", j, 1)
                    post(5)

                @blk.tensor
                def _(pe):
                    mm, tr = pe.matmul, pe.transpose

                    def three(out, s, woff, hi_, lo_, first, last):
                        wh, wl = whi[s][:, woff:woff + P], wlo[s][:, woff:woff + P]
                        mm(out, wh, hi_, start=first, stop=False)
                        mm(out, wh, lo_, start=False, stop=False)
                        return mm(out, wl, hi_, start=False, stop=last)

                    def split_ready(n, j, s, part):
                        pe.wait_ge(S(f"w_lo{s}"), 2 * (P0[n] + j) + part + 1)

                    def wide_chunk(n, j, s, banks, free):
                        for i in range(2):
                            free(i)
                            for k in range(KT):
                                if i == 0 and k in (0, 4):
                                    split_ready(n, j, s, k // 4)
                                ins = three(ps[:, banks[i], 0:N], s, k * 256 + i * P, nhi[:, k, :], nlo[:, k, :], k == 0, k == KT - 1)
                            ins.then_inc(S(f"mm_done{s}"), 1)

                    def first_pair(n, e):
                        for k in range(KT):
                            pe.wait_ge(S("n_ready"), 8 * (e // 2) + k + 1)
                            if k in (0, 4):
                                split_ready(n, 0, 0, k // 4)
                            for i in range(2):
                                ins = three(ps[:, i, 0:N], 0, k * 256 + i * P, nhi[:, k, :], nlo[:, k, :], k == 0, k == KT - 1)
                                if k == KT - 1:
                                    ins.then_inc(S("mm_done0"), 1)
                        wide_chunk(n, 0, 1, (2, 3), lambda i: ss(e) if i else None)

                    def gu_step(k, j):
                        n = f"gu{k}"
                        wide_chunk(n, j, 0, (0, 1), lambda i: pe.wait_ge(S("gate_taken"), 22 * (k - 1) + 2 * j + i + 1))
                        wide_chunk(n, j, 1, (2, 3), lambda i: pe.wait_ge(S("up_taken"), 22 * (k - 1) + 2 * j + i + 1))

                    def dn_pair(k, q):
                        n, e = f"dn{k}", {1: 1, 2: 5}[k]
                        for m in range(2):
                            j = 2 * q + m
                            pe.wait_ge(S("sq"), 8 * e + j - 1)
                            for s in range(2):
                                for kk in range(11):
                                    if kk in (0, 6):
                                        split_ready(n, j, s, kk // 6)
                                    t = 11 * s + kk
                                    ins = three(ps[:, 4 + m, 0:N], s, kk * P, hhi[:, t, :], hlo[:, t, :], t == 0, t == FT - 1)
                                ins.then_inc(S(f"mm_done{s}"), 1)

                    def ss(e):
                        pe.wait_ge(S("ss_acc"), e + 1)
                        mm(ps[:, 7, 0:N], C("mean"), ss_acc[:, :], start=True, stop=True).then_inc(S("ss"), 1)

                    pe.wait_ge(S("gain_in"), 16)
                    tr(ps[:, 4, 0:48], gin[0:48, :], C("ident", 48)[:, 0:48]).then_inc(S("par_turned"), 1)
                    first_pair("gu1", 0)
                    pe.wait_ge(S("par_in"), 48)
                    pe.wait_ge(S("par_taken"), 1)
                    for g in range(H):
                        tr(ps[:, 5, g * P:(g + 1) * P], win[:, g, :], ident)
                    tr(ps[:, 6, 0:H], bin_[:, :], C("ident", H)[:, 0:H]).then_inc(S("par_turned"), 1)
                    for t in range(NCT):
                        ins = tr(ps[:, 4, 64 + 4 * t:68 + 4 * t], cwin[:, t * P:(t + 1) * P], C("ident", 4)[:, 0:4])
                    ins.then_inc(S("par_turned"), 1)
                    with pe.Fori(1, GU_P) as j:
                        gu_step(1, j)
                    pe.wait_ge(S("par_taken"), 4)
                    pe.wait_ge(S("h_ready"), 22)
                    with pe.Fori(0, DN_P // 2) as q:
                        dn_pair(1, q)
                    ss(1)
                    pe.wait_ge(S("pa_taken"), 2)
                    pe.wait_ge(S("pd_taken"), 2)
                    pe.wait_ge(S("up_taken"), 24)
                    first_pair("wi", 2)
                    with pe.Fori(1, WI_P - 1) as j:
                        wide_chunk("wi", j, 0, (0, 1), lambda i: pe.wait_ge(S("pa_taken"), 2 * j + i + 1))
                        wide_chunk("wi", j, 1, (2, 3), lambda i: pe.wait_ge(S("pd_taken"), 2 * j + i + 1))
                    pe.wait_ge(S("pa_taken"), 2 * (WI_P - 1) + 1)
                    for s in range(2):
                        for k in range(4):
                            if k in (0, 2):
                                split_ready("wi", WI_P - 1, s, k // 2)
                            t = 4 * s + k
                            ins = three(ps[:, 0, 0:N], s, k * P, nhi[:, t, :], nlo[:, t, :], t == 0, t == KT - 1)
                        ins.then_inc(S(f"mm_done{s}"), 1)

                    pe.wait_ge(S("pa_taken"), 2 + 2 * (WI_P - 1) + 1)
                    pe.wait_ge(S("pd_taken"), 2 + 2 * (WI_P - 1))
                    for g in range(7):
                        bk = 3 * (g % 2)
                        if g >= 2:
                            pe.wait_ge(S("tok_act"), 2 * (g - 1))
                            pe.wait_ge(S("tok_dve"), g - 1)
                        for part in range(3):
                            for i in range(4 if g < 6 else 1):
                                a, b = (part * P, part * P + P) if part < 2 else (L, N)
                                ins = tr(ps[0:b - a, bk + part, i * P:(i + 1) * P], proj[:, 4 * g + i, a:b], ident)
                            ins.then_inc(S("turned"), 1)
                    pe.wait_ge(S("gates"), 1)
                    mm(ps[:, 6, 0:8], C("upto"), gate[:, 0, 0:8], start=True, stop=True)
                    mm(ps[:, 6, 8:12], ones, gate[:, 0, 0:4], start=True, stop=False)
                    mm(ps[:, 6, 8:12], C("upto"), gate[:, 1, 0:4], start=False, stop=True)
                    mm(ps[:, 6, 12:16], C("upto"), gate[:, 1, 4:8], start=True, stop=True)
                    mm(ps[:, 6, 16:20], ones, gate[:, 0, 4:8], start=True, stop=True)
                    mm(ps[:, 6, 20:24], ones, gate[:, 1, 4:8], start=True, stop=True).then_inc(S("cum_mm"), 1)
                    pe.wait_ge(S("cum_sb"), 1)
                    for k, c0 in enumerate((0, 8, 4, 12)):
                        ins = tr(ps[0:4, 7, k * P:(k + 1) * P], cum[:, c0:c0 + 4], ident)
                    ins.then_inc(S("rows_mm"), 1)
                    pe.wait_ge(S("rows"), 1)
                    hr = lambda h: C("head_rows", 4)[:, h * P:(h + 1) * P]
                    for t in range(NT):
                        for h in range(H):
                            o = ps[:, 4 + t, h * P:(h + 1) * P]
                            mm(o, rows[:, 3, t * P:(t + 1) * P], hr(h), start=True, stop=False)
                            ins = mm(o, hr(h), rows[:, 2, t * P:(t + 1) * P], start=False, stop=True)
                    ins.then_inc(S("dt_mm"), 1)

                    def scores(m, q, k):
                        for h in range(H):
                            p0 = 64 * (h % 2)
                            qh, kh = q(h // 2)[p0:p0 + 64], k(h // 2)[p0:p0 + 64]
                            for c, qt, kt in ((0, 0, 0), (P, 1, 0), (2 * P, 1, 1)):
                                o = ps[:, h, c:c + P]
                                ins = mm(o, qh[:, qt * P:qt * P + P], kh[:, kt * P:kt * P + P], start=True, stop=(m == 1))
                                if m == 0:
                                    mm(o, rows[:, 0, qt * P:qt * P + P], hr(h), start=False, stop=False)
                                    ins = mm(o, hr(h), rows[:, 1, kt * P:kt * P + P], start=False, stop=True)
                        ins.then_inc(S("scores"), 1)

                    scores(0, lambda a: proj[:, 6 + a, :], lambda a: proj[:, 8 + a, :])
                    pe.wait_ge(S("conv_silu"), NCT)
                    pe.wait_ge(S("dt_masked"), 1)
                    for t in range(NT):
                        for c in range(NCT):
                            bk = (6 if t == 0 else 4) + c // 4
                            ins = tr(ps[:, bk, (c % 4) * P:(c % 4 + 1) * P], conv_t[:, c, t * P:(t + 1) * P], ident)
                        ins.then_inc(S("ck_turned"), 1)

                    def turn_p(m):
                        pe.wait_ge(S("p_exp"), 8 * (m + 1))
                        for k in range(3):
                            for h in range(H):
                                ins = tr(ps[:, k, h * P:(h + 1) * P], smx[:, h, k * P:(k + 1) * P], ident)
                            ins.then_inc(S("p_turned"), 1)

                    def values(m, c0):
                        pe.wait_ge(S("ptr_act"), 2 * (m + 1))
                        pe.wait_ge(S("ptr_dve"), m + 1)
                        for h in range(H):
                            hs = slice(h * P, (h + 1) * P)
                            v = lambda t: tok[:, t, c0 + h * HD:c0 + (h + 1) * HD]
                            o0, o1 = ps[:, 3, h * HD:(h + 1) * HD], ps[:, 3, GW + h * HD:GW + (h + 1) * HD]
                            mm(o0, ptr[:, 0, hs], v(0), start=True, stop=True)
                            mm(o1, ptr[:, 1, hs], v(0), start=True, stop=False)
                            ins = mm(o1, ptr[:, 2, hs], v(1), start=False, stop=True)
                        ins.then_inc(S("o_mm"), 1)

                    def sample_values(j):
                        pe.wait_ge(S("s_exp"), j + 1)
                        if j == 0:
                            pe.wait_ge(S("slot_ones"), 2)
                            pe.wait_ge(S("slot_zero"), 4)
                            pe.wait_ge(S("v_own"), 1)
                        else:
                            pe.wait_ge(S("oms"), j)
                        for i in range(2):
                            pe.wait_ge(S(f"v_in{i}"), 16 * NKT * (j + 1))
                            u = 2 * (j % 2) + i
                            for m, pages, own_page in ((0, range(0, NPG), NPG), (1, range(FOX_PG, FOX_PG + CACHE_T), NPAGE - 1)):
                                out = ps[orow(m, i):orow(m, i) + H, 7, 0:GW + 1]
                                for g in pages:
                                    mm(out, s13[:, u, g, :], vslot[:, i, g - m, :], start=(g == pages[0]), stop=False)
                                ins = mm(out, s13[0:B, u, own_page, :], v_own[:, m, :], start=False, stop=True)
                        ins.then_inc(S("pv_mm"), 1)

                    pe.wait_ge(S("ck_act"), 2)
                    pe.wait_ge(S("logf_in"), 16)
                    lf = otok[0:B * NPG, 0, 0:512].rearrange("p (n h) -> p n h", h=H)
                    for h in range(H):
                        ins = tr(ps[:, 6, h * 64:(h + 1) * 64], lf[:, :, h], C("ident", 64)[:, 0:64])
                    ins.then_inc(S("lf_turned"), 1)
                    pe.wait_ge(S("lf_sb"), 2)
                    lfs = sqt[:, 0:256]
                    dec = ps[:, 6, 256:512]
                    mm(dec, C("after"), lfs, start=True, stop=False)
                    v3 = lambda ap: ap.rearrange("p (q g) -> p q g", g=NPG)
                    for s in range(1, NPG):
                        mm(v3(dec)[:, :, 0:NPG - s], ones, v3(lfs)[:, :, s:NPG], start=False, stop=False, skip_group_check=True)
                    mm(dec, C("ones", B), sqt[0:B, 256:512], start=False, stop=True).then_inc(S("dec_mm"), 1)
                    turn_p(0)
                    values(0, VB_)
                    pe.wait_ge(S("rope"), 2)
                    pe.wait_ge(S("ck_dve"), 1)
                    for t in range(NT):
                        for c in range(4):
                            ins = tr(ps[:, 4 + t, c * P:(c + 1) * P], tok[:, t, c * P:(c + 1) * P], ident)
                    ins.then_inc(S("qk_turned"), 1)
                    pe.wait_ge(S("qk_act"), 1)
                    pe.wait_ge(S("qk_dve"), 1)
                    pe.wait_ge(S("o_att"), 1)
                    scores(1, lambda a: qkT[:, a, :], lambda a: qkT[:, 2 + a, :])
                    turn_p(1)
                    values(1, VA)
                    sample_values(0)
                    pe.wait_ge(S("kb"), 1)
                    pe.wait_ge(S("qk_n"), 2)
                    pe.wait_ge(S("dec_mm"), 1)
                    for t in range(NT):
                        if t:
                            pe.wait_ge(S("oms"), 1)
                        kinds = (ck[:, t, COFF + GW:COFF + 2 * GW], kb_n[:, t, :], ck[:, t, COFF:COFF + GW])
                        for k, src in enumerate(kinds):
                            for a in range(2):
                                n = 2 * k + a
                                ins = tr(ps[:, (4, 6)[t] + n // 4, (n % 4) * P:(n % 4 + 1) * P], src[:, a * P:(a + 1) * P], ident)
                        ins.then_inc(S("kq_turned"), 1)
                    pe.wait_ge(S("v_n"), 1)
                    pe.wait_ge(S("o_att"), 2)
                    for t in range(NT):
                        for g in range(H):
                            ins = mm(ps[:, 3, t * GW + g * HD:t * GW + (g + 1) * HD], wst[:, g, :], tok[:, t, VD + g * HD:VD + (g + 1) * HD], start=True, stop=True)
                    ins.then_inc(S("gmlp_mm"), 1)
                    pe.wait_ge(S("kq_act"), 2)
                    pe.wait_ge(S("kq_dve"), 1)
                    for t in range(NT):
                        for h in range(H):
                            p0, a = 64 * (h % 2), h // 2
                            ins = mm(ps[:, (4, 6)[t] + h % 2, (h // 2) * 256:(h // 2) * 256 + 256], kqT[p0:p0 + 64, 0, a, t * P:(t + 1) * P],
                                     kqT[p0:p0 + 64, 1:3, a, t * P:(t + 1) * P], start=True, stop=True)
                        ins.then_inc(S("kk_mm"), 1)
                    pe.wait_ge(S("tt0"), 1)
                    for t in range(NT):
                        for h in range(H):
                            hs = slice(h * P, (h + 1) * P)
                            ins = tr(ps[:, 4 + t, hs], tt[:, t, hs], ident)
                        ins.then_inc(S("tt_turned"), 1)
                    for k in range(len(LEVELS)):
                        for t in range(NT):
                            if k == 0:
                                pe.wait_ge(S("tm_act"), t + 1)
                                if t == 0:
                                    pe.wait_ge(S("gmlp_mm"), 1)
                                    pe.wait_ge(S("tt0"), 1)
                            else:
                                pe.wait_ge(S(f"lev{t}"), k)
                            for h in range(H):
                                hs = slice(h * P, (h + 1) * P)
                                ins = mm(ps[:, 3 * t, hs], at_[:, t, hs], tm[:, t, hs], start=True, stop=True)
                            ins.then_inc(S(f"y_mm{t}"), 1)
                        for t in range(NT):
                            pe.wait_ge(S(f"ys{t}"), k + 1)
                            if k == 0 and t == 0:
                                pe.wait_ge(S("tm_act"), 2)
                            for h in range(H):
                                hs = slice(h * P, (h + 1) * P)
                                if k < len(LEVELS) - 1:
                                    mm(ps[:, 3 * t + 1, hs], tt[:, t, hs], ys[:, t, hs], start=True, stop=True)
                                ins = mm(ps[:, 3 * t + 2, hs], ys[:, t, hs], tt[:, t, hs], start=True, stop=True)
                            ins.then_inc(S(f"z_mm{t}"), 1)
                        if k == 1:
                            sample_values(1)
                    nl = len(LEVELS)
                    pe.wait_ge(S("lev0"), nl)
                    pe.wait_ge(S("lev1"), nl)
                    hd = lambda h: slice(h * HD, (h + 1) * HD)
                    hp = lambda h: slice(h * P, (h + 1) * P)

                    def new_values(t, rhs):
                        for h in range(H):
                            ins = mm(ps[:, 0, hd(h)], tt[:, t, hp(h)], rhs[:, hd(h)], start=True, stop=True)
                        ins.then_inc(S("vn_mm"), 1)

                    def out_state(t):
                        pe.wait_ge(S("vn"), t + 1)
                        for h in range(H):
                            mm(ps[:, 1, hd(h)], qkt[:, t, hp(h)], vn[:, t, hd(h)], start=True, stop=True)
                        for h in range(H):
                            p0, a = 64 * (h % 2), h // 2
                            ins = mm(ps[p0:p0 + 64, 2, a * HD:(a + 1) * HD], kd[:, t, hd(h)], vn[:, t, hd(h)], start=True, stop=True)
                        ins.then_inc(S("oc_mm"), 1)

                    sample_values(2)
                    new_values(0, ck[:, 0, COFF + 2 * GW:COFF + 3 * GW])
                    out_state(0)
                    pe.wait_ge(S("st"), 1)
                    for kind in (1, 2):
                        for h in range(H):
                            p0, a = 64 * (h % 2), h // 2
                            c = P * (kind - 1) + a * HD
                            ins = mm(ps[:, 3 + h % 2, c:c + HD], kqT[p0:p0 + 64, kind, a, P:L], st_s[p0:p0 + 64, a, :], start=True, stop=True)
                    ins.then_inc(S("ks_mm"), 1)
                    pe.wait_ge(S("rhs1"), 1)
                    new_values(1, kb_n[:, 0, :])
                    out_state(1)
                    for k in range(2):
                        pe.wait_ge(S("sk"), k + 1)
                        mm(ps[:, 6, 0:HD], C("same_state"), sk_r[:, :], start=True, stop=True).then_inc(S("sk_mm"), 1)
                    sample_values(3)
                    pe.wait_ge(S("oms"), 4)
                    for m in range(2):
                        for j in range(B // 2):
                            c = m * (B // 2) + j
                            ins = mm(ps[0:B, 5, (1 - m) * GW:(2 - m) * GW], C("to_token", OROWS)[:, c * B:(c + 1) * B], oms[:, j, :], start=(j == 0), stop=(j == B // 2 - 1))
                    ins.then_inc(S("so_mm"), 1)
                    pe.wait_ge(S("so"), 1)
                    pe.wait_ge(S("mixed"), 2)
                    for t in range(KT):
                        for a in range(NT):
                            tr(ps[:, t, a * P:(a + 1) * P], otok[:, a, t * P:(t + 1) * P], ident)
                        tr(ps[:, t, L:N], smp_o[:, t * P:(t + 1) * P], C("ident", B)[:, 0:B]).then_inc(S("o_turned"), 1)

                    pe.wait_ge(S("mix_ready"), 8)
                    for j in range(WO_P):
                        for s in range(2):
                            wide_chunk("wo", j, s, (2 * s, 2 * s + 1), lambda i: pe.wait_ge(S("sq"), 24 + 4 * j + 2 * s + i - 3) if j else None)
                    ss(3)
                    first_pair("gu2", 4)
                    with pe.Fori(1, GU_P) as j:
                        gu_step(2, j)
                    pe.wait_ge(S("h_ready"), 44)
                    with pe.Fori(0, DN_P // 2) as q:
                        dn_pair(2, q)
                    ss(5)

            nc.all_engine_barrier()
            for s in sems.values():
                nc.gpsimd.sem_clear(s)
            nc.all_engine_barrier()

        with nc.Block() as blk:
            @blk.tensor
            def _(pe):
                for t in range(KT):
                    if t >= 4:
                        pe.wait_ge(S("par_taken"), 2 * (t - 3))
                    for a in range(NT):
                        pe.transpose(ps[:, 2 * (t % 4), a * P:(a + 1) * P], x[:, t, a * P:(a + 1) * P], ident)
                    pe.transpose(ps[0:B, 2 * (t % 4) + 1, 0:P], x[:, t, L:N], ident).then_inc(S("par_turned"), 1)

            @blk.vector
            def _(dve):
                for t in range(KT):
                    dve.wait_ge(S("par_turned"), t + 1)
                    dve.tensor_copy(xin[:, 0:2, t * P:(t + 1) * P], ps[:, 2 * (t % 4), 0:L].rearrange("p (a n) -> p a n", a=2)).then_inc(S("par_taken"), 1)
                    dve.tensor_copy(xin[0:B, 2, t * P:(t + 1) * P], ps[0:B, 2 * (t % 4) + 1, 0:P]).then_inc(S("par_taken"), 1)

            @blk.sync
            def _(sp):
                sp.wait_ge(S("par_taken"), 16)
                sp.dma_start(io["outs"]["y_prompt"][0].rearrange("(t p) d -> p t d", p=P), xin[:, 0:2, :]).then_inc(S("stored"), 16)
                sp.dma_start(io["outs"]["y_sample"].rearrange("b t d -> (b t) d"), xin[0:B, 2, :]).then_inc(S("stored"), 16)
                sp.wait_ge(S("stored"), 32)


_INS = ["x_prompt", "x_sample", "cache_fox_k", "cache_fox_v", "cache_fox_logf", "page_table", "state_swa_k", "state_swa_v",
        "state_gdn_s", "state_gdn_conv", "norm_g", "w_in", "w_out", "out_norm_g", "fox_bias", "gdn_conv_w", "gdn_a_log",
        "gdn_dt_bias", "gmlp_ws", "gmlp_bs", "gmlp_norm_g", "ffn1_gate", "ffn1_up", "ffn1_down", "ffn2_gate", "ffn2_up", "ffn2_down"]
_OUTS = {
    "y_prompt": (1, L, D), "y_sample": (B, 1, D),
    "fox_k_prompt": (1, DEPTH, L, H, HD), "fox_v_prompt": (1, DEPTH, L, H, HD), "fox_logf_prompt": (1, DEPTH, L, H),
    "fox_k_sample": (B, DEPTH, 1, H, HD), "fox_v_sample": (B, DEPTH, 1, H, HD), "fox_logf_sample": (B, DEPTH, 1, H),
    "swa_k_prompt": (1, DEPTH, L, H, HD), "swa_v_prompt": (1, DEPTH, L, H, HD),
    "swa_k_sample": (B, DEPTH, 1, H, HD), "swa_v_sample": (B, DEPTH, 1, H, HD),
    "gdn_s_prompt": (1, DEPTH, H, HD, HD), "gdn_conv_prompt": (1, DEPTH, 3, 768),
    "gdn_s_sample": (B, DEPTH, H, HD, HD), "gdn_conv_sample": (B, DEPTH, 3, 768),
    "gmlp_v_sample": (B, DEPTH, 1, GW),
}


def kernel(**inputs):
    import numpy as _np
    import concourse.bacc as _bacc
    from concourse import mybir as _mybir
    from concourse.bass_utils import run_bass_kernel_spmd as _run

    nc = _bacc.Bacc("TRN2", target_bir_lowering=False, num_devices=1, dynamic_dma_scratch_size=1024)
    arrays, io = {}, {}
    for name in _INS + ["const"]:
        a = CONST if name == "const" else _np.ascontiguousarray(inputs[name])
        arrays[f"in_{name}_dram"] = a
        io[name] = nc.dram_tensor(f"in_{name}_dram", a.shape, _mybir.dt.from_np(a.dtype), kind="ExternalInput").ap()
    io["n_pool"] = inputs["cache_fox_k"].shape[0]
    io["outs"] = {name: nc.dram_tensor(f"out_{name}_dram", shape, _mybir.dt.from_np(_np.dtype("float32")), kind="ExternalOutput").ap()
                  for name, shape in _OUTS.items()}
    build(nc, io)
    r = _run(nc, [arrays], core_ids=[0])
    return tuple(r.results[0][f"out_{name}_dram"] for name in _OUTS)
```
